# Optimizing a Trainium2 kernel written in Bass

```python
import math
import jax, jax.numpy as jnp
from jax import lax
import numpy as np

D_MODEL = 1024
BATCH = 1
SEQ = 256
DEPTH = 1

MOBA_HEADS = 8
MOBA_HEAD_DIM = 64
MOBA_BLOCK = 256
MOBA_TOPK = 3
MOBA_QCHUNK = 64
SWA_Q_HEADS = 8
SWA_KV_HEADS = 2
SWA_HEAD_DIM = 64
SWA_WINDOW = 128
SWA_BLOCK = 128
MEM_HEADS = 4
MEM_HEAD_DIM = 128
MEM_LEN = 256
NUM_BUCKETS = 32
MAX_EXACT = NUM_BUCKETS // 2
REL_MAX_DISTANCE = 128
N_SELF_HEADS = MOBA_HEADS + SWA_Q_HEADS
FFN_HIDDEN = 2816
CONV_WIDTH = 3
RMS_EPS = 1e-6
MOBA_W = MOBA_HEADS * MOBA_HEAD_DIM
SWA_QW = SWA_Q_HEADS * SWA_HEAD_DIM
SWA_KVW = SWA_KV_HEADS * SWA_HEAD_DIM
MEM_W = MEM_HEADS * MEM_HEAD_DIM
IN_SPLITS = (MOBA_W, MOBA_W, MOBA_W, SWA_QW, SWA_KVW, SWA_KVW, MEM_W, D_MODEL, D_MODEL, D_MODEL)
IN_WIDTH = 3 * MOBA_W + SWA_QW + 2 * SWA_KVW + MEM_W + 3 * D_MODEL


def rmsnorm(x, g):
    xf = x.astype(jnp.float32)
    r = lax.rsqrt(jnp.mean(xf * xf, axis=-1, keepdims=True) + RMS_EPS)
    return (xf * r * g.astype(jnp.float32)).astype(x.dtype)

def t5_bucket(dist):
    n = jnp.maximum(dist, 0)
    nf = jnp.maximum(n, 1).astype(jnp.float32)
    large = MAX_EXACT + (jnp.log(nf / MAX_EXACT) / math.log(REL_MAX_DISTANCE / MAX_EXACT)
                         * (NUM_BUCKETS - MAX_EXACT)).astype(jnp.int32)
    large = jnp.minimum(large, NUM_BUCKETS - 1)
    return jnp.where(n < MAX_EXACT, n, large)

def moba_attention(q, k, v, bias_table):
    B_, S_, H, dh = q.shape
    Sp = -(-S_ // MOBA_BLOCK) * MOBA_BLOCK
    pad = Sp - S_
    if pad:
        padw = ((0, 0), (0, pad), (0, 0), (0, 0))
        q, k, v = jnp.pad(q, padw), jnp.pad(k, padw), jnp.pad(v, padw)
    NB = Sp // MOBA_BLOCK
    scale = 1.0 / math.sqrt(dh)
    qh = q.transpose(0, 2, 1, 3)
    kb = k.reshape(B_, NB, MOBA_BLOCK, H, dh).transpose(0, 3, 1, 2, 4)
    vb = v.reshape(B_, NB, MOBA_BLOCK, H, dh).transpose(0, 3, 1, 2, 4)
    kmean = jnp.mean(kb.astype(jnp.float32), axis=3)
    gate = jnp.einsum('bhsd,bhnd->bhsn', qh.astype(jnp.float32), kmean)
    qblk = jnp.arange(Sp) // MOBA_BLOCK
    past = jnp.arange(NB)[None, :] < qblk[:, None]
    gate = jnp.where(past, gate, -jnp.inf)
    k_sel = min(MOBA_TOPK, NB)
    _, sel = lax.top_k(gate, k_sel)
    sel_valid = jnp.arange(k_sel)[None, :] < qblk[:, None]
    bi = jnp.arange(B_)[:, None, None, None]
    hi = jnp.arange(H)[None, :, None, None]
    hb = jnp.arange(H)[None, :, None, None, None]
    kpos_in = jnp.arange(MOBA_BLOCK)

    def chunk(i):
        q0 = i * MOBA_QCHUNK
        qc = lax.dynamic_slice_in_dim(qh, q0, MOBA_QCHUNK, axis=2)
        selc = lax.dynamic_slice_in_dim(sel, q0, MOBA_QCHUNK, axis=2)
        validc = lax.dynamic_slice_in_dim(sel_valid, q0, MOBA_QCHUNK, axis=0)
        c = q0 // MOBA_BLOCK
        kg = kb[bi, hi, selc]
        vg = vb[bi, hi, selc]
        k_own = lax.dynamic_index_in_dim(kb, c, axis=2, keepdims=False)
        v_own = lax.dynamic_index_in_dim(vb, c, axis=2, keepdims=False)
        qpos = q0 + jnp.arange(MOBA_QCHUNK)
        kpos_sel = selc[..., None] * MOBA_BLOCK + kpos_in
        s_sel = (jnp.einsum('bhqd,bhqnkd->bhqnk', qc, kg).astype(jnp.float32) * scale
                 + bias_table[hb, t5_bucket(qpos[:, None, None] - kpos_sel)].astype(jnp.float32))
        s_sel = jnp.where(validc[:, :, None], s_sel, -jnp.inf)
        dist_own = qpos[:, None] - (c * MOBA_BLOCK + kpos_in)[None, :]
        s_own = (jnp.einsum('bhqd,bhkd->bhqk', qc, k_own).astype(jnp.float32) * scale
                 + bias_table[:, t5_bucket(dist_own)].astype(jnp.float32))
        s_own = jnp.where(dist_own >= 0, s_own, -jnp.inf)
        s_all = jnp.concatenate(
            [s_sel.reshape(B_, H, MOBA_QCHUNK, k_sel * MOBA_BLOCK), s_own], axis=-1)
        p = jax.nn.softmax(s_all, axis=-1).astype(v.dtype)
        p_sel = p[..., :k_sel * MOBA_BLOCK].reshape(B_, H, MOBA_QCHUNK, k_sel, MOBA_BLOCK)
        p_own = p[..., k_sel * MOBA_BLOCK:]
        return (jnp.einsum('bhqnk,bhqnkd->bhqd', p_sel, vg)
                + jnp.einsum('bhqk,bhkd->bhqd', p_own, v_own))

    outs = lax.map(chunk, jnp.arange(Sp // MOBA_QCHUNK))
    out = outs.transpose(1, 0, 3, 2, 4).reshape(B_, Sp, H, dh)
    return out[:, :S_]

def swa_attention(q, k, v, sinks, bias_table):
    B_, S_, HQ, dh = q.shape
    HKV = k.shape[2]
    G = HQ // HKV
    QB = SWA_BLOCK
    nblk = S_ // QB
    scale = 1.0 / math.sqrt(dh)
    qb = q.reshape(B_, nblk, QB, HKV, G, dh)
    kb = k.reshape(B_, nblk, QB, HKV, dh)
    vb = v.reshape(B_, nblk, QB, HKV, dh)
    padw = ((0, 0), (1, 0), (0, 0), (0, 0), (0, 0))
    kband = jnp.concatenate([jnp.pad(kb, padw)[:, :-1], kb], axis=2)
    vband = jnp.concatenate([jnp.pad(vb, padw)[:, :-1], vb], axis=2)
    s = jnp.einsum('bnqhgd,bnkhd->bhgnqk', qb, kband).astype(jnp.float32) * scale
    dist = QB + jnp.arange(QB)[:, None] - jnp.arange(2 * QB)[None, :]
    bias = bias_table[:, t5_bucket(dist)].astype(jnp.float32).reshape(HKV, G, 1, QB, 2 * QB)
    s = s + bias
    kpos = (jnp.arange(nblk)[:, None] - 1) * QB + jnp.arange(2 * QB)[None, :]
    allowed = ((dist >= 0) & (dist < SWA_WINDOW))[None] & (kpos >= 0)[:, None, :]
    s = jnp.where(allowed, s, -jnp.inf)
    sink = sinks.astype(jnp.float32).reshape(HKV, G, 1, 1, 1)
    m = jnp.maximum(jnp.max(s, axis=-1, keepdims=True), sink)
    p = jnp.exp(s - m)
    denom = jnp.sum(p, axis=-1, keepdims=True) + jnp.exp(sink - m)
    p = (p / denom).astype(v.dtype)
    o = jnp.einsum('bhgnqk,bnkhd->bnqhgd', p, vband)
    return o.reshape(B_, S_, HQ * dh)

def memory_attention(q, km, vm):
    B_, S_, Hm, dm = q.shape
    s = jnp.einsum('bshd,bmhd->bhsm', q, km).astype(jnp.float32) * (1.0 / math.sqrt(dm))
    p = jax.nn.softmax(s, axis=-1).astype(vm.dtype)
    return jnp.einsum('bhsm,bmhd->bshd', p, vm).reshape(B_, S_, Hm * dm)

def causal_depthwise_conv(u, w, b):
    S_ = u.shape[1]
    up = jnp.pad(u, ((0, 0), (CONV_WIDTH - 1, 0), (0, 0)))
    out = b.astype(u.dtype)
    for t in range(CONV_WIDTH):
        out = out + w[t].astype(u.dtype) * up[:, t:t + S_]
    return out

def _normal(k, shape, scale):
    return jax.random.normal(k, shape, jnp.float32) * scale

def first_inputs(seed: int = 0) -> dict:
    key = jax.random.key(seed)
    ks = jax.random.split(key, 20)
    L, D, F = DEPTH, D_MODEL, FFN_HIDDEN
    return {
        "x": _normal(ks[0], (BATCH, SEQ, D), 1.0),
        "mem": _normal(ks[1], (BATCH, MEM_LEN, D), 1.0),
        "norm_mix_pre": 1.0 + _normal(ks[2], (L, D), 0.05),
        "norm_mix_post": 1.0 + _normal(ks[3], (L, D), 0.05),
        "norm_ffn_pre": 1.0 + _normal(ks[4], (L, D), 0.05),
        "norm_ffn_post": 1.0 + _normal(ks[5], (L, D), 0.05),
        "norm_mem": 1.0 + _normal(ks[6], (L, D), 0.05),
        "w_in": _normal(ks[7], (L, D, IN_WIDTH), D ** -0.5),
        "rel_bias": _normal(ks[8], (NUM_BUCKETS, N_SELF_HEADS), 0.3),
        "swa_sinks": _normal(ks[9], (L, SWA_Q_HEADS), 1.0),
        "w_mem_kv": _normal(ks[10], (L, D, 2 * MEM_W), D ** -0.5),
        "w_branch_moba": _normal(ks[11], (L, MOBA_W, D), MOBA_W ** -0.5),
        "w_branch_swa": _normal(ks[12], (L, SWA_QW, D), SWA_QW ** -0.5),
        "w_branch_mem": _normal(ks[13], (L, MEM_W, D), MEM_W ** -0.5),
        "w_out": _normal(ks[14], (L, D, D), D ** -0.5),
        "w_ffn_up": _normal(ks[15], (L, D, 2 * F), D ** -0.5),
        "ffn_conv_w": _normal(ks[16], (L, CONV_WIDTH, 2 * F), CONV_WIDTH ** -0.5),
        "ffn_conv_b": _normal(ks[17], (L, 2 * F), 0.02),
        "w_ffn_down": _normal(ks[18], (L, F, D), F ** -0.5),
    }

def first_block(x, mem, norm_mix_pre, norm_mix_post, norm_ffn_pre, norm_ffn_post, norm_mem,
              w_in, rel_bias, swa_sinks, w_mem_kv, w_branch_moba, w_branch_swa, w_branch_mem,
              w_out, w_ffn_up, ffn_conv_w, ffn_conv_b, w_ffn_down):
    B_, S_, _ = x.shape
    cuts = []
    acc = 0
    for width in IN_SPLITS[:-1]:
        acc += width
        cuts.append(acc)
    bias_moba = rel_bias[:, :MOBA_HEADS].T
    bias_swa = rel_bias[:, MOBA_HEADS:].T
    for l in range(DEPTH):
        h = rmsnorm(x, norm_mix_pre[l])
        proj = h @ w_in[l]
        (q_mb, k_mb, v_mb, q_sw, k_sw, v_sw, q_me,
         g_mb, g_sw, g_me) = jnp.split(proj, cuts, axis=-1)
        o_mb = moba_attention(
            q_mb.reshape(B_, S_, MOBA_HEADS, MOBA_HEAD_DIM),
            k_mb.reshape(B_, S_, MOBA_HEADS, MOBA_HEAD_DIM),
            v_mb.reshape(B_, S_, MOBA_HEADS, MOBA_HEAD_DIM), bias_moba).reshape(B_, S_, MOBA_W)
        o_sw = swa_attention(
            q_sw.reshape(B_, S_, SWA_Q_HEADS, SWA_HEAD_DIM),
            k_sw.reshape(B_, S_, SWA_KV_HEADS, SWA_HEAD_DIM),
            v_sw.reshape(B_, S_, SWA_KV_HEADS, SWA_HEAD_DIM), swa_sinks[l], bias_swa)
        kv_me = rmsnorm(mem, norm_mem[l]) @ w_mem_kv[l]
        M_ = mem.shape[1]
        k_me = kv_me[..., :MEM_W].reshape(B_, M_, MEM_HEADS, MEM_HEAD_DIM)
        v_me = kv_me[..., MEM_W:].reshape(B_, M_, MEM_HEADS, MEM_HEAD_DIM)
        o_me = memory_attention(q_me.reshape(B_, S_, MEM_HEADS, MEM_HEAD_DIM), k_me, v_me)
        merged = (jax.nn.sigmoid(g_mb) * (o_mb @ w_branch_moba[l])
                  + jax.nn.sigmoid(g_sw) * (o_sw @ w_branch_swa[l])
                  + jax.nn.sigmoid(g_me) * (o_me @ w_branch_mem[l]))
        x = x + rmsnorm(merged @ w_out[l], norm_mix_post[l])
        h = rmsnorm(x, norm_ffn_pre[l])
        u = causal_depthwise_conv(h @ w_ffn_up[l], ffn_conv_w[l], ffn_conv_b[l])
        u_gate, u_val = jnp.split(u, 2, axis=-1)
        y = (jax.nn.gelu(u_gate, approximate=True) * u_val) @ w_ffn_down[l]
        x = x + rmsnorm(y, norm_ffn_post[l])
    return x


DEPTH_2 = 2

CTX_LEN = 256
GRID_W = 64
N_HEADS = 8
HEAD_DIM = 64
V_DIM = 2 * HEAD_DIM
QK_W = N_HEADS * 2 * HEAD_DIM
ATTN_WIDTH = N_HEADS * V_DIM
N_FGROUPS = 4
FGROUP_DIM = 128
FOURIER_WIDTH = N_FGROUPS * FGROUP_DIM
F_OFF = 2 * QK_W + ATTN_WIDTH
G_OFF = F_OFF + FOURIER_WIDTH
IN_WIDTH_2 = G_OFF + 2 * D_MODEL
D_FF = 2816
AXIS_DIM = HEAD_DIM // 2
ROPE_BASE = 10000.0
Q_BLOCK = 128
N_MOD = 9
EPS = 1e-6


def rms_norm(x, g):
    xf = x.astype(jnp.float32)
    y = xf * lax.rsqrt(jnp.mean(xf * xf, axis=-1, keepdims=True) + EPS)
    return (y * g.astype(jnp.float32)).astype(x.dtype)

def adaln_mod(cond, w_mod, b_mod):
    m = jax.nn.silu(cond) @ w_mod + b_mod
    return m.reshape(cond.shape[:-1] + (N_MOD, D_MODEL))

def modulate(x, m, i):
    shift = m[:, 3 * i][:, None]
    scale = m[:, 3 * i + 1][:, None]
    return x * (1 + scale) + shift

def swiglu(u, w_in, w_out):
    a, b = jnp.split(u @ w_in, 2, axis=-1)
    return (jax.nn.silu(a) * b) @ w_out

def ffn_sublayer(x, m, i, g, w_in, w_out):
    u = modulate(rms_norm(x, g), m, i)
    return x + 0.5 * m[:, 3 * i + 2][:, None] * swiglu(u, w_in, w_out)

def split_qkv(p):
    B, S = p.shape[:2]
    q = p[..., :QK_W].reshape(B, S, N_HEADS, 2, HEAD_DIM)
    k = p[..., QK_W:2 * QK_W].reshape(B, S, N_HEADS, 2, HEAD_DIM)
    v = p[..., 2 * QK_W:F_OFF].reshape(B, S, N_HEADS, V_DIM)
    return q, k, v

def rope_tables(S):
    ROWS = S // GRID_W
    row = jnp.broadcast_to(jnp.arange(ROWS, dtype=jnp.int32)[:, None], (ROWS, GRID_W)).reshape(S)
    col = jnp.broadcast_to(jnp.arange(GRID_W, dtype=jnp.int32)[None, :], (ROWS, GRID_W)).reshape(S)
    inv = 1.0 / (ROPE_BASE ** (jnp.arange(0, AXIS_DIM, 2, dtype=jnp.float32) / AXIS_DIM))

    def tab(pos):
        ang = pos.astype(jnp.float32)[:, None] * inv[None, :]
        ang = jnp.concatenate([ang, ang], axis=-1)
        return jnp.cos(ang), jnp.sin(ang)

    cr, sr = tab(row)
    cc, sc = tab(col)
    return cr, sr, cc, sc

def rotate(xh, cos, sin):
    cos = cos[None, :, None, None, :].astype(xh.dtype)
    sin = sin[None, :, None, None, :].astype(xh.dtype)
    x1, x2 = jnp.split(xh, 2, axis=-1)
    return xh * cos + jnp.concatenate([-x2, x1], axis=-1) * sin

def apply_rope2d(x, tabs):
    cr, sr, cc, sc = tabs
    return jnp.concatenate([rotate(x[..., :AXIS_DIM], cr, sr),
                            rotate(x[..., AXIS_DIM:], cc, sc)], axis=-1)

def diff_attend(q, k, v, lam):
    s = jnp.einsum("bqhcd,bkhcd->bhcqk", q, k).astype(jnp.float32) * (HEAD_DIM ** -0.5)
    p = jax.nn.softmax(s, axis=-1)
    a = p[:, :, 0] - lam * p[:, :, 1]
    return jnp.einsum("bhqk,bkhe->bqhe", a.astype(v.dtype), v)

def latent_diff_attention(q, k_all, v_all, lam):
    B, S = q.shape[:2]
    nb = S // Q_BLOCK
    qb = jnp.moveaxis(q.reshape(B, nb, Q_BLOCK, N_HEADS, 2, HEAD_DIM), 1, 0)
    out = lax.map(lambda blk: diff_attend(blk, k_all, v_all, lam), qb)
    return jnp.moveaxis(out, 0, 1).reshape(B, S, N_HEADS, V_DIM)

def fourier_mix(f):
    B, S = f.shape[:2]
    fg = f.reshape(B, S, N_FGROUPS, FGROUP_DIM).astype(jnp.float32)
    y = jnp.fft.fft2(fg, axes=(1, 3), norm="ortho").real
    return y.reshape(B, S, FOURIER_WIDTH).astype(f.dtype)

def mixer_merge(attn_heads, f, g_logits, lam_init, subln_g, w_attn_out, w_four_out, b_gate, w_o):
    B, S = attn_heads.shape[:2]
    a = (rms_norm(attn_heads, subln_g) * (1 - lam_init)).reshape(B, S, ATTN_WIDTH) @ w_attn_out
    fr = fourier_mix(f) @ w_four_out
    ga, gf = jnp.split(g_logits, 2, axis=-1)
    merged = jax.nn.sigmoid(ga + b_gate[0]) * a + jax.nn.sigmoid(gf + b_gate[1]) * fr
    return merged @ w_o

def second_inputs(seed: int = 0) -> dict:
    key = jax.random.key(seed)
    ks = jax.random.split(key, 20)
    f32 = jnp.float32
    D = D_MODEL

    def nrm(k, shape, scale):
        return jax.random.normal(k, shape, f32) * scale

    return {
        "x": nrm(ks[0], (BATCH, SEQ, D), 1.0),
        "c": nrm(ks[1], (BATCH, D), 1.0),
        "ctx": nrm(ks[2], (BATCH, CTX_LEN, D), 1.0),
        "c_ctx": nrm(ks[3], (D,), 1.0),
        "w_mod": nrm(ks[4], (DEPTH_2, D, N_MOD * D), 0.5 * D ** -0.5),
        "b_mod": nrm(ks[5], (DEPTH_2, N_MOD * D), 0.01),
        "norm_g": 1.0 + nrm(ks[6], (DEPTH_2, 3, D), 0.1),
        "ffn_w_in": nrm(ks[7], (DEPTH_2, 2, D, 2 * D_FF), D ** -0.5),
        "ffn_w_out": nrm(ks[8], (DEPTH_2, 2, D_FF, D), D_FF ** -0.5),
        "w_in": nrm(ks[9], (DEPTH_2, D, IN_WIDTH_2), D ** -0.5),
        "b_gate": nrm(ks[10], (DEPTH_2, 2, D), 0.01),
        "lam_params": nrm(ks[11], (DEPTH_2, 4, HEAD_DIM), 0.1),
        "subln_g": 1.0 + nrm(ks[12], (DEPTH_2, V_DIM), 0.1),
        "w_attn_out": nrm(ks[13], (DEPTH_2, ATTN_WIDTH, D), ATTN_WIDTH ** -0.5),
        "w_four_out": nrm(ks[14], (DEPTH_2, FOURIER_WIDTH, D), FOURIER_WIDTH ** -0.5),
        "w_o": nrm(ks[15], (DEPTH_2, D, D), D ** -0.5),
        "final_g": 1.0 + nrm(ks[16], (D,), 0.1),
    }

def second_block(x, c, ctx, c_ctx, w_mod, b_mod, norm_g, ffn_w_in, ffn_w_out, w_in, b_gate,
              lam_params, subln_g, w_attn_out, w_four_out, w_o, final_g):
    S = x.shape[1]
    tabs = rope_tables(S)
    x_lat = x
    x_ctx = ctx
    for l in range(DEPTH_2):
        last = l == DEPTH_2 - 1
        lam_init = 0.8 - 0.6 * math.exp(-0.3 * l)
        lp = lam_params[l].astype(jnp.float32)
        lam = jnp.exp(jnp.sum(lp[0] * lp[1])) - jnp.exp(jnp.sum(lp[2] * lp[3])) + lam_init

        m_lat = adaln_mod(c, w_mod[l], b_mod[l])
        m_ctx = adaln_mod(c_ctx, w_mod[l], b_mod[l])[None]

        x_lat = ffn_sublayer(x_lat, m_lat, 0, norm_g[l, 0], ffn_w_in[l, 0], ffn_w_out[l, 0])
        x_ctx = ffn_sublayer(x_ctx, m_ctx, 0, norm_g[l, 0], ffn_w_in[l, 0], ffn_w_out[l, 0])

        u_lat = modulate(rms_norm(x_lat, norm_g[l, 1]), m_lat, 1)
        u_ctx = modulate(rms_norm(x_ctx, norm_g[l, 1]), m_ctx, 1)
        p_lat = u_lat @ w_in[l]
        q_l, k_l, v_l = split_qkv(p_lat)
        q_l = apply_rope2d(q_l, tabs)
        k_l = apply_rope2d(k_l, tabs)
        if last:
            kv_c = u_ctx @ w_in[l][:, QK_W:F_OFF]
            B = kv_c.shape[0]
            k_c = kv_c[..., :QK_W].reshape(B, CTX_LEN, N_HEADS, 2, HEAD_DIM)
            v_c = kv_c[..., QK_W:].reshape(B, CTX_LEN, N_HEADS, V_DIM)
        else:
            p_ctx = u_ctx @ w_in[l]
            q_c, k_c, v_c = split_qkv(p_ctx)

        k_all = jnp.concatenate([k_c, k_l], axis=1)
        v_all = jnp.concatenate([v_c, v_l], axis=1)
        attn_l = latent_diff_attention(q_l, k_all, v_all, lam)
        mix_l = mixer_merge(attn_l, p_lat[..., F_OFF:G_OFF], p_lat[..., G_OFF:], lam_init,
                            subln_g[l], w_attn_out[l], w_four_out[l], b_gate[l], w_o[l])
        x_lat = x_lat + m_lat[:, 5][:, None] * mix_l

        if not last:
            attn_c = diff_attend(q_c, k_c, v_c, lam)
            mix_c = mixer_merge(attn_c, p_ctx[..., F_OFF:G_OFF], p_ctx[..., G_OFF:], lam_init,
                                subln_g[l], w_attn_out[l], w_four_out[l], b_gate[l], w_o[l])
            x_ctx = x_ctx + m_ctx[:, 5][:, None] * mix_c
            x_ctx = ffn_sublayer(x_ctx, m_ctx, 2, norm_g[l, 2], ffn_w_in[l, 1], ffn_w_out[l, 1])

        x_lat = ffn_sublayer(x_lat, m_lat, 2, norm_g[l, 2], ffn_w_in[l, 1], ffn_w_out[l, 1])

    return rms_norm(x_lat, final_g)


def setup_inputs(seed=0):
    out = dict(first_inputs(seed))
    for name, value in second_inputs(seed + 1).items():
        if name != "x":
            out[name + "_2"] = value
    return out


def reference(
    x, mem, norm_mix_pre, norm_mix_post, norm_ffn_pre, norm_ffn_post, norm_mem, w_in, rel_bias,
    swa_sinks, w_mem_kv, w_branch_moba, w_branch_swa, w_branch_mem, w_out, w_ffn_up, ffn_conv_w,
    ffn_conv_b, w_ffn_down, c_2, ctx_2, c_ctx_2, w_mod_2, b_mod_2, norm_g_2, ffn_w_in_2,
    ffn_w_out_2, w_in_2, b_gate_2, lam_params_2, subln_g_2, w_attn_out_2, w_four_out_2, w_o_2,
    final_g_2,
):
    x = first_block(
        x, mem, norm_mix_pre, norm_mix_post, norm_ffn_pre, norm_ffn_post, norm_mem, w_in,
        rel_bias, swa_sinks, w_mem_kv, w_branch_moba, w_branch_swa, w_branch_mem, w_out,
        w_ffn_up, ffn_conv_w, ffn_conv_b, w_ffn_down,
    )
    return second_block(
        x, c_2, ctx_2, c_ctx_2, w_mod_2, b_mod_2, norm_g_2, ffn_w_in_2, ffn_w_out_2, w_in_2,
        b_gate_2, lam_params_2, subln_g_2, w_attn_out_2, w_four_out_2, w_o_2, final_g_2,
    )


_drawn_inputs = setup_inputs


def setup_inputs(seed=0):
    import zlib

    import numpy as np

    out = dict(_drawn_inputs(seed))
    spreads = {}
    factors = {'ffn_conv_b': 3.426,
     'b_mod_2': 7.388,
     'b_gate_2': 27.836,
     'lam_params_2': 8.0,
     'subln_g_2': 5.131}
    for name, (base, spread) in spreads.items():
        noise = np.random.default_rng([zlib.crc32(name.encode()), seed]).standard_normal(out[name].shape)
        drawn = base * np.exp(spread * noise) if base else spread * noise
        out[name] = __import__('jax').numpy.asarray(drawn.astype(out[name].dtype))
    for name, factor in factors.items():
        out[name] = (out[name] * factor).astype(out[name].dtype)
    return out
```

```python
import math
from contextlib import ExitStack

import numpy as np
import concourse.bass as bass
from concourse import mybir

P = 128
D = 1024
KD = D // P
S = 256
T = 2 * S
F = 2816
KF = F // P
EPS = 1e-6
LAYERS = 2
N_MOD = 9
MOD_TILES = N_MOD * KD
BLK = 256
DOWN_KT = KF // 2
MASKED = -1e30
HANK = 3 * P
CTX, LAT = 0, 1

ROWS = {}
ROW_TILES = [
    [("g_mix_pre", 8), ("g_mix_post", 8), ("g_ffn_pre", 8), ("g_ffn_post", 8), ("g_mem", 8),
     ("norm_g", 48), ("b_gate", 32), ("g_final", 8)],
    [("conv_w0", 44), ("conv_w1", 44), ("c_ctx", 8), ("c_lat", 8), ("subln", 2)],
    [("conv_w2", 44), ("conv_b", 44)],
    [("b_mod0", 72)],
    [("b_mod1", 72)],
]
COL = {}
_at = 0
for _t, _rows in enumerate(ROW_TILES):
    _r = 0
    for _name, _n in _rows:
        ROWS[_name] = (_t, _r, _n)
        COL[_name] = _at + _r
        _r += _n
    _at += _r
N_COLS = _at

C_ID, C_REV = 0, 128
N_CONST = 256
C_ROT, C_COS, C_SIN, C_DFT, C_DC, C_DS = 256, 384, 640, 896, 1920, 2048
N_TABS = 1920


def shape_constants():
    c = np.zeros((P, N_CONST + N_TABS), np.float32)
    c[:, C_ID:C_ID + P] = np.eye(P)
    c[:, C_REV:C_REV + P] = np.eye(P)[::-1]
    for g in range(0, P, 32):
        for j in range(16):
            c[g + 16 + j, C_ROT + g + j] = -1.0
            c[g + j, C_ROT + g + 16 + j] = 1.0
    inv = 1.0 / (10000.0 ** (np.arange(0, 32, 2, dtype=np.float32) / np.float32(32)))
    pos = np.arange(S)
    for r in range(P):
        w = r % 64
        p = (pos // 64 if w < 32 else pos % 64).astype(np.float32)
        ang = p * np.float32(inv[(w % 32) % 16])
        c[r, C_COS:C_COS + S] = np.cos(ang)
        c[r, C_SIN:C_SIN + S] = np.sin(ang)
    a = 2 * np.pi * (np.outer(np.arange(S), np.arange(S)) % S) / S
    for tt in range(2):
        at = C_DFT + 512 * tt
        c[:, at:at + S] = np.cos(a[tt * P:(tt + 1) * P])
        c[:, at + S:at + 2 * S] = np.sin(a[tt * P:(tt + 1) * P])
    b = 2 * np.pi * (np.outer(np.arange(P), np.arange(P)) % P) / P
    norm = 1.0 / math.sqrt(S * P)
    c[:, C_DC:C_DC + P] = np.cos(b) * norm
    c[:, C_DS:C_DS + P] = -np.sin(b) * norm
    hot = np.zeros((33, 2, 512), np.float32)
    for i in range(511):
        dist = 255 - i
        n = max(dist, 0)
        big = 16 + int(np.float32(np.log(np.float32(max(n, 1)) / np.float32(16)))
                       / np.float32(math.log(8.0)) * np.float32(16))
        bucket = n if n < 16 else min(big, 31)
        hot[bucket, :, i] = 1.0
        hot[32, 0, i] = float(dist < 0)
        hot[32, 1, i] = float(dist < 0 or dist >= 128)
    return c, hot.reshape(33, 1024)


class Plan:

    def __init__(self):
        self.total, self.before = {}, {}

    def add(self, step, **counts):
        self.before[step] = dict(self.total)
        for k, n in counts.items():
            self.total[k] = self.total.get(k, 0) + n

    def at(self, step, key):
        return self.before[step].get(key, 0)


class Gemm:

    def __init__(self, plan, name, src, blocks, per, kt, cols, gpb, banks, mod=None):
        self.name, self.src, self.kt, self.cols = name, src, kt, cols
        self.per, self.bodies, self.gpb, self.banks = per, blocks // per, gpb, banks
        self.blocks = blocks
        self.first = plan.total.get("blk", 0)
        self.g0 = plan.total.get("grp", 0)
        self.mod = mod
        self.mod0 = plan.total.get(f"mod{mod}", 0)
        counts = {f"b{b}": self.bodies for b in banks}
        if mod is not None:
            counts[f"mod{mod}"] = self.bodies
        plan.add(name, blk=blocks, grp=blocks * gpb, **counts)
        self.use0 = {b: plan.at(name, f"b{b}") for b in banks}

    def done(self, i, n):
        return self.g0 + self.gpb * self.per * i + n

    def taken(self, i, bank):
        return self.use0[bank] + i + 1


def make_plan(a):
    plan, gemms = Plan(), {}

    def gemm(name, src, blocks, per=2, kt=KD, cols=BLK, gpb=2, banks=(0, 1, 2, 3), mod=None):
        gemms[name] = Gemm(plan, name, src, blocks, per, kt, cols, gpb, banks, mod)

    def norm(name, kind):
        plan.add(name, sq=KD, rstd=1, xn=KD, b4=1, **kind)

    TO_U, MOD_U, TO_X, TO_OUT = {"u": KD}, {"u": KD, "xm": KD}, {"upd": KD}, {"upd": KD}

    def cols(w, first):
        return lambda j: w[:, bass.ds(j * BLK + first, BLK)].rearrange("(k p) n -> p k n", p=P)

    def pairs(w):
        return lambda j, c: w[:, bass.ds(j * BLK + c * F, BLK)].rearrange("(k p) n -> p k n", p=P)

    def down(w):
        return lambda j, c: w[c * DOWN_KT * P:(c + 1) * DOWN_KT * P, bass.ds(j * P, P)] \
            .rearrange("(k p) n -> p k n", p=P)

    plan.add("boot", b4=6, b5=8, b6=3)
    w_in, w_kv = a["w_in"][0], a["w_mem_kv"][0]
    norm("n_mem", TO_U)
    gemm("k_me", cols(w_kv, 0), 2, mod=0)
    gemm("v_me", cols(w_kv, 512), 2, gpb=1, banks=(0, 2), mod=0)
    norm("n_mix", TO_U)
    gemm("qk_mb", cols(w_in, 0), 4, mod=0)
    gemm("v_mb", cols(w_in, 1024), 2, gpb=1, banks=(0, 2), mod=0)
    gemm("q_sw", cols(w_in, 1536), 2, mod=0)
    gemm("kv_sw", cols(w_in, 2048), 1, per=1, banks=(0, 1))
    gemm("q_me", cols(w_in, 2304), 2, mod=0)
    plan.add("att1", b0=10, b1=10, b2=10, b3=10, b4=10, b5=10)
    for n, w in enumerate(("w_branch_moba", "w_branch_swa", "w_branch_mem")):
        gemm(f"branch{n}", cols(a[w][0], 0), 4, kt=4, mod=0)
    gemm("gates1", cols(w_in, 2816), 12, mod=0)
    gemm("w_out", cols(a["w_out"][0], 0), 4, mod=0)
    norm("n_mix_post", TO_X)
    norm("n_ffn", TO_U)
    gemm("up1", pairs(a["w_ffn_up"][0]), 22, mod=0)
    gemm("down1", down(a["w_ffn_down"][0]), 16, per=4, kt=DOWN_KT, cols=P, gpb=1, banks=(0, 1), mod=0)
    norm("n_ffn_post", TO_X)
    for l in range(LAYERS):
        last = l == LAYERS - 1
        m = 1 if l == 0 else None
        w = a["w_in_2"][l]
        plan.add(f"mod_{l}", b7=1)
        norm(f"n0_{l}", MOD_U)
        gemm(f"up_{l}0", pairs(a["ffn_w_in_2"][l, 0]), 22, mod=m)
        gemm(f"down_{l}0", down(a["ffn_w_out_2"][l, 0]), 16, per=4, kt=DOWN_KT, cols=P, gpb=1, banks=(0, 1))
        norm(f"n1_{l}", MOD_U)
        gemm(f"q_{l}", cols(w, 0), 4, mod=m)
        gemm(f"k_{l}", cols(w, 1024), 4, mod=m)
        gemm(f"v_{l}", cols(w, 2048), 4, mod=m)
        gemm(f"f_{l}", cols(w, 3072), 2, gpb=1 if last else 2, banks=(0, 2) if last else (0, 1, 2, 3))
        rope = 8 if last else 16
        plan.add(f"rope_{l}", b4=8, b5=8)
        halves = 1 if last else 2
        plan.add(f"four_{l}", b4=4 * halves, b5=4 * halves)
        units = 16 * halves
        plan.add(f"att_{l}", b0=units // 2, b1=units // 2, b2=units // 2, b3=units // 2,
                 b4=units // 2, b5=units // 2, b6=units // 2, unit=units, pair=units // 2)
        plan.add(f"subln_{l}", sq=KD, rstd=KD, b4=4, b5=4, xn=KD, o=KD)
        gemm(f"attn_out_{l}", cols(a["w_attn_out_2"][l], 0), 4, mod=m)
        gemm(f"four_out_{l}", cols(a["w_four_out_2"][l], 0), 4, kt=4)
        gemm(f"gates_{l}0", cols(w, 3584), 4, mod=m)
        gemm(f"gates_{l}1", cols(w, 4608), 4, mod=m)
        gemm(f"w_o_{l}", cols(a["w_o_2"][l], 0), 4, mod=m)
        norm(f"n2_{l}", MOD_U)
        gemm(f"up_{l}1", pairs(a["ffn_w_in_2"][l, 1]), 22, mod=m)
        gemm(f"down_{l}1", down(a["ffn_w_out_2"][l, 1]), 16, per=4, kt=DOWN_KT, cols=P, gpb=1, banks=(0, 1))
    norm("n_final", TO_OUT)
    plan.add("store", b5=2, b6=2)
    assert plan.total["mod0"] == plan.total["mod1"] == MOD_TILES // 2
    return plan, gemms


def two_blocks(nc, a, out):
    f32, f32r = mybir.dt.float32, mybir.dt.float32r
    ACT, ALU, AX = mybir.ActivationFunctionType, mybir.AluOpType, mybir.AxisListType
    plan, gemms = make_plan(a)
    stream = list(gemms.values())
    scratch = nc.dram_tensor("bias_tables", (2, 8, 512), f32, kind="Internal").ap()

    ctx = ExitStack()
    with ctx:
        def sb(name, shape, dt=f32, on=ctx):
            return on.enter_context(nc.sbuf_tensor(name, shape, dt))

        def sem(name):
            return ctx.enter_context(nc.semaphore(name))

        raw = [sb(f"raw{n}", [P, 2048]) for n in range(2)]
        w_hi = [sb(f"w_hi{n}", [P, 2048], f32r) for n in range(2)]
        w_lo = [sb(f"w_lo{n}", [P, 2048], f32r) for n in range(2)]
        mod_raw = [sb(f"mod_raw{n}", [P, KD, P]) for n in range(2)]
        x = sb("x", [P, KD, T])
        u_hi = sb("u_hi", [P, KD, T], f32r)
        u_lo = sb("u_lo", [P, KD, T], f32r)
        const = sb("const", [P, N_CONST])
        ones = sb("ones", [P, P])
        eps = sb("eps", [P, 1])
        col = sb("col", [P, N_COLS])
        cond = sb("cond", [P, KD, 2])
        mod = sb("mod", [P, MOD_TILES, 2])
        mod_a = sb("mod_a", [P, 3, KD, 2])
        mod_g = sb("mod_g", [P, 3, KD, 2])
        sub_g = sb("sub_g", [P, LAYERS])
        sinks = sb("sinks", [P, 8])
        lam = sb("lam", [P, LAYERS])
        stat = sb("stat", [P, 2, 16])
        xn = sb("xn", [P, 2, T])
        sq = xn
        root = sb("root", [P, 2, T])
        rstd = root
        work = sb("work", [P, 4, T])

        a1 = ExitStack()
        tok = sb("tok", [P, 3, 2, D], on=a1)
        hank = tok[:, :, :, :].rearrange("p a b n -> p (a b n)").rearrange("p (h n) -> p h n", h=16)
        branch = tok[:, :, :, :].rearrange("p a b n -> p (a b n)").rearrange("p (j t) -> p j t", t=S)
        qk_mb = sb("qk_mb", [P, 8, S], on=a1)
        v_mb = sb("v_mb", [P, 2, 512], on=a1)
        q_sw = sb("q_sw", [P, 4, S], on=a1)
        k_sw = sb("k_sw", [P, 2, S], on=a1)
        v_sw = sb("v_sw", [P, 2, P], on=a1)
        q_me = sb("q_me", [P, 4, S], on=a1)
        y = sb("y", [P, KD, S], on=a1)
        k_me = y[:, 0:4, :]
        v_me = y[:, 4:8, :].rearrange("p (t a) s -> p t (a s)", t=2)
        boot = ExitStack()
        rows = sb("rows", [P, len(ROW_TILES), P], on=boot)
        hot = sb("hot", [33, 2, 512], on=boot)
        tables = sb("tables", [8, 2, 512], on=boot)
        rel = sb("rel", [33, 16], on=boot)
        sink_row = sb("sink_row", [1, 8], on=boot)
        lam_in = sb("lam_in", [1, LAYERS, 4, 64], on=boot)
        lam_p = sb("lam_p", [1, LAYERS, 2, 64], on=boot)
        lam_s = sb("lam_s", [1, LAYERS, 2], on=boot)
        lam_e = sb("lam_e", [P, LAYERS, 2], on=boot)
        boot.close()
        o1_hi = sb("o1_hi", [P, 12, S], f32r, on=a1)
        o1_lo = sb("o1_lo", [P, 12, S], f32r, on=a1)
        p_t = xn[:, :, :].rearrange("p s (k q) -> p s k q", k=2)
        a1.close()
        h1 = ExitStack()
        hid1_hi = sb("hid1_hi", [P, KF, S], f32r, on=h1)
        hid1_lo = sb("hid1_lo", [P, KF, S], f32r, on=h1)
        h1.close()
        a2 = ExitStack()
        q2 = sb("q2", [P, KD, T], on=a2)
        a2k = ExitStack()
        k2 = sb("k2", [P, KD, T], on=a2k)
        v2 = sb("v2", [P, 4, D], on=a2k)
        a2k.close()
        o2_hi = sb("o2_hi", [P, KD, T], f32r, on=a2)
        o2_lo = sb("o2_lo", [P, KD, T], f32r, on=a2)
        fa = sb("fa", [P, 4096], on=a2)
        f2 = fa[:, 0:2048].rearrange("p (t n) -> p t n", t=4)
        a_t = fa[:, 2048:4096].rearrange("p (s k q) -> p s k q", s=2, k=4)
        fr = fa[:, :].rearrange("p (j t) -> p j t", t=T)
        yf_hi = sb("yf_hi", [P, 4, T], f32r, on=a2)
        yf_lo = sb("yf_lo", [P, 4, T], f32r, on=a2)
        dft = work[:, 2:4, :]
        tabs = sb("tabs", [P, N_TABS], on=a2)
        a2.close()
        h2 = ExitStack()
        hid2_hi = sb("hid2_hi", [P, KF, T], f32r, on=h2)
        hid2_lo = sb("hid2_lo", [P, KF, T], f32r, on=h2)
        h2.close()
        h3 = ExitStack()
        fin = sb("fin", [P, KD, S], on=h3)
        rows_out = sb("rows_out", [P, 2, D], on=h3)
        h3.close()

        bank = [ctx.enter_context(nc.psum_tensor(f"bank{b}", [P, 512], f32)) for b in range(8)]

        ident = const[:, C_ID:C_ID + P]
        reverse = const[:, C_REV:C_REV + P]

        def table(first, n):
            return tabs[:, first - N_CONST:first - N_CONST + n]

        rot, cos, sin = table(C_ROT, P), table(C_COS, S), table(C_SIN, S)

        raw_ready = [sem(f"raw_ready{n}") for n in range(2)]
        hi_ready = sem("hi_ready")
        lo_ready = sem("lo_ready")
        mod_ready = [sem(f"mod_ready{n}") for n in range(2)]
        mod_used = sem("mod_used")
        group_done = sem("group_done")
        taken = [sem(f"taken{b}") for b in range(8)]
        tok_ready = [sem(f"tok_ready{n}") for n in range(3)]
        const_ready = sem("const_ready")
        tabs_ready = sem("tabs_ready")
        rows_ready = sem("rows_ready")
        rel_ready = sem("rel_ready")
        set_ready = sem("set_ready")
        boot_done = sem("boot_done")
        scratch_ready = sem("scratch_ready")
        hank_ready = sem("hank_ready")
        cond_ready = sem("cond_ready")
        lam_ready = sem("lam_ready")
        sq_ready = sem("sq_ready")
        sq_used = sem("sq_used")
        rstd_ready = sem("rstd_ready")
        xn_ready = sem("xn_ready")
        xm_ready = sem("xm_ready")
        u_part = sem("u_part")
        u_ready = sem("u_ready")
        updated = sem("updated")
        cv_first = sem("cv_first")
        cv_mid = sem("cv_mid")
        gelu_ready = sem("gelu_ready")
        hid_prod = sem("hid_prod")
        hid_part = sem("hid_part")
        hid_ready = sem("hid_ready")
        gated = sem("gated")
        dve_step = sem("dve_step")
        merged_ready = sem("merged_ready")
        score_ready = sem("score_ready")
        nmax_ready = sem("nmax_ready")
        prob_ready = sem("prob_ready")
        pt_done = sem("pt_done")
        o_done = sem("o_done")
        o_ready = sem("o_ready")
        rot_done = sem("rot_done")
        rope_ready = sem("rope_ready")
        dft_done = sem("dft_done")
        yf_ready = sem("yf_ready")
        mod_taken = sem("mod_taken")
        out_done = sem("out_done")

        block = ctx.enter_context(nc.Block())

        UNITS1 = [("moba", h) for h in range(8)] + [("swa", h) for h in range(8)] + [("mem", h) for h in range(4)]

        def halves_of(l, step):
            if l == LAYERS - 1 and step in ("q", "f", "merge", "ffn1"):
                return [LAT]
            return [CTX, LAT]

        def span(halves):
            return slice(halves[0] * S, (halves[-1] + 1) * S)

        def gate_base(l, n):
            return 24 + 16 * l + 8 * n

        def dft_base(l):
            return 16 * l

        def rope_base(l):
            return 16 * l

        def rope_tiles(l):
            return [(t, j) for t in range(2) for j in range(KD)]

        def att_units(l):
            return [(h, half, qb) for h in range(8) for half in reversed(halves_of(l, "q")) for qb in range(2)]

        def yf_base(l):
            return 8 * l

        @block.sync
        def _(sp):
            def load(st, i, c):
                n = st.first + c
                j = i * (st.per // 2) + c // 2 if st.per != 2 else i
                if st.per == 2 and st.name[:2] != "up":
                    src = st.src(i * 2 + c)
                elif st.per == 1:
                    src = st.src(0)
                else:
                    src = st.src(j, c % 2)
                slot = raw[n % 2][:, 0:st.kt * st.cols].rearrange("p (k n) -> p k n", k=st.kt)
                sp.dma_start(slot, src).then_inc(raw_ready[n % 2], 16)

            def mod_loads(st, i):
                for c in range(2):
                    pair = i + st.mod0 + (st.mod * MOD_TILES // 2)
                    if not (isinstance(pair, int) and pair == 0):
                        sp.wait_ge(mod_used, pair * 2 + c - 1)
                    sp.dma_start(mod_raw[c][:, :, :],
                                 a["w_mod_2"][st.mod][:, bass.ds((i + st.mod0) * 2 * P + c * P, P)]
                                 .rearrange("(k p) n -> p k n", p=P)).then_inc(mod_ready[c], 16)

            def body(st, i):
                for c in range(st.per):
                    s = i * st.per + (st.first + c - 1)
                    if not (isinstance(s, int) and s < 1):
                        sp.wait_ge(lo_ready, s)
                    load(st, i, c)
                if st.mod is not None:
                    mod_loads(st, i)

            for st in stream:
                body(st, 0)
                if st.bodies > 1:
                    with sp.Fori(1, st.bodies) as i:
                        body(st, i)
            for tt in range(2):
                sp.wait_ge(taken[5 + tt], plan.at("store", f"b{5 + tt}") + 2)
            sp.dma_start(out.rearrange("b (t p) n -> p (b t) n", p=P), rows_out[:, :, :]).then_inc(out_done, 16)
            sp.wait_ge(out_done, 16)

        @block.gpsimd
        def _(pool):
            def body(st, i):
                for c in range(st.per):
                    n = st.first + c
                    size = st.kt * st.cols
                    pool.wait_ge(hi_ready, i * st.per + (n + 1))
                    pool.tensor_tensor(w_lo[n % 2][:, 0:size], raw[n % 2][:, 0:size],
                                       w_hi[n % 2][:, 0:size].bitcast(f32), ALU.subtract).then_inc(lo_ready, 1)

            for st in stream:
                if st.bodies == 1:
                    body(st, 0)
                else:
                    with pool.Fori(0, st.bodies) as i:
                        body(st, i)

        @block.scalar
        def _(act):
            mem_v, x_v, ctx_v = (a[n][0].rearrange("(t p) n -> p t n", p=P) for n in ("mem", "x", "ctx_2"))
            act.dma_start(const[:, :], a["shape_const"][:, 0:N_CONST]).then_inc(const_ready, 16)
            for n, v in enumerate((mem_v, x_v, ctx_v)):
                act.dma_start(tok[:, n, :, :], v).then_inc(tok_ready[n], 16)
            row_src = {
                "g_mix_pre": a["norm_mix_pre"], "g_mix_post": a["norm_mix_post"], "g_ffn_pre": a["norm_ffn_pre"],
                "g_ffn_post": a["norm_ffn_post"], "g_mem": a["norm_mem"], "norm_g": a["norm_g_2"],
                "b_gate": a["b_gate_2"], "g_final": a["final_g_2"], "conv_w0": a["ffn_conv_w"][0, 0],
                "conv_w1": a["ffn_conv_w"][0, 1], "conv_w2": a["ffn_conv_w"][0, 2], "conv_b": a["ffn_conv_b"],
                "c_ctx": a["c_ctx_2"], "c_lat": a["c_2"], "subln": a["subln_g_2"],
                "b_mod0": a["b_mod_2"][0], "b_mod1": a["b_mod_2"][1],
            }
            flat = {1: "(r p) -> r p", 2: "a (r p) -> (a r) p", 3: "a b (r p) -> (a b r) p"}
            for name, (t, r, n) in ROWS.items():
                v = row_src[name]
                act.dma_start(rows[r:r + n, t, :], v.rearrange(flat[len(v.shape)], p=P)).then_inc(rows_ready, 16)
            act.dma_start(hot[:, :, :], a["shape_hot"].rearrange("b (v n) -> b v n", v=2)).then_inc(rel_ready, 16)
            act.wait_ge(set_ready, 1)
            act.dma_start(rel[0:32, :], a["rel_bias"]).then_inc(rel_ready, 16)
            act.dma_start(sink_row[:, :], a["swa_sinks"]).then_inc(rel_ready, 16)
            act.dma_start(lam_in[:, :, :, :].rearrange("o l j d -> o (l j d)"),
                          a["lam_params_2"].rearrange("(o l) j d -> o (l j d)", o=1)).then_inc(rel_ready, 16)

            def split(s):
                for st in stream:
                    if st.first <= s < st.first + st.blocks:
                        break
                else:
                    return
                act.wait_ge(raw_ready[s % 2], 16 * (s // 2 + 1))
                if s >= 2:
                    old = [q for q in stream if q.first <= s - 2 < q.first + q.blocks][0]
                    act.wait_ge(group_done, old.g0 + old.gpb * (s - 2 - old.first + 1))
                size = st.kt * st.cols
                act.activation(w_hi[s % 2][:, 0:size], raw[s % 2][:, 0:size], ACT.Copy).then_inc(hi_ready, 1)

            def split_two_ahead(st, i, c, final):
                if final and c + 2 >= st.per:
                    return split(st.first + st.per * (st.bodies - 1) + c + 2)
                n = st.first + c + 2
                act.wait_ge(raw_ready[n % 2], i * (8 * st.per) + 16 * (n // 2 + 1))
                act.wait_ge(group_done, st.done(i, st.gpb * (c + 1)))
                size = st.kt * st.cols
                act.activation(w_hi[n % 2][:, 0:size], raw[n % 2][:, 0:size], ACT.Copy).then_inc(hi_ready, 1)

            def gemm(name, evac=None):
                st = gemms[name]

                def body(i, final):
                    for c in range(st.per):
                        if evac is not None:
                            evac(st, i, c)
                        split_two_ahead(st, i, c, final)

                if st.bodies > 1:
                    with act.Fori(0, st.bodies - 1) as i:
                        body(i, False)
                body(st.bodies - 1, True)

            def copy_tiles(dst, cols):
                def evac(st, i, c):
                    for t in range(2):
                        act.wait_ge(group_done, st.done(i, 2 * c + t + 1))
                        b = 2 * c + t
                        act.activation(dst[:, bass.ds(i * 4 + b, 1), cols], bank[b][:, 0:cols.stop - cols.start]
                                       .rearrange("p (o t) -> p o t", o=1), ACT.Copy).then_inc(taken[b], 1)
                return evac

            def copy_rows(dst, first, tiles):
                per_block = tiles // 2

                def evac(st, i, c):
                    for t in range(per_block):
                        act.wait_ge(group_done, st.done(i, per_block * c + t + 1))
                        b = 2 * c + t
                        act.activation(dst[:, first + 2 * t:first + 2 * t + 2, bass.ds(i * 2 * BLK + c * BLK, BLK)],
                                       bank[b][:, :].rearrange("p (t n) -> p t n", t=2), ACT.Copy) \
                           .then_inc(taken[b], 1)
                return evac

            def squares(name, src, ready):
                q0, w = plan.at(name, "sq"), src(0).shape[-1]
                for k in range(KD):
                    for s, v in ready(k):
                        act.wait_ge(s, v)
                    if q0 + k >= 2:
                        act.wait_ge(sq_used, q0 + k - 1)
                    act.activation(sq[:, k % 2, 0:w], src(k), ACT.Square).then_inc(sq_ready, 1)
                act.wait_ge(sq_used, q0 + KD)
                if plan.at(name, "xn"):
                    act.wait_ge(xn_ready, plan.at(name, "xn"))
                act.activation(root[:, 0, 0:w], bank[4][:, 0:w], ACT.Sqrt, bias=eps[:, 0:1], scale=1.0 / D) \
                   .then_inc(taken[4], 1)

            def modulated(name, l, i, halves):
                x0, u0, m0 = plan.at(name, "xn"), plan.at(name, "u"), plan.at(name, "xm")
                for k in range(KD):
                    act.wait_ge(xn_ready, x0 + k + 1)
                    act.wait_ge(u_ready, u0 + k - 1)
                    for h in halves:
                        lo = (h - halves[0]) * S
                        ins = act.activation(work[:, k % 2, lo:lo + S], xn[:, k % 2, lo:lo + S], ACT.Identity,
                                             bias=mod[:, 3 * i * KD + k, h:h + 1], scale=mod_a[:, i, k, h:h + 1])
                    ins.then_inc(xm_ready, 1)

            def silu_tiles(w):
                def evac(st, i, c):
                    if c == 0:
                        for t in range(2):
                            act.wait_ge(group_done, st.done(i, t + 1))
                            act.wait_ge(taken[2 + t], st.taken(i, 2 + t) - 1)
                            act.activation(work[:, t, 0:w], bank[t][:, 0:w], ACT.Silu).then_inc(taken[t], 1)
                return evac

            def sigmoid_tiles(step, w, bias):
                def evac(st, i, c):
                    for t in range(2):
                        b = 2 * c + t
                        act.wait_ge(group_done, st.done(i, b + 1))
                        act.wait_ge(gated, i * 4 + (plan.at(step, "gate") + 1))
                        act.activation(work[:, b, 0:w], bank[b][:, 0:w], ACT.Sigmoid,
                                       bias=bias(i * 4 + b)).then_inc(taken[b], 1)
                return evac

            split(0)
            split(1)
            act.wait_ge(taken[6], 1)
            act.activation(cond[:, :, :], col[:, COL["c_ctx"]:COL["c_ctx"] + 2 * KD]
                           .rearrange("p (c k) -> p k c", c=2), ACT.Silu).then_inc(cond_ready, 1)
            act.wait_ge(boot_done, 14)
            act.activation(lam_e[:, :, :], bank[5][:, 16:20].rearrange("p (l j) -> p l j", l=2), ACT.Exp) \
               .then_inc(taken[5], 1)
            act.wait_ge(taken[5], 8)
            act.wait_ge(taken[6], 3)
            act.dma_start(scratch.rearrange("v h n -> h v n"), tables[:, :, :]).then_inc(scratch_ready, 16)
            act.wait_ge(scratch_ready, 16)
            act.wait_ge(taken[4], 6)
            shifted = bass.AP(tensor=scratch.tensor, offset=0, ap=[[1, P], [512, 16], [1, HANK]])
            act.dma_start(hank, shifted).then_inc(hank_ready, 16)

            squares("n_mem", lambda k: y[:, k, :], lambda k: [(taken[4], 2), (taken[5], 2)])
            gemm("k_me", copy_tiles(k_me, slice(0, S)))
            gemm("v_me", copy_rows(v_me, 0, 2))
            squares("n_mix", lambda k: x[:, k, S:T], lambda k: [(taken[4], 4), (taken[5], 4)])
            gemm("qk_mb", copy_tiles(qk_mb, slice(0, S)))
            gemm("v_mb", copy_rows(v_mb, 0, 2))
            gemm("q_sw", copy_tiles(q_sw, slice(0, S)))

            def kv_sw(st, i, c):
                act.wait_ge(group_done, st.done(0, 1))
                for kv in range(2):
                    for to in range(2):
                        ins = act.activation(k_sw[64 * to:64 * to + 64, kv, :], bank[0][64 * kv:64 * kv + 64, 0:S], ACT.Copy)
                ins.then_inc(taken[0], 1)
                act.wait_ge(group_done, st.done(0, 2))
                act.activation(v_sw[:, :, :], bank[1][:, 0:2 * P].rearrange("p (t n) -> p t n", t=2), ACT.Copy) \
                   .then_inc(taken[1], 1)

            gemm("kv_sw", kv_sw)
            gemm("q_me", copy_tiles(q_me, slice(0, S)))

            def exp1(n):
                kind, h = UNITS1[n]
                scale = 0.125 if kind != "mem" else 1.0 / math.sqrt(128)
                act.wait_ge(nmax_ready, n + 1)
                if n >= 2:
                    act.wait_ge(pt_done, n - 1)
                st_ = stat[:, n % 2, :]
                if kind == "swa":
                    act.activation(st_[:, 6:8], st_[:, 2:4], ACT.Exp, bias=sinks[:, h:h + 1])
                for q in range(2):
                    ins = act.activation(work[:, n % 2, q * S:(q + 1) * S], bank[n % 2][:, q * S:(q + 1) * S], ACT.Exp,
                                         bias=st_[:, 2 + q:3 + q], scale=scale, accum_out=st_[:, 4 + q:5 + q])
                ins.then_inc(taken[n % 2], 1)

            def copy_pt1(n):
                act.wait_ge(pt_done, n + 1)
                if n >= 2:
                    act.wait_ge(o_done, n - 1)
                act.activation(p_t[:, n % 2, :, :], bank[2 + n % 2][:, :].rearrange("p (k q) -> p k q", k=2), ACT.Copy) \
                   .then_inc(taken[2 + n % 2], 1)

            for n in range(len(UNITS1) + 1):
                if n < len(UNITS1):
                    exp1(n)
                if n >= 1:
                    copy_pt1(n - 1)
            for n in range(3):
                gemm(f"branch{n}", copy_tiles(branch[:, 8 * n:8 * n + 8, :], slice(0, S)))

            def gates1(st, i, c):
                for t in range(2):
                    b = 2 * c + t
                    act.wait_ge(group_done, st.done(i, b + 1))
                    act.wait_ge(gated, i * 4 + 1)
                    act.activation(work[:, b, 0:S], bank[b][:, 0:S], ACT.Sigmoid).then_inc(taken[b], 1)

            gemm("gates1", gates1)
            gemm("w_out", copy_tiles(y, slice(0, S)))
            st = gemms["w_out"]
            squares("n_mix_post", lambda k: y[:, k, :], lambda k: [(taken[k % 4], st.taken(k // 4, k % 4))])
            squares("n_ffn", lambda k: x[:, k, S:T], lambda k: [(updated, KD)])

            def conv_tiles(st, i, c):
                for t in range(2):
                    act.wait_ge(group_done, st.done(i, 2 * c + t + 1))
                    if c == 0:
                        act.wait_ge(hid_ready, i * 2 + 1)
                    at = i * 2 + (c * KF + t)
                    b = 2 * c + t
                    act.activation(work[:, b, 0:S], bank[b][:, 0:S], ACT.Identity,
                                   bias=col[:, bass.ds(at + COL["conv_b"], 1)],
                                   scale=col[:, bass.ds(at + COL["conv_w2"], 1)]).then_inc(cv_first, 1)
                if c == 0:
                    for t in range(2):
                        act.wait_ge(taken[t], st.taken(i, t))
                        act.activation(work[:, t, 0:S], work[:, t, 0:S], ACT.Gelu_apprx_tanh).then_inc(gelu_ready, 1)

            gemm("up1", conv_tiles)
            gemm("down1")
            st = gemms["down1"]
            squares("n_ffn_post", lambda k: y[:, k, :], lambda k: [(taken[k % 2], st.taken(k // 2, k % 2))])

            def layer(l):
                both, q_h, m_h = [CTX, LAT], halves_of(l, "q"), halves_of(l, "merge")
                wq, wm = S * len(q_h), S * len(m_h)
                if l == 0:
                    ready = lambda k: [(updated, 2 * KD)]
                else:
                    st = gemms[f"down_{l - 1}1"]
                    ready = lambda k: [(taken[k % 2], st.taken(k // 2, k % 2))]
                squares(f"n0_{l}", lambda k: x[:, k, :], ready)
                modulated(f"n0_{l}", l, 0, both)
                gemm(f"up_{l}0", silu_tiles(T))
                gemm(f"down_{l}0")
                st0 = gemms[f"down_{l}0"]
                squares(f"n1_{l}", lambda k: x[:, k, :], lambda k: [(taken[k % 2], st0.taken(k // 2, k % 2))])
                act.dma_start(tabs[:, :], a["shape_const"][:, N_CONST:]).then_inc(tabs_ready, 16)
                modulated(f"n1_{l}", l, 1, both)
                gemm(f"q_{l}", copy_tiles(q2, span(q_h)))
                gemm(f"k_{l}", copy_tiles(k2, slice(0, T)))
                gemm(f"v_{l}", copy_rows(v2, 0, 4))
                gemm(f"f_{l}", copy_rows(f2, 2 * q_h[0], 2 * len(q_h)))
                b4, d0 = plan.at(f"four_{l}", "b4"), 8 * l
                n = 0
                for g in range(4):
                    for h in q_h:
                        act.wait_ge(dft_done, dft_base(l) + 2 * n + 1)
                        if n >= 2:
                            act.wait_ge(dft_done, dft_base(l) + 2 * (n - 2) + 2)
                        act.activation(dft[:, n % 2, :], bank[4][:, :], ACT.Copy).then_inc(taken[4], 1)
                        n += 1
                units = att_units(l)
                u0, p0 = plan.at(f"att_{l}", "unit"), plan.at(f"att_{l}", "pair")

                def exps(n):
                    h, half, qb = units[n]
                    nk = T if half == LAT else S
                    act.wait_ge(nmax_ready, len(UNITS1) + u0 + n + 1)
                    act.wait_ge(pt_done, len(UNITS1) + u0 + n - 1)
                    st_ = stat[:, n % 2, :]
                    for c in range(2):
                        b = 2 * (n % 2) + c
                        act.activation(work[:, b, 0:nk], bank[b][:, 0:nk], ACT.Exp, bias=st_[:, 2 + c:3 + c],
                                       scale=0.125, accum_out=st_[:, 4 + c:5 + c]).then_inc(taken[b], 1)

                def copy_pt(n):
                    h, half, qb = units[n]
                    kt = 4 if half == LAT else 2
                    act.wait_ge(pt_done, len(UNITS1) + u0 + n + 1)
                    if n >= 4:
                        act.wait_ge(o_done, len(UNITS1) + p0 + n // 2 - 1)
                    act.activation(a_t[:, (n // 2) % 2, 0:kt, qb * P:(qb + 1) * P],
                                   bank[4 + n % 2][:, 0:kt * P].rearrange("p (k q) -> p k q", k=kt), ACT.Copy) \
                       .then_inc(taken[4 + n % 2], 1)

                for n in range(len(units) + 1):
                    if n < len(units):
                        exps(n)
                    if n >= 1:
                        copy_pt(n - 1)
                q0, x0 = plan.at(f"subln_{l}", "sq"), plan.at(f"subln_{l}", "xn")
                act.wait_ge(taken[6], plan.at(f"subln_{l}", "b6"))

                def head_root(h):
                    act.wait_ge(sq_used, q0 + h + 1)
                    act.wait_ge(xn_ready, x0 + h - 1)
                    act.activation(root[:, h % 2, 0:wq], bank[4 + h % 2][:, 0:wq], ACT.Sqrt, bias=eps[:, 0:1],
                                   scale=1.0 / P).then_inc(taken[4 + h % 2], 1)

                for h in range(KD):
                    act.wait_ge(sq_used, q0 + h - 1)
                    act.activation(sq[:, h % 2, 0:wq], q2[:, h, span(q_h)], ACT.Square).then_inc(sq_ready, 1)
                    if h >= 1:
                        head_root(h - 1)
                head_root(KD - 1)
                gemm(f"attn_out_{l}", copy_tiles(q2, span(m_h)))
                gemm(f"four_out_{l}", copy_tiles(fr, span(m_h)))
                for n in range(2):
                    first = COL["b_gate"] + (2 * l + n) * KD
                    base = gate_base(l, n)

                    def gates(st, i, c, first=first, base=base):
                        for t in range(2):
                            b = 2 * c + t
                            act.wait_ge(group_done, st.done(i, b + 1))
                            act.wait_ge(gated, i * 4 + (base + 1))
                            act.activation(work[:, b, 0:wm], bank[b][:, 0:wm], ACT.Sigmoid,
                                           bias=col[:, bass.ds(i * 4 + (b + first), 1)]).then_inc(taken[b], 1)

                    gemm(f"gates_{l}{n}", gates)
                gemm(f"w_o_{l}")
                st1 = gemms[f"w_o_{l}"]
                squares(f"n2_{l}", lambda k: x[:, k, span(m_h)], lambda k: [(taken[k % 4], st1.taken(k // 4, k % 4))])
                modulated(f"n2_{l}", l, 2, m_h)
                gemm(f"up_{l}1", silu_tiles(wm))
                gemm(f"down_{l}1")

            for l in range(LAYERS):
                layer(l)
            st = gemms[f"down_{LAYERS - 1}1"]
            squares("n_final", lambda k: x[:, k, S:T], lambda k: [(taken[k % 2], st.taken(k // 2, k % 2))])

        @block.vector
        def _(dve):
            steps = [0]

            def link(ins):
                steps[0] += 1
                ins.then_inc(dve_step, 1)
                dve.wait_ge(dve_step, steps[0])

            dve.memset(rel[32:33, :], MASKED).then_inc(set_ready, 1)
            dve.memset(ones[:, :], 1.0).then_inc(set_ready, 1)
            dve.memset(eps[:, :], EPS).then_inc(set_ready, 1)
            dve.sem_inc(hid_ready, 1)
            dve.sem_inc(gated, 1)
            dve.wait_ge(boot_done, 1)
            dve.tensor_copy(col[:, :], bank[6][:, 0:N_COLS]).then_inc(taken[6], 1)
            dve.wait_ge(rel_ready, 64)
            for l in range(LAYERS):
                dve.tensor_tensor(lam_p[:, l, :, :], lam_in[:, l, 0:4:2, :], lam_in[:, l, 1:4:2, :], ALU.mult).then_inc(set_ready, 1)
            dve.wait_ge(set_ready, 5)
            dve.tensor_reduce(lam_s[:, :, :], lam_p[:, :, :, :], AX.X, ALU.add).then_inc(set_ready, 1)
            for n in range(12):
                s, q = n // 4, n % 4
                dst = y[:, 2 * q:2 * q + 2, :] if s == 0 else x[:, 2 * q:2 * q + 2, S:T] if s == 1 else x[:, 2 * q:2 * q + 2, 0:S]
                dve.wait_ge(boot_done, n + 2)
                dve.tensor_copy(dst, bank[4 + n % 2][:, :].rearrange("p (f t) -> p f t", f=2)).then_inc(taken[4 + n % 2], 1)
            dve.wait_ge(taken[5], 7)
            for l in range(LAYERS):
                init = 0.8 - 0.6 * math.exp(-0.3 * l)
                link(dve.tensor_scalar(lam[:, l:l + 1], lam_e[:, l, 0:1], lam_e[:, l, 1:2], init, ALU.subtract, ALU.add))
                link(dve.tensor_scalar(sub_g[:, l:l + 1], col[:, COL["subln"] + l:COL["subln"] + l + 1],
                                       1.0 - init, None, ALU.mult))
            dve.wait_ge(boot_done, 15)
            dve.tensor_copy(sinks[:, :], bank[6][:, 0:8]).then_inc(taken[6], 1)
            for v in range(2):
                dve.wait_ge(boot_done, 16 + v)
                dve.tensor_scalar(tables[:, v, :], bank[5 + v][0:8, :], 8.0, None, ALU.mult).then_inc(taken[5 + v], 1)

            def rstd_of(name, w):
                x0 = plan.at(name, "xn")
                if x0:
                    dve.wait_ge(xn_ready, x0)
                dve.wait_ge(taken[4], plan.at(name, "b4") + 1)
                dve.reciprocal(rstd[:, 0, 0:w], root[:, 0, 0:w]).then_inc(rstd_ready, 1)
                dve.wait_ge(rstd_ready, plan.at(name, "rstd") + 1)

            def split_u(k, src, u0, w, t0):
                dve.tensor_copy(u_hi[:, k, t0:t0 + w], src).then_inc(u_part, 1)
                dve.wait_ge(u_part, u0 + k + 1)
                dve.tensor_tensor(u_lo[:, k, t0:t0 + w], src, u_hi[:, k, t0:t0 + w].bitcast(f32), ALU.subtract) \
                   .then_inc(u_ready, 1)

            def norm_u(name, src, gain, t0):
                x0, u0 = plan.at(name, "xn"), plan.at(name, "u")
                rstd_of(name, S)
                for k in range(KD):
                    if u0 + k >= 2:
                        dve.wait_ge(u_ready, u0 + k - 1)
                    dve.scalar_tensor_tensor(xn[:, k % 2, 0:S], src(k), col[:, COL[gain] + k:COL[gain] + k + 1],
                                             rstd[:, 0, 0:S], ALU.mult, ALU.mult).then_inc(xn_ready, 1)
                    dve.wait_ge(xn_ready, x0 + k + 1)
                    split_u(k, xn[:, k % 2, 0:S], u0, S, t0)

            def norm_x(name, gain, dst=None):
                x0, n0 = plan.at(name, "xn"), plan.at(name, "upd")
                rstd_of(name, S)
                for k in range(KD):
                    g = col[:, COL[gain] + k:COL[gain] + k + 1]
                    if dst is not None:
                        dve.scalar_tensor_tensor(dst[:, k, :], x[:, k, S:T], g, rstd[:, 0, 0:S], ALU.mult, ALU.mult) \
                           .then_inc(updated, 1)
                        continue
                    if k >= 2:
                        dve.wait_ge(updated, n0 + k - 1)
                    dve.scalar_tensor_tensor(xn[:, k % 2, 0:S], y[:, k, :], g, rstd[:, 0, 0:S], ALU.mult, ALU.mult) \
                       .then_inc(xn_ready, 1)
                    dve.wait_ge(xn_ready, x0 + k + 1)
                    dve.tensor_tensor(x[:, k, S:T], x[:, k, S:T], xn[:, k % 2, 0:S], ALU.add).then_inc(updated, 1)

            def norm_mod(name, halves):
                x0, u0, m0 = plan.at(name, "xn"), plan.at(name, "u"), plan.at(name, "xm")
                w, t = S * len(halves), span(halves)
                rstd_of(name, w)
                for k in range(KD + 1):
                    if k < KD:
                        if k >= 2:
                            dve.wait_ge(xm_ready, m0 + k - 1)
                        dve.tensor_tensor(xn[:, k % 2, 0:w], x[:, k, t], rstd[:, 0, 0:w], ALU.mult).then_inc(xn_ready, 1)
                    if k >= 1:
                        dve.wait_ge(xm_ready, m0 + k)
                        split_u(k - 1, work[:, (k - 1) % 2, 0:w], u0, w, t.start)

            def gemm(name, body):
                st = gemms[name]
                if st.bodies == 1:
                    body(st, 0)
                else:
                    with dve.Fori(0, st.bodies) as i:
                        body(st, i)

            def multiply_gates(dst, w, cols, base):
                def body(st, i):
                    for b in range(4):
                        dve.wait_ge(taken[b], st.taken(i, b))
                        at = dst[:, bass.ds(i * 4 + b, 1), cols]
                        dve.tensor_tensor(at, at, work[:, b:b + 1, 0:w], ALU.mult).then_inc(gated, 1)
                return body

            def split_merged(k, src, hi, lo, n0):
                dve.tensor_copy(hi, src).then_inc(dve_step, 1)
                steps[0] += 1
                dve.wait_ge(dve_step, steps[0])
                dve.tensor_tensor(lo, src, hi.bitcast(f32), ALU.subtract).then_inc(merged_ready, 1)
                dve.wait_ge(merged_ready, n0 + k + 1)

            norm_u("n_mem", lambda k: y[:, k, :], "g_mem", 0)
            norm_u("n_mix", lambda k: x[:, k, S:T], "g_mix_pre", S)

            def max1(n):
                kind, h = UNITS1[n]
                scale = 0.125 if kind != "mem" else 1.0 / math.sqrt(128)
                dve.wait_ge(score_ready, n + 1)
                st_ = stat[:, n % 2, :]
                link(dve.tensor_reduce(st_[:, 0:2], bank[n % 2][:, :].rearrange("p (q k) -> p q k", q=2), AX.X, ALU.max))
                if kind == "swa":
                    link(dve.tensor_scalar(st_[:, 0:2], st_[:, 0:2], scale, sinks[:, h:h + 1], ALU.mult, ALU.max))
                    dve.tensor_scalar(st_[:, 2:4], st_[:, 0:2], -1.0, None, ALU.mult).then_inc(nmax_ready, 1)
                else:
                    dve.tensor_scalar(st_[:, 2:4], st_[:, 0:2], -scale, None, ALU.mult).then_inc(nmax_ready, 1)

            def probs1(n):
                kind, h = UNITS1[n]
                dve.wait_ge(taken[n % 2], plan.at("att1", f"b{n % 2}") + n // 2 + 1)
                st_ = stat[:, n % 2, :]
                if kind == "swa":
                    link(dve.tensor_tensor(st_[:, 4:6], st_[:, 4:6], st_[:, 6:8], ALU.add))
                link(dve.reciprocal(st_[:, 8:10], st_[:, 4:6]))
                for q in range(2):
                    p = work[:, n % 2, q * S:(q + 1) * S]
                    ins = dve.tensor_scalar(p, p, st_[:, 8 + q:9 + q], None, ALU.mult)
                ins.then_inc(prob_ready, 1)

            def out1(n):
                kind, h = UNITS1[n]
                b = 4 + n % 2
                dve.wait_ge(o_done, n + 1)
                if kind == "moba":
                    tile, to, of, w = h // 2, 64 * (h % 2), 64 * (h % 2), 64
                elif kind == "swa":
                    tile, to, of, w = 4 + h // 2, 64 * (h % 2), 64 * (h // 4), 64
                else:
                    tile, to, of, w = 8 + h, 0, 0, P
                if n >= 2:
                    dve.wait_ge(o_ready, n - 1)
                src = work[to:to + w, 2 + n % 2, 0:S]
                dve.tensor_copy(src, bank[b][of:of + w, 0:S]).then_inc(taken[b], 1)
                dve.wait_ge(taken[b], plan.at("att1", f"b{b}") + n // 2 + 1)
                link(dve.tensor_copy(o1_hi[to:to + w, tile, :], src))
                dve.tensor_tensor(o1_lo[to:to + w, tile, :], src, o1_hi[to:to + w, tile, :].bitcast(f32), ALU.subtract) \
                   .then_inc(o_ready, 1)

            n_units = len(UNITS1)
            dve.wait_ge(u_ready, 2 * KD)
            for n in range(n_units + 2):
                if n < n_units:
                    max1(n)
                if 1 <= n <= n_units:
                    probs1(n - 1)
                if n >= 2:
                    out1(n - 2)
            gemm("gates1", multiply_gates(branch, S, slice(0, S), 0))
            dve.wait_ge(gated, 24 + 1)
            dve.wait_ge(o_ready, n_units)
            for k in range(KD):
                m = xn[:, k % 2, 0:S]
                link(dve.tensor_tensor(m, branch[:, k, :], branch[:, KD + k, :], ALU.add))
                link(dve.tensor_tensor(m, m, branch[:, 2 * KD + k, :], ALU.add))
                split_merged(k, m, o1_hi[:, k, :], o1_lo[:, k, :], 0)
            norm_x("n_mix_post", "g_mix_post")
            dve.wait_ge(updated, KD)
            norm_u("n_ffn", lambda k: x[:, k, S:T], "g_ffn_pre", S)

            def split_hidden(i, t, base, src, hi, lo):
                dve.tensor_copy(hi, src).then_inc(hid_part, 1)
                dve.wait_ge(hid_part, i * 2 + (base + t + 1))
                dve.tensor_tensor(lo, src, hi.bitcast(f32), ALU.subtract).then_inc(hid_ready, 1)

            def conv_ffn(st, i):
                for b in range(4):
                    c, t = b // 2, b % 2
                    at = i * 2 + (c * KF + t)
                    dve.wait_ge(cv_first, i * 4 + (b + 1))
                    dve.scalar_tensor_tensor(work[:, b, 1:S], bank[b][:, 0:S - 1], col[:, bass.ds(at + COL["conv_w1"], 1)],
                                             work[:, b, 1:S], ALU.mult, ALU.add).then_inc(cv_mid, 1)
                    dve.wait_ge(cv_mid, i * 4 + (b + 1))
                    dve.scalar_tensor_tensor(work[:, b, 2:S], bank[b][:, 0:S - 2], col[:, bass.ds(at + COL["conv_w0"], 1)],
                                             work[:, b, 2:S], ALU.mult, ALU.add).then_inc(taken[b], 1)
                dve.wait_ge(hid_ready, i * 2 + 1)
                for t in range(2):
                    dve.wait_ge(gelu_ready, i * 2 + (t + 1))
                    dve.wait_ge(taken[2 + t], st.taken(i, 2 + t))
                    prod = work[:, t, S:2 * S]
                    dve.tensor_tensor(prod, work[:, t, 0:S], work[:, 2 + t, 0:S], ALU.mult).then_inc(hid_prod, 1)
                    dve.wait_ge(hid_prod, i * 2 + (t + 1))
                    at = bass.ds(i * 2 + t, 1)
                    split_hidden(i, t, 0, work[:, t:t + 1, S:2 * S], hid1_hi[:, at, :], hid1_lo[:, at, :])

            gemm("up1", conv_ffn)

            def copy_y(st, i):
                for t in range(2):
                    dve.wait_ge(group_done, st.done(i, 2 * t + 2))
                    dve.tensor_copy(y[:, bass.ds(i * 2 + t, 1), :], bank[t][:, 0:S].rearrange("p (o t) -> p o t", o=1)) \
                       .then_inc(taken[t], 1)

            gemm("down1", copy_y)
            norm_x("n_ffn_post", "g_ffn_post")

            def modulation(l):
                dve.wait_ge(mod_used, (l + 1) * MOD_TILES)
                for h in range(2):
                    ins = dve.tensor_tensor(mod[:, :, h], bank[7][:, h:2 * MOD_TILES:2],
                                            col[:, COL[f"b_mod{l}"]:COL[f"b_mod{l}"] + MOD_TILES], ALU.add)
                ins.then_inc(taken[7], 1)
                dve.wait_ge(taken[7], l + 1)
                for i in range(3):
                    g0 = COL["norm_g"] + (3 * l + i) * KD
                    for h in range(2):
                        dve.scalar_tensor_tensor(mod_a[:, i, :, h], mod[:, (3 * i + 1) * KD:(3 * i + 2) * KD, h], 1.0,
                                                 col[:, g0:g0 + KD], ALU.add, ALU.mult)
                    ins = dve.tensor_scalar(mod_g[:, i, :, :], mod[:, (3 * i + 2) * KD:(3 * i + 3) * KD, :],
                                            1.0 if i == 1 else 0.5, None, ALU.mult)
                ins.then_inc(mod_taken, 1)
                dve.wait_ge(mod_taken, l + 1)

            def ffn(name, base, w):
                def body(st, i):
                    dve.wait_ge(hid_ready, i * 2 + (base + 1))
                    for t in range(2):
                        dve.wait_ge(group_done, st.done(i, 3 + t))
                        dve.wait_ge(taken[t], st.taken(i, t))
                        dve.tensor_tensor(work[:, 2 + t, 0:w], bank[2 + t][:, 0:w], work[:, t, 0:w], ALU.mult) \
                           .then_inc(taken[2 + t], 1)
                        dve.wait_ge(taken[2 + t], st.taken(i, 2 + t))
                        at = bass.ds(i * 2 + t, 1)
                        split_hidden(i, t, base, work[:, 2 + t:3 + t, 0:w], hid2_hi[:, at, 0:w], hid2_lo[:, at, 0:w])
                gemm(name, body)

            def residual(i_mod, halves, per, tiles):
                def body(st, i):
                    for t in range(tiles):
                        dve.wait_ge(group_done, st.done(i, per(t)))
                        for h in halves:
                            at = x[:, bass.ds(i * tiles + t, 1), h * S:(h + 1) * S]
                            lo = (h - halves[0]) * S
                            ins = dve.scalar_tensor_tensor(at, bank[t][:, lo:lo + S].rearrange("p (o t) -> p o t", o=1),
                                                           mod_g[:, i_mod, bass.ds(i * tiles + t, 1), h], at,
                                                           ALU.mult, ALU.add)
                        ins.then_inc(taken[t], 1)
                return body

            def layer(l):
                both, q_h, m_h = [CTX, LAT], halves_of(l, "q"), halves_of(l, "merge")
                wq, wm = S * len(q_h), S * len(m_h)
                modulation(l)
                norm_mod(f"n0_{l}", both)
                ffn(f"up_{l}0", KF * (1 + 2 * l), T)
                gemm(f"down_{l}0", residual(0, both, lambda t: 2 * t + 2, 2))
                norm_mod(f"n1_{l}", both)
                r0 = rope_base(l)
                tiles = rope_tiles(l)
                for n, (t, j) in enumerate(tiles):
                    b = 4 + n % 2
                    cur = (q2 if t == 0 else k2)[:, j, S:T]
                    tmp = xn[:, n % 2, 0:S]
                    dve.wait_ge(rot_done, r0 + n + 1)
                    dve.tensor_tensor(tmp, bank[b][:, 0:S], sin, ALU.mult).then_inc(taken[b], 1)
                    dve.wait_ge(taken[b], plan.at(f"rope_{l}", f"b{b}") + n // 2 + 1)
                    link(dve.tensor_tensor(cur, cur, cos, ALU.mult))
                    dve.tensor_tensor(cur, cur, tmp, ALU.add).then_inc(rope_ready, 1)
                    dve.wait_ge(rope_ready, r0 + n + 1)
                n = 0
                y0 = yf_base(l)
                for g in range(4):
                    for h in q_h:
                        tmp = xn[:, n % 2, 0:S]
                        hi, lo = yf_hi[:, g, h * S:(h + 1) * S], yf_lo[:, g, h * S:(h + 1) * S]
                        dve.wait_ge(dft_done, dft_base(l) + 2 * n + 2)
                        dve.tensor_copy(tmp, bank[5][:, 0:S]).then_inc(taken[5], 1)
                        dve.wait_ge(taken[5], plan.at(f"four_{l}", "b5") + n + 1)
                        link(dve.tensor_copy(hi, tmp))
                        dve.tensor_tensor(lo, tmp, hi.bitcast(f32), ALU.subtract).then_inc(yf_ready, 1)
                        dve.wait_ge(yf_ready, y0 + n + 1)
                        n += 1
                units = att_units(l)
                u0, p0 = plan.at(f"att_{l}", "unit"), plan.at(f"att_{l}", "pair")

                def maxima(n):
                    h, half, qb = units[n]
                    nk = T if half == LAT else S
                    st_ = stat[:, n % 2, :]
                    dve.wait_ge(score_ready, n_units + u0 + n + 1)
                    for c in range(2):
                        link(dve.tensor_reduce(st_[:, c:c + 1], bank[2 * (n % 2) + c][:, 0:nk], AX.X, ALU.max))
                    dve.tensor_scalar(st_[:, 2:4], st_[:, 0:2], -0.125, None, ALU.mult).then_inc(nmax_ready, 1)

                def differences(n):
                    h, half, qb = units[n]
                    nk = T if half == LAT else S
                    st_ = stat[:, n % 2, :]
                    for c in range(2):
                        b = 2 * (n % 2) + c
                        dve.wait_ge(taken[b], plan.at(f"att_{l}", f"b{b}") + n // 2 + 1)
                    link(dve.reciprocal(st_[:, 8:10], st_[:, 4:6]))
                    link(dve.tensor_tensor(st_[:, 9:10], st_[:, 9:10], lam[:, l:l + 1], ALU.mult))
                    p1, p2 = work[:, 2 * (n % 2), 0:nk], work[:, 2 * (n % 2) + 1, 0:nk]
                    link(dve.tensor_scalar(p2, p2, st_[:, 9:10], None, ALU.mult))
                    dve.scalar_tensor_tensor(p1, p1, st_[:, 8:9], p2, ALU.mult, ALU.subtract).then_inc(prob_ready, 1)

                def heads(p):
                    h, half, _ = units[2 * p]
                    dve.wait_ge(o_done, n_units + p0 + p + 1)
                    dve.tensor_copy(q2[:, h, half * S:(half + 1) * S], bank[6][:, 0:S]).then_inc(taken[6], 1)

                for n in range(len(units) + 2):
                    if n < len(units):
                        maxima(n)
                    if 1 <= n <= len(units):
                        differences(n - 1)
                    if n >= 3 and n % 2 == 1:
                        heads((n - 3) // 2)
                r0, x0, o0 = (plan.at(f"subln_{l}", k) for k in ("rstd", "xn", "o"))
                for h in range(KD):
                    b = 4 + h % 2
                    dve.wait_ge(taken[b], plan.at(f"subln_{l}", f"b{b}") + h // 2 + 1)
                    dve.wait_ge(xn_ready, x0 + h)
                    dve.reciprocal(rstd[:, h % 2, 0:wq], root[:, h % 2, 0:wq]).then_inc(rstd_ready, 1)
                    dve.wait_ge(rstd_ready, r0 + h + 1)
                    tmp = work[:, h % 2, 0:wq]
                    dve.scalar_tensor_tensor(tmp, q2[:, h, span(q_h)], sub_g[:, l:l + 1], rstd[:, h % 2, 0:wq],
                                             ALU.mult, ALU.mult).then_inc(xn_ready, 1)
                    dve.wait_ge(xn_ready, x0 + h + 1)
                    hi, lo = o2_hi[:, h, span(q_h)], o2_lo[:, h, span(q_h)]
                    link(dve.tensor_copy(hi, tmp))
                    dve.tensor_tensor(lo, tmp, hi.bitcast(f32), ALU.subtract).then_inc(o_ready, 1)
                    dve.wait_ge(o_ready, n_units + o0 + h + 1)
                for n, dst in enumerate((q2, fr)):
                    gemm(f"gates_{l}{n}", multiply_gates(dst, wm, span(m_h), gate_base(l, n)))
                dve.wait_ge(gated, gate_base(l, 1) + 8 + 1)
                for k in range(KD):
                    m = xn[:, k % 2, 0:wm]
                    link(dve.tensor_tensor(m, q2[:, k, span(m_h)], fr[:, k, span(m_h)], ALU.add))
                    split_merged(k, m, o2_hi[:, k, span(m_h)], o2_lo[:, k, span(m_h)], KD * (1 + l))
                gemm(f"w_o_{l}", residual(1, m_h, lambda t: t + 1, 4))
                norm_mod(f"n2_{l}", m_h)
                ffn(f"up_{l}1", KF * (2 + 2 * l), wm)
                gemm(f"down_{l}1", residual(2, m_h, lambda t: 2 * t + 2, 2))

            for l in range(LAYERS):
                layer(l)
            norm_x("n_final", "g_final", fin)
            for n in range(4):
                tt, b = n // 2, 5 + n % 2
                dve.wait_ge(boot_done, 17 + n + 1)
                dve.tensor_copy(rows_out[:, tt, (n % 2) * 512:(n % 2) * 512 + 512], bank[b][:, :]).then_inc(taken[b], 1)

        @block.tensor
        def _(pe):
            def claim(step, b, nth=0):
                n = plan.at(step, f"b{b}") + nth
                if n > 0:
                    pe.wait_ge(taken[b], n)

            def three(dst, hi, lo, m_hi, m_lo, first, final, swap=False):
                for n, (w, m) in enumerate(((hi, m_hi), (hi, m_lo), (lo, m_hi))):
                    s, v = (m, w) if swap else (w, m)
                    ins = pe.matmul(dst, s, v, start=first and n == 0, stop=final and n == 2)
                return ins

            def modulate(st, i):
                for c in range(2):
                    pair = i + (st.mod0 + st.mod * MOD_TILES // 2)
                    pe.wait_ge(mod_ready[c], pair * 16 + 16)
                    for k in range(KD):
                        ins = pe.matmul(bank[7][:, bass.ds(i * 4 + (st.mod0 * 4 + 2 * c), 2)], mod_raw[c][:, k, :],
                                        cond[:, k, :], start=k == 0, stop=k == KD - 1)
                    ins.then_inc(mod_used, 1)

            def gemm(name, block_of):
                st = gemms[name]
                if st.mod is not None and st.mod0 == 0 and st.mod == 1:
                    pe.wait_ge(taken[7], 1)

                def body(i):
                    for c in range(st.per):
                        n = st.first + c
                        pe.wait_ge(lo_ready, i * st.per + (n + 1))
                        block_of(st, i, c, n % 2)
                    if st.mod is not None:
                        modulate(st, i)

                if st.bodies == 1:
                    body(0)
                else:
                    with pe.Fori(0, st.bodies) as i:
                        body(i)

            def claim_tile(st, i, b):
                pe.wait_ge(taken[b], i + st.use0[b]) if st.use0[b] > 0 or not isinstance(i, int) else None

            def features(m_hi, m_lo, w):
                def block_of(st, i, c, slot):
                    for t in range(2):
                        b = 2 * c + t
                        claim_tile(st, i, b)
                        for k in range(st.kt):
                            at = slice(k * BLK + t * P, k * BLK + (t + 1) * P)
                            ins = three(bank[b][:, 0:w], w_hi[slot][:, at], w_lo[slot][:, at], m_hi(k), m_lo(k),
                                        k == 0, k == st.kt - 1)
                        ins.then_inc(group_done, 1)
                return block_of

            def token_rows(t0, tiles):
                def block_of(st, i, c, slot):
                    for t in range(tiles):
                        b = 2 * c + t // 2
                        if t % 2 == 0:
                            claim_tile(st, i, b)
                        cols = slice(t0 + t * P, t0 + (t + 1) * P)
                        for k in range(KD):
                            at = slice(k * BLK, (k + 1) * BLK)
                            ins = three(bank[b][:, (t % 2) * BLK:(t % 2 + 1) * BLK], w_hi[slot][:, at], w_lo[slot][:, at],
                                        u_hi[:, k, cols], u_lo[:, k, cols], k == 0, k == KD - 1, swap=True)
                        if t % 2 == 1:
                            ins.then_inc(group_done, 1)
                return block_of

            def down_strips(h_hi, h_lo, w):
                def block_of(st, i, c, slot):
                    b, part = c // 2, c % 2
                    if part == 0:
                        claim_tile(st, i, b)
                    for k in range(DOWN_KT):
                        at = slice(k * P, (k + 1) * P)
                        kk = part * DOWN_KT + k
                        ins = three(bank[b][:, 0:w], w_hi[slot][:, at], w_lo[slot][:, at], h_hi[:, kk, 0:w], h_lo[:, kk, 0:w],
                                    kk == 0, kk == KF - 1)
                    ins.then_inc(group_done, 1)
                return block_of

            def u_of(cols):
                return (lambda k: u_hi[:, k, cols]), (lambda k: u_lo[:, k, cols])

            def sum_squares(name, w):
                q0 = plan.at(name, "sq")
                claim(name, 4)
                for k in range(KD):
                    pe.wait_ge(sq_ready, q0 + k + 1)
                    pe.matmul(bank[4][:, 0:w], ones[:, :], sq[:, k % 2, 0:w], start=k == 0, stop=k == KD - 1) \
                      .then_inc(sq_used, 1)

            def wait_u(name):
                pe.wait_ge(u_ready, plan.at(name, "u") + KD)

            pe.wait_ge(const_ready, 16)
            pe.wait_ge(rows_ready, 16 * len(ROWS))
            at = 0
            for t, rows_of in enumerate(ROW_TILES):
                n = sum(r for _, r in rows_of)
                ins = pe.transpose(bank[6][:, at:at + n], rows[0:n, t, :], ident[0:n, 0:n])
                at += n
            ins.then_inc(boot_done, 1)
            for n in range(12):
                s, q = n // 4, n % 4
                if q == 0:
                    pe.wait_ge(tok_ready[s], 16)
                claim("boot", 4 + n % 2, n // 2)
                for f in range(2):
                    for tt in range(2):
                        ins = pe.transpose(bank[4 + n % 2][:, f * S + tt * P:f * S + (tt + 1) * P],
                                           tok[:, s, tt, (2 * q + f) * P:(2 * q + f + 1) * P], ident)
                ins.then_inc(boot_done, 1)
            pe.wait_ge(set_ready, 6)
            claim("boot", 5, 6)
            pe.matmul(bank[5][:, 16:20], ones[0:1, :], lam_s[:, :, :].rearrange("p l j -> p (l j)"), start=True, stop=True) \
              .then_inc(boot_done, 1)
            claim("boot", 6, 1)
            pe.wait_ge(rel_ready, 64)
            pe.matmul(bank[6][:, 0:8], ones[0:1, :], sink_row[:, :], start=True, stop=True).then_inc(boot_done, 1)
            claim("boot", 5, 7)
            pe.matmul(bank[5][0:8, :], rel[:, 0:8], hot[:, 0, :], start=True, stop=True).then_inc(boot_done, 1)
            claim("boot", 6, 2)
            pe.matmul(bank[6][0:8, :], rel[:, 8:16], hot[:, 1, :], start=True, stop=True).then_inc(boot_done, 1)
            pe.wait_ge(cond_ready, 1)

            mem_cols, x_cols = slice(0, S), slice(S, T)
            sum_squares("n_mem", S)
            wait_u("n_mem")
            gemm("k_me", features(*u_of(mem_cols), S))
            gemm("v_me", token_rows(0, 2))
            sum_squares("n_mix", S)
            wait_u("n_mix")
            gemm("qk_mb", features(*u_of(x_cols), S))
            gemm("v_mb", token_rows(S, 2))
            gemm("q_sw", features(*u_of(x_cols), S))

            def kv_sw(st, i, c, slot):
                claim_tile(st, 0, 0)
                for k in range(KD):
                    at = slice(k * BLK, k * BLK + P)
                    ins = three(bank[0][:, 0:S], w_hi[slot][:, at], w_lo[slot][:, at], u_hi[:, k, x_cols], u_lo[:, k, x_cols],
                                k == 0, k == KD - 1)
                ins.then_inc(group_done, 1)
                claim_tile(st, 0, 1)
                for t in range(2):
                    cols = slice(S + t * P, S + (t + 1) * P)
                    for k in range(KD):
                        at = slice(k * BLK + P, (k + 1) * BLK)
                        ins = three(bank[1][:, t * P:(t + 1) * P], w_hi[slot][:, at], w_lo[slot][:, at],
                                    u_hi[:, k, cols], u_lo[:, k, cols], k == 0, k == KD - 1, swap=True)
                ins.then_inc(group_done, 1)

            gemm("kv_sw", kv_sw)
            gemm("q_me", features(*u_of(x_cols), S))

            def scores1(n):
                kind, h = UNITS1[n]
                b = n % 2
                claim("att1", b, n // 2)
                if kind == "moba":
                    r = slice(64 * (h % 2), 64 * (h % 2) + 64)
                    q, k, table = qk_mb[r, h // 2, :], qk_mb[r, 4 + h // 2, :], h
                elif kind == "swa":
                    r = slice(64 * (h % 2), 64 * (h % 2) + 64)
                    q, k, table = q_sw[r, h // 2, :], k_sw[r, h // 4, :], 8 + h
                else:
                    q, k, table = q_me[:, h, :], k_me[:, h, :], None
                for qb in range(2):
                    dst = bank[b][:, qb * S:(qb + 1) * S]
                    ins = pe.matmul(dst, q[:, qb * P:(qb + 1) * P], k, start=True, stop=table is None)
                    if table is not None:
                        shift = P * (1 - qb)
                        ins = pe.matmul(dst, reverse, hank[:, table, shift:shift + S], start=False, stop=True)
                ins.then_inc(score_ready, 1)

            def transposes1(n):
                b = 2 + n % 2
                pe.wait_ge(prob_ready, n + 1)
                claim("att1", b, n // 2)
                for kt in range(2):
                    for qb in range(2):
                        ins = pe.transpose(bank[b][:, kt * S + qb * P:kt * S + (qb + 1) * P],
                                           work[:, n % 2, qb * S + kt * P:qb * S + (kt + 1) * P], ident)
                ins.then_inc(pt_done, 1)

            def outputs1(n):
                kind, h = UNITS1[n]
                b = 4 + n % 2
                pe.wait_ge(taken[2 + n % 2], plan.at("att1", f"b{2 + n % 2}") + n // 2 + 1)
                claim("att1", b, n // 2)
                for kt in range(2):
                    if kind == "moba":
                        v = v_mb[:, kt, (h // 2) * P:(h // 2 + 1) * P]
                    elif kind == "swa":
                        v = v_sw[:, kt, :]
                    else:
                        v = v_me[:, kt, h * P:(h + 1) * P]
                    ins = pe.matmul(bank[b][:, 0:S], v, p_t[:, n % 2, kt, :], start=kt == 0, stop=kt == 1)
                ins.then_inc(o_done, 1)

            for name, b in (("q_me", 0), ("q_me", 1), ("q_me", 2), ("q_me", 3)):
                pe.wait_ge(taken[b], gemms[name].taken(0, b))
            pe.wait_ge(hank_ready, 16)
            n_units = len(UNITS1)
            for n in range(n_units + 2):
                if n < n_units:
                    scores1(n)
                if 1 <= n <= n_units:
                    transposes1(n - 1)
                if n >= 2:
                    outputs1(n - 2)
            pe.wait_ge(o_ready, n_units)
            for n in range(3):
                gemm(f"branch{n}", features(lambda k, n=n: o1_hi[:, 4 * n + k, :], lambda k, n=n: o1_lo[:, 4 * n + k, :], S))
            gemm("gates1", features(*u_of(x_cols), S))
            pe.wait_ge(merged_ready, KD)
            gemm("w_out", features(lambda k: o1_hi[:, k, :], lambda k: o1_lo[:, k, :], S))
            sum_squares("n_mix_post", S)
            sum_squares("n_ffn", S)
            wait_u("n_ffn")
            gemm("up1", features(*u_of(x_cols), S))
            pe.wait_ge(hid_ready, KF + 1)
            gemm("down1", down_strips(hid1_hi, hid1_lo, S))
            sum_squares("n_ffn_post", S)

            def layer(l):
                both, q_h, m_h = [CTX, LAT], halves_of(l, "q"), halves_of(l, "merge")
                wq, wm = S * len(q_h), S * len(m_h)
                all_cols = slice(0, T)
                sum_squares(f"n0_{l}", T)
                wait_u(f"n0_{l}")
                gemm(f"up_{l}0", features(*u_of(all_cols), T))
                pe.wait_ge(hid_ready, KF * (2 + 2 * l) + 1)
                gemm(f"down_{l}0", down_strips(hid2_hi, hid2_lo, T))
                sum_squares(f"n1_{l}", T)
                wait_u(f"n1_{l}")
                gemm(f"q_{l}", features(*u_of(span(q_h)), wq))
                gemm(f"k_{l}", features(*u_of(all_cols), T))
                gemm(f"v_{l}", token_rows(0, 4))
                gemm(f"f_{l}", token_rows(span(q_h).start, 2 * len(q_h)))
                for b in range(4):
                    pe.wait_ge(taken[b], gemms[f"k_{l}"].taken(1, b))
                pe.wait_ge(tabs_ready, 16 * (l + 1))
                for n, (t, j) in enumerate(rope_tiles(l)):
                    b = 4 + n % 2
                    claim(f"rope_{l}", b, n // 2)
                    pe.matmul(bank[b][:, 0:S], rot, (q2 if t == 0 else k2)[:, j, S:T], start=True, stop=True) \
                      .then_inc(rot_done, 1)
                st = gemms[f"f_{l}"]
                for b in st.banks:
                    pe.wait_ge(taken[b], st.taken(0, b))
                n = 0
                for g in range(4):
                    for h in q_h:
                        claim(f"four_{l}", 4, n)
                        for tt in range(2):
                            ins = pe.matmul(bank[4][:, :], f2[:, 2 * h + tt, g * P:(g + 1) * P],
                                            table(C_DFT + 512 * tt, 512), start=tt == 0, stop=tt == 1)
                        ins.then_inc(dft_done, 1)
                        claim(f"four_{l}", 5, n)
                        pe.wait_ge(taken[4], plan.at(f"four_{l}", "b4") + n + 1)
                        for s, c in enumerate((C_DC, C_DS)):
                            ins = pe.matmul(bank[5][:, 0:S], table(c, P), dft[:, n % 2, s * S:(s + 1) * S],
                                            start=s == 0, stop=s == 1)
                        ins.then_inc(dft_done, 1)
                        n += 1
                units = att_units(l)
                u0, p0 = plan.at(f"att_{l}", "unit"), plan.at(f"att_{l}", "pair")
                pe.wait_ge(rope_ready, rope_base(l) + 16)

                def scores(n):
                    h, half, qb = units[n]
                    nk = T if half == LAT else S
                    at = half * S + qb * P
                    for c in range(2):
                        b = 2 * (n % 2) + c
                        claim(f"att_{l}", b, n // 2)
                        r = slice(64 * c, 64 * c + 64)
                        ins = pe.matmul(bank[b][:, 0:nk], q2[r, h, at:at + P], k2[r, h, 0:nk], start=True, stop=True)
                    ins.then_inc(score_ready, 1)

                def transposes(n):
                    h, half, qb = units[n]
                    kt = 4 if half == LAT else 2
                    pe.wait_ge(prob_ready, n_units + u0 + n + 1)
                    claim(f"att_{l}", 4 + n % 2, n // 2)
                    for k in range(kt):
                        ins = pe.transpose(bank[4 + n % 2][:, k * P:(k + 1) * P],
                                           work[:, 2 * (n % 2), k * P:(k + 1) * P], ident)
                    ins.then_inc(pt_done, 1)

                def outputs(p):
                    h, half, _ = units[2 * p]
                    kt = 4 if half == LAT else 2
                    for b in (4, 5):
                        pe.wait_ge(taken[b], plan.at(f"att_{l}", f"b{b}") + p + 1)
                    claim(f"att_{l}", 6, p)
                    for k in range(kt):
                        ins = pe.matmul(bank[6][:, 0:S], v2[:, k, h * P:(h + 1) * P], a_t[:, p % 2, k, :],
                                        start=k == 0, stop=k == kt - 1)
                    ins.then_inc(o_done, 1)

                for n in range(len(units) + 2):
                    if n < len(units):
                        scores(n)
                    if 1 <= n <= len(units):
                        transposes(n - 1)
                    if n >= 3 and n % 2 == 1:
                        outputs((n - 3) // 2)
                q0 = plan.at(f"subln_{l}", "sq")
                for h in range(KD):
                    b = 4 + h % 2
                    claim(f"subln_{l}", b, h // 2)
                    pe.wait_ge(sq_ready, q0 + h + 1)
                    pe.matmul(bank[b][:, 0:wq], ones[:, :], sq[:, h % 2, 0:wq], start=True, stop=True).then_inc(sq_used, 1)
                pe.wait_ge(o_ready, n_units + plan.at(f"subln_{l}", "o") + KD)
                m_cols = span(m_h)
                gemm(f"attn_out_{l}", features(lambda k: o2_hi[:, k, m_cols], lambda k: o2_lo[:, k, m_cols], wm))
                pe.wait_ge(yf_ready, yf_base(l) + 4 * len(q_h))
                gemm(f"four_out_{l}", features(lambda k: yf_hi[:, k, m_cols], lambda k: yf_lo[:, k, m_cols], wm))
                for n in range(2):
                    gemm(f"gates_{l}{n}", features(*u_of(m_cols), wm))
                pe.wait_ge(merged_ready, KD * (2 + l))
                gemm(f"w_o_{l}", features(lambda k: o2_hi[:, k, m_cols], lambda k: o2_lo[:, k, m_cols], wm))
                sum_squares(f"n2_{l}", wm)
                wait_u(f"n2_{l}")
                gemm(f"up_{l}1", features(*u_of(m_cols), wm))
                pe.wait_ge(hid_ready, KF * (3 + 2 * l) + 1)
                gemm(f"down_{l}1", down_strips(hid2_hi, hid2_lo, wm))

            for l in range(LAYERS):
                layer(l)
            sum_squares("n_final", S)
            pe.wait_ge(updated, 3 * KD)
            for n in range(4):
                tt, b = n // 2, 5 + n % 2
                claim("store", b, n // 2)
                for k in range(4):
                    ins = pe.transpose(bank[b][:, k * P:(k + 1) * P],
                                       fin[:, 4 * (n % 2) + k, tt * P:(tt + 1) * P], ident)
                ins.then_inc(boot_done, 1)


_INS = ["x", "mem", "norm_mix_pre", "norm_mix_post", "norm_ffn_pre", "norm_ffn_post", "norm_mem", "w_in", "rel_bias",
        "swa_sinks", "w_mem_kv", "w_branch_moba", "w_branch_swa", "w_branch_mem", "w_out", "w_ffn_up", "ffn_conv_w",
        "ffn_conv_b", "w_ffn_down", "c_2", "ctx_2", "c_ctx_2", "w_mod_2", "b_mod_2", "norm_g_2", "ffn_w_in_2",
        "ffn_w_out_2", "w_in_2", "b_gate_2", "lam_params_2", "subln_g_2", "w_attn_out_2", "w_four_out_2", "w_o_2",
        "final_g_2"]


def kernel(**inputs):
    import numpy as _np
    import concourse.bacc as _bacc
    from concourse import mybir as _mybir
    from concourse.bass_utils import run_bass_kernel_spmd as _run

    nc = _bacc.Bacc("TRN2", target_bir_lowering=False, num_devices=1, dynamic_dma_scratch_size=1024)
    arrays, aps = {}, {}
    consts = dict(zip(("shape_const", "shape_hot"), shape_constants()))
    for name, v in [(n, inputs[n]) for n in _INS] + list(consts.items()):
        v = _np.ascontiguousarray(v)
        arrays[f"in_{name}"] = v
        aps[name] = nc.dram_tensor(f"in_{name}", v.shape, _mybir.dt.from_np(v.dtype), kind="ExternalInput").ap()
    out = nc.dram_tensor("out_rows", (1, S, D), _mybir.dt.float32, kind="ExternalOutput").ap()
    two_blocks(nc, aps, out)
    r = _run(nc, [arrays], core_ids=[0])
    return r.results[0]["out_rows"]
```

```python
import math
from contextlib import ExitStack

import numpy as np
import concourse.bass as bass
from concourse import mybir

P = 128
D = 1024
KD = D // P
S = 256
T = 2 * S
F = 2816
KF = F // P
EPS = 1e-6
LAYERS = 2
N_MOD = 9
MOD_TILES = N_MOD * KD
MOD_PAIRS = MOD_TILES // 2
BLK = 256
DOWN_KT = KF // 2
MASKED = -1e30
T_LAG, O_LAG = 3, 4
HANK = 3 * P
CTX, LAT = 0, 1

ROWS = {}
ROW_TILES = [
    [("g_mix_pre", 8), ("g_mix_post", 8), ("g_ffn_pre", 8), ("g_ffn_post", 8), ("g_mem", 8),
     ("norm_g", 48), ("b_gate", 32), ("g_final", 8)],
    [("conv_w0", 44), ("conv_w1", 44), ("c_ctx", 8), ("c_lat", 8), ("subln", 2)],
    [("conv_w2", 44), ("conv_b", 44)],
    [("b_mod0", 72)],
    [("b_mod1", 72)],
]
COL = {}
_at = 0
for _t, _rows in enumerate(ROW_TILES):
    _r = 0
    for _name, _n in _rows:
        ROWS[_name] = (_t, _r, _n)
        COL[_name] = _at + _r
        _r += _n
    _at += _r
N_COLS = _at

C_ID, C_REV = 0, 128
N_CONST = 256
C_ROT, C_COS, C_SIN, C_DFT, C_DC, C_DS = 256, 384, 640, 896, 1920, 2048
N_TABS = 1920


def shape_constants():
    c = np.zeros((P, N_CONST + N_TABS), np.float32)
    c[:, C_ID:C_ID + P] = np.eye(P)
    c[:, C_REV:C_REV + P] = np.eye(P)[::-1]
    for g in range(0, P, 32):
        for j in range(16):
            c[g + 16 + j, C_ROT + g + j] = -1.0
            c[g + j, C_ROT + g + 16 + j] = 1.0
    inv = 1.0 / (10000.0 ** (np.arange(0, 32, 2, dtype=np.float32) / np.float32(32)))
    pos = np.arange(S)
    for r in range(P):
        w = r % 64
        p = (pos // 64 if w < 32 else pos % 64).astype(np.float32)
        ang = p * np.float32(inv[(w % 32) % 16])
        c[r, C_COS:C_COS + S] = np.cos(ang)
        c[r, C_SIN:C_SIN + S] = np.sin(ang)
    a = 2 * np.pi * (np.outer(np.arange(S), np.arange(S)) % S) / S
    for tt in range(2):
        at = C_DFT + 512 * tt
        c[:, at:at + S] = np.cos(a[tt * P:(tt + 1) * P])
        c[:, at + S:at + 2 * S] = np.sin(a[tt * P:(tt + 1) * P])
    b = 2 * np.pi * (np.outer(np.arange(P), np.arange(P)) % P) / P
    norm = 1.0 / math.sqrt(S * P)
    c[:, C_DC:C_DC + P] = np.cos(b) * norm
    c[:, C_DS:C_DS + P] = -np.sin(b) * norm
    hot = np.zeros((33, 2, 512), np.float32)
    for i in range(511):
        dist = 255 - i
        n = max(dist, 0)
        big = 16 + int(np.float32(np.log(np.float32(max(n, 1)) / np.float32(16)))
                       / np.float32(math.log(8.0)) * np.float32(16))
        bucket = n if n < 16 else min(big, 31)
        hot[bucket, :, i] = 1.0
        hot[32, 0, i] = float(dist < 0)
        hot[32, 1, i] = float(dist < 0 or dist >= 128)
    return c, hot.reshape(33, 1024)


class Plan:

    def __init__(self):
        self.total, self.before = {}, {}

    def add(self, step, **counts):
        self.before[step] = dict(self.total)
        for k, n in counts.items():
            self.total[k] = self.total.get(k, 0) + n

    def at(self, step, key):
        return self.before[step].get(key, 0)


class Gemm:

    def __init__(self, plan, name, src, blocks, per, kt, cols, gpb, banks, mod=False, acc=0):
        self.name, self.src, self.kt, self.cols = name, src, kt, cols
        self.per, self.bodies, self.gpb, self.banks = per, blocks // per, gpb, banks
        self.blocks = blocks
        self.first = plan.total.get("blk", 0)
        self.g0 = plan.total.get("grp", 0)
        self.mod = mod
        self.pair0 = plan.total.get("pair_mod", 0)
        self.acc0, self.acc = plan.total.get("acc", 0), acc
        counts = {f"b{b}": self.bodies for b in banks}
        counts["pair_mod"] = self.bodies if mod else 0
        counts["acc"] = 2 * acc * self.bodies
        plan.add(name, blk=blocks, grp=blocks * gpb, **counts)
        self.use0 = {b: plan.at(name, f"b{b}") for b in banks}

    def done(self, i, n):
        return self.g0 + self.gpb * self.per * i + n

    def taken(self, i, bank):
        return self.use0[bank] + i + 1


def make_plan(a):
    plan, gemms = Plan(), {}

    def gemm(name, src, blocks, per=2, kt=KD, cols=BLK, gpb=2, banks=(0, 1, 2, 3), mod=False, acc=0):
        gemms[name] = Gemm(plan, name, src, blocks, per, kt, cols, gpb, banks, mod, acc)

    def norm(name, kind, summed=False):
        plan.add(name, sq=0 if summed else KD, sums=1 if summed else KD, diag=1, bc=1, xn=KD, b4=1, **kind)

    TO_U, MOD_U, TO_X, TO_OUT = {"u": KD}, {"u": KD, "xm": KD}, {"upd": KD}, {"upd": KD}

    def cols(w, first):
        return lambda j: w[:, bass.ds(j * BLK + first, BLK)].rearrange("(k p) n -> p k n", p=P)

    def pairs(w):
        return lambda j, c: w[:, bass.ds(j * BLK + c * F, BLK)].rearrange("(k p) n -> p k n", p=P)

    def down(w):
        return lambda j, c: w[c * DOWN_KT * P:(c + 1) * DOWN_KT * P, bass.ds(j * P, P)] \
            .rearrange("(k p) n -> p k n", p=P)

    plan.add("boot", b4=6, b5=8, b6=3)
    w_in, w_kv = a["w_in"][0], a["w_mem_kv"][0]
    norm("n_mem", TO_U)
    norm("n_mix", TO_U)
    gemm("k_me", cols(w_kv, 0), 2)
    gemm("v_me", cols(w_kv, 512), 2, gpb=1, banks=(0, 2))
    gemm("qk_mb", cols(w_in, 0), 4, mod=True)
    gemm("v_mb", cols(w_in, 1024), 2, gpb=1, banks=(0, 2), mod=True)
    gemm("q_sw", cols(w_in, 1536), 2, mod=True)
    gemm("kv_sw", cols(w_in, 2048), 1, per=1, banks=(0, 1))
    gemm("q_me", cols(w_in, 2304), 2, mod=True)
    plan.add("att1", b0=10, b1=10, b2=10, b3=10, b4=10, b5=10)
    for n, w in enumerate(("w_branch_moba", "w_branch_swa", "w_branch_mem")):
        gemm(f"branch{n}", cols(a[w][0], 0), 4, kt=4)
    for n in range(3):
        gemm(f"gates1_{n}", cols(w_in, 2816 + n * D), 4, mod=n < 2)
    gemm("w_out", cols(a["w_out"][0], 0), 4, mod=True, acc=4)
    norm("n_mix_post", TO_X, summed=True)
    norm("n_ffn", TO_U)
    gemm("up1", pairs(a["w_ffn_up"][0]), 22)
    gemm("down1", down(a["w_ffn_down"][0]), 16, per=4, kt=DOWN_KT, cols=P, gpb=1, banks=(0, 1), mod=True, acc=2)
    norm("n_ffn_post", TO_X, summed=True)
    for l in range(LAYERS):
        last = l == LAYERS - 1
        w = a["w_in_2"][l]
        halves = 1 if last else 2
        norm(f"n0_{l}", MOD_U, summed=l > 0)
        gemm(f"up_{l}0", pairs(a["ffn_w_in_2"][l, 0]), 22, mod=True)
        gemm(f"down_{l}0", down(a["ffn_w_out_2"][l, 0]), 16, per=4, kt=DOWN_KT, cols=P, gpb=1, banks=(0, 1),
             mod=last, acc=2)
        norm(f"n1_{l}", MOD_U, summed=True)
        gemm(f"q_{l}", cols(w, 0), 4, mod=True)
        gemm(f"k_{l}", cols(w, 1024), 4, mod=True)
        gemm(f"f_{l}", cols(w, 3072), 2, gpb=halves, banks=(0, 2) if last else (0, 1, 2, 3))
        plan.add(f"rope_{l}", b4=16)
        plan.add(f"four_{l}", b5=4 * halves, b6=4 * halves)
        gemm(f"v_{l}", cols(w, 2048), 4)
        units = 16 * halves
        plan.add(f"att_{l}", b0=units // 2, b1=units // 2, b2=units // 2, b3=units // 2,
                 b4=units // 2, b5=units // 2, b6=units // 2, unit=units, pair=units // 2)
        gemm(f"four_out_{l}", cols(a["w_four_out_2"][l], 0), 4, kt=4)
        plan.add(f"subln_{l}", sq=KD, sums=1, diag=KD, bc=KD, xn=KD, o=KD, b4=1)
        gemm(f"gates_{l}1", cols(w, 4608), 4, mod=not last)
        gemm(f"attn_out_{l}", cols(a["w_attn_out_2"][l], 0), 4, mod=not last)
        gemm(f"gates_{l}0", cols(w, 3584), 4, mod=not last)
        gemm(f"w_o_{l}", cols(a["w_o_2"][l], 0), 4, mod=not last, acc=4)
        norm(f"n2_{l}", MOD_U, summed=True)
        gemm(f"up_{l}1", pairs(a["ffn_w_in_2"][l, 1]), 22, mod=not last)
        gemm(f"down_{l}1", down(a["ffn_w_out_2"][l, 1]), 16, per=4, kt=DOWN_KT, cols=P, gpb=1, banks=(0, 1),
             mod=not last, acc=2)
    norm("n_final", TO_OUT, summed=True)
    plan.add("store", b5=2, b6=2)
    assert plan.total["pair_mod"] == LAYERS * MOD_PAIRS
    for l in range(LAYERS):
        for i in range(3):
            assert plan.at(f"n{i}_{l}", "pair_mod") >= MOD_PAIRS * l + MOD_PAIRS // 3 * (i + 1)
    for st in gemms.values():
        assert not st.mod or st.pair0 // MOD_PAIRS == (st.pair0 + st.bodies - 1) // MOD_PAIRS
    return plan, gemms


def two_blocks(nc, a, out):
    f32, f32r = mybir.dt.float32, mybir.dt.float32r
    ACT, ALU, AX = mybir.ActivationFunctionType, mybir.AluOpType, mybir.AxisListType
    plan, gemms = make_plan(a)
    stream = list(gemms.values())
    scratch = nc.dram_tensor("bias_tables", (2, 8, 512), f32, kind="Internal").ap()

    ctx = ExitStack()
    with ctx:
        def sb(name, shape, dt=f32, on=ctx):
            return on.enter_context(nc.sbuf_tensor(name, shape, dt))

        def sem(name):
            return ctx.enter_context(nc.semaphore(name))

        raw = [sb(f"raw{n}", [P, 2048]) for n in range(2)]
        w_hi = [sb(f"w_hi{n}", [P, 2048], f32r) for n in range(2)]
        w_lo = [sb(f"w_lo{n}", [P, 2048], f32r) for n in range(2)]
        mod_raw = [sb(f"mod_raw{n}", [P, KD, P]) for n in range(2)]
        x = sb("x", [P, KD, T])
        u_hi = sb("u_hi", [P, KD, T], f32r)
        u_lo = sb("u_lo", [P, KD, T], f32r)
        const = sb("const", [P, N_CONST])
        ones = sb("ones", [P, P])
        eps = sb("eps", [P, 1])
        col = sb("col", [P, N_COLS])
        cond = sb("cond", [P, KD, 2])
        mod_acc = sb("mod_acc", [P, 2, 2, P])
        mod_sum = sb("mod_sum", [P, 2 * MOD_TILES])
        mod = sb("mod", [P, MOD_TILES, 2])
        mod_a = sb("mod_a", [P, 3, KD, 2])
        mod_g = sb("mod_g", [P, 3, KD, 2])
        sub_g = sb("sub_g", [P, LAYERS])
        sinks = sb("sinks", [P, 8])
        lam = sb("lam", [P, LAYERS])
        stat = sb("stat", [P, 2, 16])
        xn = sb("xn", [P, 2, T])
        root = sb("root", [P, 2, T])
        diag = root[:, 0, :].rearrange("p (t q) -> p t q", t=4)
        probs = root
        rms = sb("rms", [P, 2, 4 * KD])
        work = sb("work", [P, 4, T])
        sq = work[:, 2:4, :]

        a1 = ExitStack()
        tok = sb("tok", [P, 3, 2, D], on=a1)
        hank = tok[:, :, :, :].rearrange("p a b n -> p (a b n)").rearrange("p (h n) -> p h n", h=16)
        branch = tok[:, :, :, :].rearrange("p a b n -> p (a b n)").rearrange("p (j t) -> p j t", t=S)
        qk_mb = sb("qk_mb", [P, 8, S], on=a1)
        v_mb = sb("v_mb", [P, 2, 512], on=a1)
        q_sw = sb("q_sw", [P, 4, S], on=a1)
        k_sw = sb("k_sw", [P, 2, S], on=a1)
        v_sw = sb("v_sw", [P, 2, P], on=a1)
        q_me = sb("q_me", [P, 4, S], on=a1)
        y = sb("y", [P, KD, S], on=a1)
        k_me = y[:, 0:4, :]
        v_me = y[:, 4:8, :].rearrange("p (t a) s -> p t (a s)", t=2)
        boot = ExitStack()
        rows = sb("rows", [P, len(ROW_TILES), P], on=boot)
        hot = sb("hot", [33, 2, 512], on=boot)
        tables = sb("tables", [8, 2, 512], on=boot)
        rel = sb("rel", [33, 16], on=boot)
        sink_row = sb("sink_row", [1, 8], on=boot)
        lam_in = sb("lam_in", [1, LAYERS, 4, 64], on=boot)
        lam_p = sb("lam_p", [1, LAYERS, 2, 64], on=boot)
        lam_s = sb("lam_s", [1, LAYERS, 2], on=boot)
        lam_e = sb("lam_e", [P, LAYERS, 2], on=boot)
        boot.close()
        o1_hi = sb("o1_hi", [P, 12, S], f32r, on=a1)
        o1_lo = sb("o1_lo", [P, 12, S], f32r, on=a1)
        p_t = xn[:, :, :].rearrange("p s (k q) -> p s k q", k=2)
        a1.close()
        h1 = ExitStack()
        hid1_hi = sb("hid1_hi", [P, KF, S], f32r, on=h1)
        hid1_lo = sb("hid1_lo", [P, KF, S], f32r, on=h1)
        h1.close()
        a2 = ExitStack()
        q2 = sb("q2", [P, KD, T], on=a2)
        a2k = ExitStack()
        k2 = sb("k2", [P, KD, T], on=a2k)
        v2 = sb("v2", [P, 4, D], on=a2k)
        a2k.close()
        o2_hi = sb("o2_hi", [P, KD, T], f32r, on=a2)
        o2_lo = sb("o2_lo", [P, KD, T], f32r, on=a2)
        fa = sb("fa", [P, 4096], on=a2)
        f2 = fa[:, 0:2048].rearrange("p (t n) -> p t n", t=4)
        a_t = fa[:, 2048:4096].rearrange("p (s k q) -> p s k q", s=2, k=4)
        fr = fa[:, :].rearrange("p (j t) -> p j t", t=T)
        yf_hi = sb("yf_hi", [P, 4, T], f32r, on=a2)
        yf_lo = sb("yf_lo", [P, 4, T], f32r, on=a2)
        head_sq = k2
        head_diag = v2[:, :, :].rearrange("p t n -> p (t n)").rearrange("p (h t) -> p h t", t=T)
        dft = work[:, 2:4, :]
        tabs = sb("tabs", [P, N_TABS], on=a2)
        a2.close()
        h2 = ExitStack()
        hid2_hi = sb("hid2_hi", [P, KF, T], f32r, on=h2)
        hid2_lo = sb("hid2_lo", [P, KF, T], f32r, on=h2)
        h2.close()
        h3 = ExitStack()
        fin = sb("fin", [P, KD, S], on=h3)
        rows_out = sb("rows_out", [P, 2, D], on=h3)
        h3.close()

        bank = [ctx.enter_context(nc.psum_tensor(f"bank{b}", [P, 512], f32)) for b in range(8)]

        ident = const[:, C_ID:C_ID + P]
        reverse = const[:, C_REV:C_REV + P]

        def table(first, n):
            return tabs[:, first - N_CONST:first - N_CONST + n]

        rot, cos, sin = table(C_ROT, P), table(C_COS, S), table(C_SIN, S)

        raw_ready = [sem(f"raw_ready{n}") for n in range(2)]
        hi_ready = sem("hi_ready")
        lo_ready = sem("lo_ready")
        mod_ready = [sem(f"mod_ready{n}") for n in range(2)]
        mod_step = sem("mod_step")
        mod_done = sem("mod_done")
        group_done = sem("group_done")
        taken = [sem(f"taken{b}") for b in range(8)]
        tok_ready = [sem(f"tok_ready{n}") for n in range(3)]
        const_ready = sem("const_ready")
        tabs_ready = sem("tabs_ready")
        rows_ready = sem("rows_ready")
        rel_ready = sem("rel_ready")
        set_ready = sem("set_ready")
        boot_done = sem("boot_done")
        scratch_ready = sem("scratch_ready")
        hank_ready = sem("hank_ready")
        cond_ready = sem("cond_ready")
        lam_ready = sem("lam_ready")
        sq_ready = sem("sq_ready")
        acc_step = sem("acc_step")
        sums_done = sem("sums_done")
        diag_ready = sem("diag_ready")
        bcast_done = sem("bcast_done")
        xn_ready = sem("xn_ready")
        xm_ready = sem("xm_ready")
        u_part = sem("u_part")
        u_ready = sem("u_ready")
        updated = sem("updated")
        cv_first = sem("cv_first")
        cv_mid = sem("cv_mid")
        gelu_ready = sem("gelu_ready")
        hid_prod = sem("hid_prod")
        hid_part = sem("hid_part")
        hid_ready = sem("hid_ready")
        gated = sem("gated")
        dve_step = sem("dve_step")
        merge_step = sem("merge_step")
        merged_ready = sem("merged_ready")
        score_ready = sem("score_ready")
        nmax_ready = sem("nmax_ready")
        prob_ready = sem("prob_ready")
        pt_done = sem("pt_done")
        o_done = sem("o_done")
        o_ready = sem("o_ready")
        rot_done = sem("rot_done")
        rope_ready = sem("rope_ready")
        dft_done = sem("dft_done")
        yf_ready = sem("yf_ready")
        mod_taken = sem("mod_taken")
        out_done = sem("out_done")

        block = ctx.enter_context(nc.Block())

        UNITS1 = [("moba", h) for h in range(8)] + [("swa", h) for h in range(8)] + [("mem", h) for h in range(4)]

        def halves_of(l, step):
            if l == LAYERS - 1 and step in ("q", "f", "merge", "ffn1"):
                return [LAT]
            return [CTX, LAT]

        def span(halves):
            return slice(halves[0] * S, (halves[-1] + 1) * S)

        def gate_base(l, nth):
            return 24 + 16 * l + 8 * nth

        def mod_pair(st, i):
            return i + st.pair0

        def dft_base(l):
            return 16 * l

        def rope_base(l):
            return 16 * l

        def rope_tiles(l):
            return [(t, j) for t in range(2) for j in range(KD)]

        def att_units(l):
            return [(h, half, qb) for h in range(8) for half in reversed(halves_of(l, "q")) for qb in range(2)]

        def v_slots(l):
            n_four = 4 * len(halves_of(l, "q"))
            slots = []
            for m in range(16):
                ropes = [m] if m < 14 else [14, 15] if m == 14 else []
                slots.append((ropes, m // 2 if m // 2 < n_four else None, m % 2))
            return slots

        def four_unit(l, n):
            hs = halves_of(l, "q")
            return n // len(hs), hs[n % len(hs)]

        def yf_base(l):
            return 8 * l

        @block.sync
        def _(sp):
            def load(st, i, c):
                n = st.first + c
                j = i * (st.per // 2) + c // 2 if st.per != 2 else i
                if st.per == 2 and st.name[:2] != "up":
                    src = st.src(i * 2 + c)
                elif st.per == 1:
                    src = st.src(0)
                else:
                    src = st.src(j, c % 2)
                slot = raw[n % 2][:, 0:st.kt * st.cols].rearrange("p (k n) -> p k n", k=st.kt)
                sp.dma_start(slot, src).then_inc(raw_ready[n % 2], 16)

            def mod_loads(st, i):
                pair = mod_pair(st, i)
                l, in_layer = st.pair0 // MOD_PAIRS, st.pair0 % MOD_PAIRS
                for c in range(2):
                    if not (isinstance(pair, int) and pair == 0):
                        sp.wait_ge(mod_step, (pair - 1) * (4 * KD) + 2 * KD * (c + 1))
                    sp.dma_start(mod_raw[c][:, :, :],
                                 a["w_mod_2"][l][:, bass.ds((i + in_layer) * 2 * P + c * P, P)]
                                 .rearrange("(k p) n -> p k n", p=P)).then_inc(mod_ready[c], 16)

            def body(st, i):
                for c in range(st.per):
                    s = i * st.per + (st.first + c - 1)
                    if not (isinstance(s, int) and s < 1):
                        sp.wait_ge(lo_ready, s)
                    load(st, i, c)
                if st.mod:
                    mod_loads(st, i)

            for st in stream:
                body(st, 0)
                if st.bodies > 1:
                    with sp.Fori(1, st.bodies) as i:
                        body(st, i)
            for tt in range(2):
                sp.wait_ge(taken[5 + tt], plan.at("store", f"b{5 + tt}") + 2)
            sp.dma_start(out.rearrange("b (t p) n -> p (b t) n", p=P), rows_out[:, :, :]).then_inc(out_done, 16)
            sp.wait_ge(out_done, 16)

        @block.gpsimd
        def _(pool):
            def body(st, i):
                for c in range(st.per):
                    n = st.first + c
                    size = st.kt * st.cols
                    pool.wait_ge(hi_ready, i * st.per + (n + 1))
                    pool.tensor_tensor(w_lo[n % 2][:, 0:size], raw[n % 2][:, 0:size],
                                       w_hi[n % 2][:, 0:size].bitcast(f32), ALU.subtract).then_inc(lo_ready, 1)

            for st in stream:
                if st.bodies == 1:
                    body(st, 0)
                else:
                    with pool.Fori(0, st.bodies) as i:
                        body(st, i)

        @block.scalar
        def _(act):
            mem_v, x_v, ctx_v = (a[n][0].rearrange("(t p) n -> p t n", p=P) for n in ("mem", "x", "ctx_2"))
            act.dma_start(const[:, :], a["shape_const"][:, 0:N_CONST]).then_inc(const_ready, 16)
            for n, v in enumerate((mem_v, x_v, ctx_v)):
                act.dma_start(tok[:, n, :, :], v).then_inc(tok_ready[n], 16)
            row_src = {
                "g_mix_pre": a["norm_mix_pre"], "g_mix_post": a["norm_mix_post"], "g_ffn_pre": a["norm_ffn_pre"],
                "g_ffn_post": a["norm_ffn_post"], "g_mem": a["norm_mem"], "norm_g": a["norm_g_2"],
                "b_gate": a["b_gate_2"], "g_final": a["final_g_2"], "conv_w0": a["ffn_conv_w"][0, 0],
                "conv_w1": a["ffn_conv_w"][0, 1], "conv_w2": a["ffn_conv_w"][0, 2], "conv_b": a["ffn_conv_b"],
                "c_ctx": a["c_ctx_2"], "c_lat": a["c_2"], "subln": a["subln_g_2"],
                "b_mod0": a["b_mod_2"][0], "b_mod1": a["b_mod_2"][1],
            }
            flat = {1: "(r p) -> r p", 2: "a (r p) -> (a r) p", 3: "a b (r p) -> (a b r) p"}
            for name, (t, r, n) in ROWS.items():
                v = row_src[name]
                act.dma_start(rows[r:r + n, t, :], v.rearrange(flat[len(v.shape)], p=P)).then_inc(rows_ready, 16)
            act.dma_start(hot[:, :, :], a["shape_hot"].rearrange("b (v n) -> b v n", v=2)).then_inc(rel_ready, 16)
            act.wait_ge(set_ready, 1)
            act.dma_start(rel[0:32, :], a["rel_bias"]).then_inc(rel_ready, 16)
            act.dma_start(sink_row[:, :], a["swa_sinks"]).then_inc(rel_ready, 16)
            act.dma_start(lam_in[:, :, :, :].rearrange("o l j d -> o (l j d)"),
                          a["lam_params_2"].rearrange("(o l) j d -> o (l j d)", o=1)).then_inc(rel_ready, 16)

            def split(s):
                for st in stream:
                    if st.first <= s < st.first + st.blocks:
                        break
                else:
                    return
                act.wait_ge(raw_ready[s % 2], 16 * (s // 2 + 1))
                if s >= 2:
                    old = [q for q in stream if q.first <= s - 2 < q.first + q.blocks][0]
                    act.wait_ge(group_done, old.g0 + old.gpb * (s - 2 - old.first + 1))
                size = st.kt * st.cols
                act.activation(w_hi[s % 2][:, 0:size], raw[s % 2][:, 0:size], ACT.Copy).then_inc(hi_ready, 1)

            def split_two_ahead(st, i, c, final):
                if final and c + 2 >= st.per:
                    return split(st.first + st.per * (st.bodies - 1) + c + 2)
                n = st.first + c + 2
                act.wait_ge(raw_ready[n % 2], i * (8 * st.per) + 16 * (n // 2 + 1))
                act.wait_ge(group_done, st.done(i, st.gpb * (c + 1)))
                size = st.kt * st.cols
                act.activation(w_hi[n % 2][:, 0:size], raw[n % 2][:, 0:size], ACT.Copy).then_inc(hi_ready, 1)

            def take_mod(st, i):
                act.wait_ge(mod_done, mod_pair(st, i) + 2)
                at = bass.ds(i * 4 + 4 * (st.pair0 % MOD_PAIRS), 4)
                act.activation(mod_sum[:, at], bank[7][:, 0:4], ACT.Copy).then_inc(taken[7], 1)

            def gemm(name, evac=None, unrolled=False):
                st = gemms[name]

                def body(i, final):
                    for c in range(st.per):
                        if evac is not None:
                            evac(st, i, c)
                        split_two_ahead(st, i, c, final)
                    if st.mod:
                        take_mod(st, i)

                if unrolled:
                    for i in range(st.bodies - 1):
                        body(i, False)
                elif st.bodies > 1:
                    with act.Fori(0, st.bodies - 1) as i:
                        body(i, False)
                body(st.bodies - 1, True)

            def copy_tiles(dst, cols):
                def evac(st, i, c):
                    for t in range(2):
                        act.wait_ge(group_done, st.done(i, 2 * c + t + 1))
                        b = 2 * c + t
                        act.activation(dst[:, bass.ds(i * 4 + b, 1), cols], bank[b][:, 0:cols.stop - cols.start]
                                       .rearrange("p (o t) -> p o t", o=1), ACT.Copy).then_inc(taken[b], 1)
                return evac

            def copy_rows(dst, first, tiles):
                per_block = tiles // 2

                def evac(st, i, c):
                    for t in range(per_block):
                        act.wait_ge(group_done, st.done(i, per_block * c + t + 1))
                        b = 2 * c + t
                        act.activation(dst[:, first + 2 * t:first + 2 * t + 2, bass.ds(i * 2 * BLK + c * BLK, BLK)],
                                       bank[b][:, :].rearrange("p (t n) -> p t n", t=2), ACT.Copy) \
                           .then_inc(taken[b], 1)
                return evac

            def squares(name, src, ready):
                q0, s0, w = plan.at(name, "sq"), plan.at(name, "sums"), src(0).shape[-1]
                for k in range(KD):
                    for s, v in ready(k):
                        act.wait_ge(s, v)
                    if s0 + k >= 2:
                        act.wait_ge(sums_done, s0 + k - 1)
                    act.activation(sq[:, k % 2, 0:w], src(k), ACT.Square).then_inc(sq_ready, 1)

            def mean_root(name, w, n_sums):
                act.wait_ge(sums_done, plan.at(name, "sums") + n_sums)
                if plan.at(name, "diag"):
                    act.wait_ge(diag_ready, plan.at(name, "diag"))
                act.activation(rms[:, 0, 0:w // P], bank[4][:, 0:w // P], ACT.Sqrt, bias=eps[:, 0:1], scale=1.0 / D) \
                   .then_inc(taken[4], 1)

            def hi_tiles(name, w, t0):
                for k in range(KD):
                    act.wait_ge(xn_ready, plan.at(name, "xn") + k + 1)
                    act.activation(u_hi[:, k, t0:t0 + w], xn[:, k % 2, 0:w], ACT.Copy).then_inc(u_part, 1)

            def modulated(name, l, i, halves):
                x0, u0, m0 = plan.at(name, "xn"), plan.at(name, "u"), plan.at(name, "xm")
                w, t = S * len(halves), span(halves)
                for k in range(KD):
                    act.wait_ge(xn_ready, x0 + k + 1)
                    act.wait_ge(u_ready, u0 + k - 1)
                    for h in halves:
                        lo = (h - halves[0]) * S
                        ins = act.activation(work[:, k % 2, lo:lo + S], xn[:, k % 2, lo:lo + S], ACT.Identity,
                                             bias=mod[:, 3 * i * KD + k, h:h + 1], scale=mod_a[:, i, k, h:h + 1])
                    ins.then_inc(xm_ready, 1)
                    act.wait_ge(xm_ready, m0 + k + 1)
                    act.activation(u_hi[:, k, t], work[:, k % 2, 0:w], ACT.Copy).then_inc(u_part, 1)

            def silu_tiles(w):
                def evac(st, i, c):
                    if c == 0:
                        for t in range(2):
                            act.wait_ge(group_done, st.done(i, t + 1))
                            act.wait_ge(taken[2 + t], st.taken(i, 2 + t) - 1)
                            act.activation(work[:, t, 0:w], bank[t][:, 0:w], ACT.Silu).then_inc(taken[t], 1)
                return evac

            split(0)
            split(1)
            act.wait_ge(taken[6], 1)
            act.activation(cond[:, :, :], col[:, COL["c_ctx"]:COL["c_ctx"] + 2 * KD]
                           .rearrange("p (c k) -> p k c", c=2), ACT.Silu).then_inc(cond_ready, 1)
            act.wait_ge(boot_done, 14)
            act.activation(lam_e[:, :, :], bank[5][:, 16:20].rearrange("p (l j) -> p l j", l=2), ACT.Exp) \
               .then_inc(taken[5], 1)
            act.wait_ge(taken[5], 8)
            act.wait_ge(taken[6], 3)
            act.dma_start(scratch.rearrange("v h n -> h v n"), tables[:, :, :]).then_inc(scratch_ready, 16)
            act.wait_ge(scratch_ready, 16)
            act.wait_ge(taken[4], 6)
            shifted = bass.AP(tensor=scratch.tensor, offset=0, ap=[[1, P], [512, 16], [1, HANK]])
            act.dma_start(hank, shifted).then_inc(hank_ready, 16)

            squares("n_mem", lambda k: y[:, k, :], lambda k: [(taken[4], 2), (taken[5], 2)])
            mean_root("n_mem", S, KD)
            squares("n_mix", lambda k: x[:, k, S:T], lambda k: [(taken[4], 4), (taken[5], 4)])
            mean_root("n_mix", S, KD)
            hi_tiles("n_mem", S, 0)
            gemm("k_me", copy_tiles(k_me, slice(0, S)))
            gemm("v_me", copy_rows(v_me, 0, 2))
            hi_tiles("n_mix", S, S)
            gemm("qk_mb", copy_tiles(qk_mb, slice(0, S)))
            gemm("v_mb", copy_rows(v_mb, 0, 2))
            gemm("q_sw", copy_tiles(q_sw, slice(0, S)))

            def kv_sw(st, i, c):
                act.wait_ge(group_done, st.done(0, 1))
                for kv in range(2):
                    for to in range(2):
                        ins = act.activation(k_sw[64 * to:64 * to + 64, kv, :], bank[0][64 * kv:64 * kv + 64, 0:S], ACT.Copy)
                ins.then_inc(taken[0], 1)
                act.wait_ge(group_done, st.done(0, 2))
                act.activation(v_sw[:, :, :], bank[1][:, 0:2 * P].rearrange("p (t n) -> p t n", t=2), ACT.Copy) \
                   .then_inc(taken[1], 1)

            gemm("kv_sw", kv_sw)
            gemm("q_me", copy_tiles(q_me, slice(0, S)))

            def exp1(n):
                kind, h = UNITS1[n]
                scale = 0.125 if kind != "mem" else 1.0 / math.sqrt(128)
                act.wait_ge(nmax_ready, n + 1)
                if n >= 2:
                    act.wait_ge(prob_ready, n - 1)
                st_ = stat[:, n % 2, :]
                if kind == "swa":
                    act.activation(st_[:, 6:8], st_[:, 2:4], ACT.Exp, bias=sinks[:, h:h + 1])
                for q in range(2):
                    ins = act.activation(work[:, n % 2, q * S:(q + 1) * S], bank[n % 2][:, q * S:(q + 1) * S], ACT.Exp,
                                         bias=st_[:, 2 + q:3 + q], scale=scale, accum_out=st_[:, 4 + q:5 + q])
                ins.then_inc(taken[n % 2], 1)

            def copy_pt1(n):
                act.wait_ge(pt_done, n + 1)
                if n >= 2:
                    act.wait_ge(o_done, n - 1)
                act.activation(p_t[:, n % 2, :, :], bank[2 + n % 2][:, :].rearrange("p (k q) -> p k q", k=2), ACT.Copy) \
                   .then_inc(taken[2 + n % 2], 1)

            for n in range(len(UNITS1) + T_LAG):
                if n >= T_LAG:
                    copy_pt1(n - T_LAG)
                if n < len(UNITS1):
                    exp1(n)
            for n in range(3):
                gemm(f"branch{n}", copy_tiles(branch[:, 8 * n:8 * n + 8, :], slice(0, S)))

            def gates(w, base, bias=None):
                def evac(st, i, c):
                    for t in range(2):
                        b = 2 * c + t
                        act.wait_ge(group_done, st.done(i, b + 1))
                        act.wait_ge(gated, i * 4 + (base + 1))
                        kw = {} if bias is None else {"bias": col[:, bass.ds(i * 4 + (b + bias), 1)]}
                        act.activation(work[:, b, 0:w], bank[b][:, 0:w], ACT.Sigmoid, **kw).then_inc(taken[b], 1)
                return evac

            for n in range(3):
                gemm(f"gates1_{n}", gates(S, 8 * n))
            gemm("w_out")
            mean_root("n_mix_post", S, 1)
            squares("n_ffn", lambda k: x[:, k, S:T], lambda k: [(updated, k + 1)])
            mean_root("n_ffn", S, KD)
            hi_tiles("n_ffn", S, S)

            def conv_tiles(st, i, c):
                for t in range(2):
                    act.wait_ge(group_done, st.done(i, 2 * c + t + 1))
                    if c == 0:
                        act.wait_ge(hid_ready, i * 2 + 1)
                    at = i * 2 + (c * KF + t)
                    b = 2 * c + t
                    act.activation(work[:, b, 0:S], bank[b][:, 0:S], ACT.Identity,
                                   bias=col[:, bass.ds(at + COL["conv_b"], 1)],
                                   scale=col[:, bass.ds(at + COL["conv_w2"], 1)]).then_inc(cv_first, 1)
                if c == 0:
                    for t in range(2):
                        act.wait_ge(taken[t], st.taken(i, t))
                        act.activation(work[:, t, 0:S], work[:, t, 0:S], ACT.Gelu_apprx_tanh).then_inc(gelu_ready, 1)

            gemm("up1", conv_tiles)
            gemm("down1")
            mean_root("n_ffn_post", S, 1)

            def layer(l):
                both, q_h, m_h = [CTX, LAT], halves_of(l, "q"), halves_of(l, "merge")
                wq, wm = S * len(q_h), S * len(m_h)
                if l == 0:
                    squares("n0_0", lambda k: x[:, k, :], lambda k: [(updated, KD + k + 1)])
                mean_root(f"n0_{l}", T, KD if l == 0 else 1)
                modulated(f"n0_{l}", l, 0, both)
                gemm(f"up_{l}0", silu_tiles(T))
                gemm(f"down_{l}0")
                mean_root(f"n1_{l}", T, 1)
                act.dma_start(tabs[:, :], a["shape_const"][:, N_CONST:]).then_inc(tabs_ready, 16)
                modulated(f"n1_{l}", l, 1, both)
                gemm(f"q_{l}", copy_tiles(q2, span(q_h)))
                gemm(f"k_{l}", copy_tiles(k2, slice(0, T)))
                gemm(f"f_{l}", copy_rows(f2, 2 * q_h[0], 2 * len(q_h)))
                slots = v_slots(l)

                def values(st, i, c):
                    for t in range(4):
                        _, n, step = slots[(2 * i + c) * 4 + t]
                        if n is not None and step == 0:
                            act.wait_ge(dft_done, dft_base(l) + 2 * n + 1)
                            act.activation(dft[:, n % 2, :], bank[5][:, :], ACT.Copy).then_inc(taken[5], 1)
                        if t % 2 == 1:
                            b = 2 * c + t // 2
                            act.wait_ge(group_done, st.done(i, b + 1))
                            at = (2 * i + c) * BLK
                            act.activation(v2[:, t - 1:t + 1, at:at + BLK],
                                           bank[b][:, :].rearrange("p (t n) -> p t n", t=2), ACT.Copy) \
                               .then_inc(taken[b], 1)

                gemm(f"v_{l}", values, unrolled=True)
                units = att_units(l)
                u0, p0 = plan.at(f"att_{l}", "unit"), plan.at(f"att_{l}", "pair")

                def exps(n):
                    h, half, qb = units[n]
                    nk = T if half == LAT else S
                    act.wait_ge(nmax_ready, len(UNITS1) + u0 + n + 1)
                    act.wait_ge(prob_ready, len(UNITS1) + u0 + n - 1)
                    st_ = stat[:, n % 2, :]
                    for c in range(2):
                        b = 2 * (n % 2) + c
                        act.activation(work[:, b, 0:nk], bank[b][:, 0:nk], ACT.Exp, bias=st_[:, 2 + c:3 + c],
                                       scale=0.125, accum_out=st_[:, 4 + c:5 + c]).then_inc(taken[b], 1)

                def copy_pt(n):
                    h, half, qb = units[n]
                    kt = 4 if half == LAT else 2
                    act.wait_ge(pt_done, len(UNITS1) + u0 + n + 1)
                    if n >= 4:
                        act.wait_ge(o_done, len(UNITS1) + p0 + n // 2 - 1)
                    act.activation(a_t[:, (n // 2) % 2, 0:kt, qb * P:(qb + 1) * P],
                                   bank[4 + n % 2][:, 0:kt * P].rearrange("p (k q) -> p k q", k=kt), ACT.Copy) \
                       .then_inc(taken[4 + n % 2], 1)

                for n in range(len(units) + T_LAG):
                    if n >= T_LAG:
                        copy_pt(n - T_LAG)
                    if n < len(units):
                        exps(n)
                act.wait_ge(taken[6], plan.at(f"subln_{l}", "b6"))
                for h in range(KD):
                    act.activation(head_sq[:, h, 0:wq], q2[:, h, span(q_h)], ACT.Square).then_inc(sq_ready, 1)
                gemm(f"four_out_{l}", copy_tiles(fr, span(m_h)))
                act.wait_ge(sums_done, plan.at(f"subln_{l}", "sums") + 1)
                act.wait_ge(diag_ready, plan.at(f"subln_{l}", "diag"))
                nt = KD * wq // P
                act.activation(rms[:, 0, 0:nt], bank[4][:, 0:nt], ACT.Sqrt, bias=eps[:, 0:1], scale=1.0 / P) \
                   .then_inc(taken[4], 1)
                b_gate = COL["b_gate"] + 2 * l * KD
                gemm(f"gates_{l}1", gates(wm, gate_base(l, 0), b_gate + KD))
                gemm(f"attn_out_{l}", copy_tiles(q2, span(m_h)))
                gemm(f"gates_{l}0", gates(wm, gate_base(l, 1), b_gate))
                gemm(f"w_o_{l}")
                mean_root(f"n2_{l}", wm, 1)
                modulated(f"n2_{l}", l, 2, m_h)
                gemm(f"up_{l}1", silu_tiles(wm))
                gemm(f"down_{l}1")

            for l in range(LAYERS):
                layer(l)
            mean_root("n_final", S, 1)

        @block.vector
        def _(dve):
            steps = [0]

            def link(ins):
                steps[0] += 1
                ins.then_inc(dve_step, 1)
                dve.wait_ge(dve_step, steps[0])

            dve.memset(rel[32:33, :], MASKED).then_inc(set_ready, 1)
            dve.memset(ones[:, :], 1.0).then_inc(set_ready, 1)
            dve.memset(eps[:, :], EPS).then_inc(set_ready, 1)
            dve.sem_inc(hid_ready, 1)
            dve.sem_inc(gated, 1)
            dve.sem_inc(taken[7], 1)
            dve.sem_inc(mod_done, 1)
            dve.wait_ge(boot_done, 1)
            dve.tensor_copy(col[:, :], bank[6][:, 0:N_COLS]).then_inc(taken[6], 1)
            dve.wait_ge(rel_ready, 64)
            for l in range(LAYERS):
                dve.tensor_tensor(lam_p[:, l, :, :], lam_in[:, l, 0:4:2, :], lam_in[:, l, 1:4:2, :], ALU.mult).then_inc(set_ready, 1)
            dve.wait_ge(set_ready, 5)
            dve.tensor_reduce(lam_s[:, :, :], lam_p[:, :, :, :], AX.X, ALU.add).then_inc(set_ready, 1)
            for n in range(12):
                s, q = n // 4, n % 4
                dst = y[:, 2 * q:2 * q + 2, :] if s == 0 else x[:, 2 * q:2 * q + 2, S:T] if s == 1 else x[:, 2 * q:2 * q + 2, 0:S]
                dve.wait_ge(boot_done, n + 2)
                dve.tensor_copy(dst, bank[4 + n % 2][:, :].rearrange("p (f t) -> p f t", f=2)).then_inc(taken[4 + n % 2], 1)
            dve.wait_ge(taken[5], 7)
            for l in range(LAYERS):
                init = 0.8 - 0.6 * math.exp(-0.3 * l)
                link(dve.tensor_scalar(lam[:, l:l + 1], lam_e[:, l, 0:1], lam_e[:, l, 1:2], init, ALU.subtract, ALU.add))
                link(dve.tensor_scalar(sub_g[:, l:l + 1], col[:, COL["subln"] + l:COL["subln"] + l + 1],
                                       1.0 - init, None, ALU.mult))
            dve.wait_ge(boot_done, 15)
            dve.tensor_copy(sinks[:, :], bank[6][:, 0:8]).then_inc(taken[6], 1)
            for v in range(2):
                dve.wait_ge(boot_done, 16 + v)
                dve.tensor_scalar(tables[:, v, :], bank[5 + v][0:8, :], 8.0, None, ALU.mult).then_inc(taken[5 + v], 1)

            def rstd_of(name, w):
                nt = w // P
                dve.wait_ge(taken[4], plan.at(name, "b4") + 1)
                link(dve.reciprocal(rms[:, 1, 0:nt], rms[:, 0, 0:nt]))
                dve.tensor_tensor(diag[:, 0:nt, :], ident.unsqueeze(1).broadcast_to([P, nt, P]),
                                  rms[:, 1, 0:nt].unsqueeze(2).broadcast_to([P, nt, P]), ALU.mult).then_inc(diag_ready, 1)
                dve.wait_ge(bcast_done, plan.at(name, "bc") + 1)

            def lo_part(k, src, u0, w, t0):
                dve.wait_ge(u_part, u0 + k + 1)
                dve.tensor_tensor(u_lo[:, k, t0:t0 + w], src, u_hi[:, k, t0:t0 + w].bitcast(f32), ALU.subtract) \
                   .then_inc(u_ready, 1)

            def norm_u(name, src, gain, t0):
                x0, u0 = plan.at(name, "xn"), plan.at(name, "u")
                rstd_of(name, S)
                for k in range(KD + 1):
                    if k < KD:
                        if u0 + k >= 2:
                            dve.wait_ge(u_ready, u0 + k - 1)
                        dve.scalar_tensor_tensor(xn[:, k % 2, 0:S], src(k), col[:, COL[gain] + k:COL[gain] + k + 1],
                                                 bank[5][:, 0:S], ALU.mult, ALU.mult).then_inc(xn_ready, 1)
                    if k >= 1:
                        lo_part(k - 1, xn[:, (k - 1) % 2, 0:S], u0, S, t0)

            def norm_x(name, gain, dst=None):
                x0, n0 = plan.at(name, "xn"), plan.at(name, "upd")
                rstd_of(name, S)
                for k in range(KD):
                    g = col[:, COL[gain] + k:COL[gain] + k + 1]
                    if dst is not None:
                        dve.scalar_tensor_tensor(dst[:, k, :], x[:, k, S:T], g, bank[5][:, 0:S], ALU.mult, ALU.mult) \
                           .then_inc(updated, 1)
                        continue
                    if k >= 2:
                        dve.wait_ge(updated, n0 + k - 1)
                    dve.scalar_tensor_tensor(xn[:, k % 2, 0:S], y[:, k, :], g, bank[5][:, 0:S], ALU.mult, ALU.mult) \
                       .then_inc(xn_ready, 1)
                    dve.wait_ge(xn_ready, x0 + k + 1)
                    dve.tensor_tensor(x[:, k, S:T], x[:, k, S:T], xn[:, k % 2, 0:S], ALU.add).then_inc(updated, 1)

            def norm_mod(name, halves):
                u0, m0 = plan.at(name, "u"), plan.at(name, "xm")
                w, t = S * len(halves), span(halves)
                rstd_of(name, w)
                for k in range(KD + 1):
                    if k < KD:
                        if k >= 2:
                            dve.wait_ge(xm_ready, m0 + k - 1)
                        dve.tensor_tensor(xn[:, k % 2, 0:w], x[:, k, t], bank[5][:, 0:w], ALU.mult).then_inc(xn_ready, 1)
                    if k >= 1:
                        lo_part(k - 1, work[:, (k - 1) % 2, 0:w], u0, w, t.start)

            def sum_squares(st, i, t, src, w):
                n = i * (2 * st.acc) + (st.acc0 + 2 * t)
                dve.tensor_tensor(xn[:, t % 2:t % 2 + 1, 0:w], src, src, ALU.mult).then_inc(acc_step, 1)
                dve.wait_ge(acc_step, n + 1)
                acc = root[:, t % 2, 0:w]
                dve.tensor_tensor(acc, acc, xn[:, t % 2, 0:w], ALU.add).then_inc(acc_step, 1)
                dve.wait_ge(acc_step, n + 2)

            def clear_sums():
                link(dve.memset(root[:, :, :], 0.0))

            def mod_products(st, i):
                pair = mod_pair(st, i)
                dve.wait_ge(mod_done, pair + 1)
                for c in range(2):
                    dve.wait_ge(mod_ready[c], pair * 16 + 16)
                    for k in range(KD):
                        for h in range(2):
                            acc, by = mod_acc[:, c, h, :], cond[:, k, h:h + 1]
                            if k == 0:
                                ins = dve.tensor_scalar(acc, mod_raw[c][:, k, :], by, None, ALU.mult)
                            else:
                                dve.wait_ge(mod_step, pair * (4 * KD) + (2 * KD * c + 2 * k + h - 1))
                                ins = dve.scalar_tensor_tensor(acc, mod_raw[c][:, k, :], by, acc, ALU.mult, ALU.add)
                            ins.then_inc(mod_step, 1)

            def gemm(name, evac=None, unrolled=False):
                st = gemms[name]
                if evac is None and not st.mod:
                    return

                def body(i):
                    if st.mod:
                        mod_products(st, i)
                    if evac is not None:
                        evac(st, i)

                if unrolled or st.bodies == 1:
                    for i in range(st.bodies):
                        body(i)
                else:
                    with dve.Fori(0, st.bodies) as i:
                        body(i)

            def multiply_gate(st, i, b, at, w):
                dve.wait_ge(taken[b], st.taken(i, b))
                dve.tensor_tensor(at, at, work[:, b:b + 1, 0:w], ALU.mult).then_inc(gated, 1)

            def multiply_gates(dst, w, cols):
                def evac(st, i):
                    for b in range(4):
                        multiply_gate(st, i, b, dst[:, bass.ds(i * 4 + b, 1), cols], w)
                return evac

            def merge_gates(dst, others, w, cols, hi, lo, base, n0, g0):
                per = len(others) + 1

                def evac(st, i):
                    for b in range(4):
                        at = bass.ds(i * 4 + b, 1)
                        m = dst[:, at, cols]
                        multiply_gate(st, i, b, m, w)
                        dve.wait_ge(gated, i * 4 + (g0 + b + 2))
                        for n, o in enumerate(others):
                            dve.tensor_tensor(m, m, o[:, at, cols], ALU.add).then_inc(merge_step, 1)
                            dve.wait_ge(merge_step, i * (4 * per) + (base + per * b + n + 1))
                        dve.tensor_copy(hi[:, at, cols], m).then_inc(merge_step, 1)
                        dve.wait_ge(merge_step, i * (4 * per) + (base + per * b + per))
                        dve.tensor_tensor(lo[:, at, cols], m, hi[:, at, cols].bitcast(f32), ALU.subtract) \
                           .then_inc(merged_ready, 1)
                return evac

            norm_u("n_mem", lambda k: y[:, k, :], "g_mem", 0)
            norm_u("n_mix", lambda k: x[:, k, S:T], "g_mix_pre", S)
            dve.wait_ge(cond_ready, 1)
            for name in ("qk_mb", "v_mb", "q_sw", "q_me"):
                gemm(name)

            def max1(n):
                kind, h = UNITS1[n]
                scale = 0.125 if kind != "mem" else 1.0 / math.sqrt(128)
                dve.wait_ge(score_ready, n + 1)
                st_ = stat[:, n % 2, :]
                link(dve.tensor_reduce(st_[:, 0:2], bank[n % 2][:, :].rearrange("p (q k) -> p q k", q=2), AX.X, ALU.max))
                if kind == "swa":
                    link(dve.tensor_scalar(st_[:, 0:2], st_[:, 0:2], scale, sinks[:, h:h + 1], ALU.mult, ALU.max))
                    dve.tensor_scalar(st_[:, 2:4], st_[:, 0:2], -1.0, None, ALU.mult).then_inc(nmax_ready, 1)
                else:
                    dve.tensor_scalar(st_[:, 2:4], st_[:, 0:2], -scale, None, ALU.mult).then_inc(nmax_ready, 1)

            def probs1(n):
                kind, h = UNITS1[n]
                dve.wait_ge(taken[n % 2], plan.at("att1", f"b{n % 2}") + n // 2 + 1)
                st_ = stat[:, n % 2, :]
                if kind == "swa":
                    link(dve.tensor_tensor(st_[:, 4:6], st_[:, 4:6], st_[:, 6:8], ALU.add))
                link(dve.reciprocal(st_[:, 8:10], st_[:, 4:6]))
                if n >= 2:
                    dve.wait_ge(pt_done, n - 1)
                for q in range(2):
                    cols = slice(q * S, (q + 1) * S)
                    ins = dve.tensor_scalar(probs[:, n % 2, cols], work[:, n % 2, cols], st_[:, 8 + q:9 + q], None, ALU.mult)
                ins.then_inc(prob_ready, 1)

            def out1(n):
                kind, h = UNITS1[n]
                b = 4 + n % 2
                dve.wait_ge(o_done, n + 1)
                if kind == "moba":
                    tile, to, of, w = h // 2, 64 * (h % 2), 64 * (h % 2), 64
                elif kind == "swa":
                    tile, to, of, w = 4 + h // 2, 64 * (h % 2), 64 * (h // 4), 64
                else:
                    tile, to, of, w = 8 + h, 0, 0, P
                if n >= 2:
                    dve.wait_ge(o_ready, n - 1)
                src = work[to:to + w, 2 + n % 2, 0:S]
                dve.tensor_copy(src, bank[b][of:of + w, 0:S]).then_inc(taken[b], 1)
                dve.wait_ge(taken[b], plan.at("att1", f"b{b}") + n // 2 + 1)
                link(dve.tensor_copy(o1_hi[to:to + w, tile, :], src))
                dve.tensor_tensor(o1_lo[to:to + w, tile, :], src, o1_hi[to:to + w, tile, :].bitcast(f32), ALU.subtract) \
                   .then_inc(o_ready, 1)

            n_units = len(UNITS1)
            dve.wait_ge(u_ready, 2 * KD)
            for n in range(n_units + O_LAG + 1):
                if n < n_units:
                    max1(n)
                if 1 <= n <= n_units:
                    probs1(n - 1)
                if n >= O_LAG + 1:
                    out1(n - O_LAG - 1)
            def first_branch(n):
                return branch[:, KD * n:KD * (n + 1), :]

            for n in range(2):
                gemm(f"gates1_{n}", multiply_gates(first_branch(n), S, slice(0, S)))
            gemm("gates1_2", merge_gates(first_branch(2), (first_branch(0), first_branch(1)), S, slice(0, S),
                                         o1_hi, o1_lo, 0, 0, 16))

            def copy_y(tiles, per):
                def evac(st, i):
                    for t in range(tiles):
                        dve.wait_ge(group_done, st.done(i, per * (t + 1)))
                        at = y[:, bass.ds(i * tiles + t, 1), :]
                        dve.tensor_copy(at, bank[t][:, 0:S].rearrange("p (o t) -> p o t", o=1)).then_inc(taken[t], 1)
                        dve.wait_ge(taken[t], st.taken(i, t))
                        sum_squares(st, i, t, at, S)
                return evac

            clear_sums()
            gemm("w_out", copy_y(4, 1))
            norm_x("n_mix_post", "g_mix_post")
            dve.wait_ge(updated, KD)
            norm_u("n_ffn", lambda k: x[:, k, S:T], "g_ffn_pre", S)

            def split_hidden(i, t, base, src, hi, lo):
                dve.tensor_copy(hi, src).then_inc(hid_part, 1)
                dve.wait_ge(hid_part, i * 2 + (base + t + 1))
                dve.tensor_tensor(lo, src, hi.bitcast(f32), ALU.subtract).then_inc(hid_ready, 1)

            def conv_ffn(st, i):
                for b in range(4):
                    c, t = b // 2, b % 2
                    at = i * 2 + (c * KF + t)
                    dve.wait_ge(cv_first, i * 4 + (b + 1))
                    dve.scalar_tensor_tensor(work[:, b, 1:S], bank[b][:, 0:S - 1], col[:, bass.ds(at + COL["conv_w1"], 1)],
                                             work[:, b, 1:S], ALU.mult, ALU.add).then_inc(cv_mid, 1)
                    dve.wait_ge(cv_mid, i * 4 + (b + 1))
                    dve.scalar_tensor_tensor(work[:, b, 2:S], bank[b][:, 0:S - 2], col[:, bass.ds(at + COL["conv_w0"], 1)],
                                             work[:, b, 2:S], ALU.mult, ALU.add).then_inc(taken[b], 1)
                dve.wait_ge(hid_ready, i * 2 + 1)
                for t in range(2):
                    dve.wait_ge(gelu_ready, i * 2 + (t + 1))
                    dve.wait_ge(taken[2 + t], st.taken(i, 2 + t))
                    prod = work[:, t, S:2 * S]
                    dve.tensor_tensor(prod, work[:, t, 0:S], work[:, 2 + t, 0:S], ALU.mult).then_inc(hid_prod, 1)
                    dve.wait_ge(hid_prod, i * 2 + (t + 1))
                    at = bass.ds(i * 2 + t, 1)
                    split_hidden(i, t, 0, work[:, t:t + 1, S:2 * S], hid1_hi[:, at, :], hid1_lo[:, at, :])

            gemm("up1", conv_ffn)

            clear_sums()
            gemm("down1", copy_y(2, 2))
            norm_x("n_ffn_post", "g_ffn_post")

            def modulation(l, i):
                pairs, n = MOD_PAIRS // 3, 3 * KD
                dve.wait_ge(taken[7], l * MOD_PAIRS + (i + 1) * pairs + 1)
                b0, g0 = COL[f"b_mod{l}"] + i * n, COL["norm_g"] + (3 * l + i) * KD
                m = mod[:, i * n:(i + 1) * n, :]
                for h in range(2):
                    ins = dve.tensor_tensor(m[:, :, h], mod_sum[:, 2 * i * n + h:2 * (i + 1) * n:2], col[:, b0:b0 + n], ALU.add)
                link(ins)
                for h in range(2):
                    dve.scalar_tensor_tensor(mod_a[:, i, :, h], m[:, KD:2 * KD, h], 1.0, col[:, g0:g0 + KD], ALU.add, ALU.mult)
                link(dve.tensor_scalar(mod_g[:, i, :, :], m[:, 2 * KD:3 * KD, :], 1.0 if i == 1 else 0.5, None, ALU.mult))

            def ffn(name, base, w):
                def body(st, i):
                    dve.wait_ge(hid_ready, i * 2 + (base + 1))
                    for t in range(2):
                        dve.wait_ge(group_done, st.done(i, 3 + t))
                        dve.wait_ge(taken[t], st.taken(i, t))
                        dve.tensor_tensor(work[:, 2 + t, 0:w], bank[2 + t][:, 0:w], work[:, t, 0:w], ALU.mult) \
                           .then_inc(taken[2 + t], 1)
                        dve.wait_ge(taken[2 + t], st.taken(i, 2 + t))
                        at = bass.ds(i * 2 + t, 1)
                        split_hidden(i, t, base, work[:, 2 + t:3 + t, 0:w], hid2_hi[:, at, 0:w], hid2_lo[:, at, 0:w])
                gemm(name, body)

            def residual(i_mod, halves, per, tiles):
                def body(st, i):
                    for t in range(tiles):
                        dve.wait_ge(group_done, st.done(i, per(t)))
                        for h in halves:
                            at = x[:, bass.ds(i * tiles + t, 1), h * S:(h + 1) * S]
                            lo = (h - halves[0]) * S
                            ins = dve.scalar_tensor_tensor(at, bank[t][:, lo:lo + S].rearrange("p (o t) -> p o t", o=1),
                                                           mod_g[:, i_mod, bass.ds(i * tiles + t, 1), h], at,
                                                           ALU.mult, ALU.add)
                        ins.then_inc(taken[t], 1)
                        dve.wait_ge(taken[t], st.taken(i, t))
                        sum_squares(st, i, t, x[:, bass.ds(i * tiles + t, 1), span(halves)], S * len(halves))
                return body

            def layer(l):
                both, q_h, m_h = [CTX, LAT], halves_of(l, "q"), halves_of(l, "merge")
                wq, wm = S * len(q_h), S * len(m_h)
                modulation(l, 0)
                norm_mod(f"n0_{l}", both)
                ffn(f"up_{l}0", KF * (1 + 2 * l), T)
                clear_sums()
                gemm(f"down_{l}0", residual(0, both, lambda t: 2 * t + 2, 2))
                modulation(l, 1)
                norm_mod(f"n1_{l}", both)
                gemm(f"q_{l}")
                gemm(f"k_{l}")
                r0, y0 = rope_base(l), yf_base(l)
                tiles = rope_tiles(l)

                def rotate(n):
                    t, j = tiles[n]
                    cur = (q2 if t == 0 else k2)[:, j, S:T]
                    tmp = xn[:, n % 2, 0:S]
                    dve.wait_ge(rot_done, r0 + n + 1)
                    dve.tensor_tensor(tmp, bank[4][:, 0:S], sin, ALU.mult).then_inc(taken[4], 1)
                    link(dve.tensor_tensor(cur, cur, cos, ALU.mult))
                    dve.wait_ge(taken[4], plan.at(f"rope_{l}", "b4") + n + 1)
                    dve.tensor_tensor(cur, cur, tmp, ALU.add).then_inc(rope_ready, 1)
                    dve.wait_ge(rope_ready, r0 + n + 1)

                def channels(n):
                    g, h = four_unit(l, n)
                    tmp = xn[:, n % 2, S:2 * S]
                    hi, lo = yf_hi[:, g, h * S:(h + 1) * S], yf_lo[:, g, h * S:(h + 1) * S]
                    dve.wait_ge(dft_done, dft_base(l) + 2 * n + 2)
                    dve.tensor_copy(tmp, bank[6][:, 0:S]).then_inc(taken[6], 1)
                    dve.wait_ge(taken[6], plan.at(f"four_{l}", "b6") + n + 1)
                    link(dve.tensor_copy(hi, tmp))
                    dve.tensor_tensor(lo, tmp, hi.bitcast(f32), ALU.subtract).then_inc(yf_ready, 1)
                    dve.wait_ge(yf_ready, y0 + n + 1)

                for ropes, n, step in v_slots(l):
                    for r in ropes:
                        rotate(r)
                    if n is not None and step == 1:
                        channels(n)
                units = att_units(l)
                u0, p0 = plan.at(f"att_{l}", "unit"), plan.at(f"att_{l}", "pair")

                def maxima(n):
                    h, half, qb = units[n]
                    nk = T if half == LAT else S
                    st_ = stat[:, n % 2, :]
                    dve.wait_ge(score_ready, n_units + u0 + n + 1)
                    for c in range(2):
                        link(dve.tensor_reduce(st_[:, c:c + 1], bank[2 * (n % 2) + c][:, 0:nk], AX.X, ALU.max))
                    dve.tensor_scalar(st_[:, 2:4], st_[:, 0:2], -0.125, None, ALU.mult).then_inc(nmax_ready, 1)

                def differences(n):
                    h, half, qb = units[n]
                    nk = T if half == LAT else S
                    st_ = stat[:, n % 2, :]
                    for c in range(2):
                        b = 2 * (n % 2) + c
                        dve.wait_ge(taken[b], plan.at(f"att_{l}", f"b{b}") + n // 2 + 1)
                    link(dve.reciprocal(st_[:, 8:10], st_[:, 4:6]))
                    link(dve.tensor_tensor(st_[:, 9:10], st_[:, 9:10], lam[:, l:l + 1], ALU.mult))
                    p1, p2 = work[:, 2 * (n % 2), 0:nk], work[:, 2 * (n % 2) + 1, 0:nk]
                    link(dve.tensor_scalar(p2, p2, st_[:, 9:10], None, ALU.mult))
                    dve.wait_ge(pt_done, n_units + u0 + n - 1)
                    dve.scalar_tensor_tensor(probs[:, n % 2, 0:nk], p1, st_[:, 8:9], p2, ALU.mult, ALU.subtract) \
                       .then_inc(prob_ready, 1)

                def heads(p):
                    h, half, _ = units[2 * p]
                    dve.wait_ge(o_done, n_units + p0 + p + 1)
                    dve.tensor_copy(q2[:, h, half * S:(half + 1) * S], bank[6][:, 0:S]).then_inc(taken[6], 1)

                for n in range(len(units) + O_LAG + 1):
                    if n < len(units):
                        maxima(n)
                    if 1 <= n <= len(units):
                        differences(n - 1)
                    if n >= O_LAG + 2 and n % 2 == O_LAG % 2:
                        heads((n - O_LAG - 2) // 2)
                d0, c0, x0, o0 = (plan.at(f"subln_{l}", k) for k in ("diag", "bc", "xn", "o"))
                nt = wq // P
                dve.wait_ge(taken[4], plan.at(f"subln_{l}", "b4") + 1)
                link(dve.reciprocal(rms[:, 1, 0:KD * nt], rms[:, 0, 0:KD * nt]))
                for h in range(KD):
                    dve.tensor_tensor(head_diag[:, h, 0:wq].rearrange("p (t q) -> p t q", t=nt),
                                      ident.unsqueeze(1).broadcast_to([P, nt, P]),
                                      rms[:, 1, h * nt:(h + 1) * nt].unsqueeze(2).broadcast_to([P, nt, P]), ALU.mult) \
                       .then_inc(diag_ready, 1)

                def norm_head(h):
                    dve.wait_ge(bcast_done, c0 + h + 1)
                    if h >= 2:
                        dve.wait_ge(o_ready, n_units + o0 + h - 1)
                    tmp = xn[:, h % 2, 0:wq]
                    dve.scalar_tensor_tensor(tmp, q2[:, h, span(q_h)], sub_g[:, l:l + 1], bank[5][:, 0:wq],
                                             ALU.mult, ALU.mult).then_inc(xn_ready, 1)
                    dve.wait_ge(xn_ready, x0 + h + 1)
                    hi, lo = o2_hi[:, h, span(q_h)], o2_lo[:, h, span(q_h)]
                    link(dve.tensor_copy(hi, tmp))
                    dve.tensor_tensor(lo, tmp, hi.bitcast(f32), ALU.subtract).then_inc(o_ready, 1)

                def fourier_gates(st, i):
                    for b in range(4):
                        multiply_gate(st, i, b, fr[:, 4 * i + b:4 * i + b + 1, span(m_h)], wm)
                        norm_head(4 * i + b)

                gemm(f"gates_{l}1", fourier_gates, unrolled=True)
                gemm(f"attn_out_{l}")
                gemm(f"gates_{l}0", merge_gates(q2, (fr,), wm, span(m_h), o2_hi, o2_lo,
                                                3 * KD + 2 * KD * l, KD * (1 + l), gate_base(l, 1)))
                clear_sums()
                gemm(f"w_o_{l}", residual(1, m_h, lambda t: t + 1, 4))
                modulation(l, 2)
                norm_mod(f"n2_{l}", m_h)
                ffn(f"up_{l}1", KF * (2 + 2 * l), wm)
                clear_sums()
                gemm(f"down_{l}1", residual(2, m_h, lambda t: 2 * t + 2, 2))

            for l in range(LAYERS):
                layer(l)
            norm_x("n_final", "g_final", fin)
            for n in range(4):
                tt, b = n // 2, 5 + n % 2
                dve.wait_ge(boot_done, 17 + n + 1)
                dve.tensor_copy(rows_out[:, tt, (n % 2) * 512:(n % 2) * 512 + 512], bank[b][:, :]).then_inc(taken[b], 1)

        @block.tensor
        def _(pe):
            def claim(step, b, nth=0):
                n = plan.at(step, f"b{b}") + nth
                if n > 0:
                    pe.wait_ge(taken[b], n)

            def three(dst, hi, lo, m_hi, m_lo, first, final, swap=False):
                for n, (w, m) in enumerate(((hi, m_hi), (hi, m_lo), (lo, m_hi))):
                    s, v = (m, w) if swap else (w, m)
                    ins = pe.matmul(dst, s, v, start=first and n == 0, stop=final and n == 2)
                return ins

            def modulate(st, i):
                pair = mod_pair(st, i)
                pe.wait_ge(taken[7], pair + 1)
                pe.wait_ge(mod_step, pair * (4 * KD) + 4 * KD)
                for c in range(2):
                    for h in range(2):
                        ins = pe.matmul(bank[7][:, 2 * c + h:2 * c + h + 1], mod_acc[:, c, h, :], ones[:, 0:1],
                                        start=True, stop=True)
                ins.then_inc(mod_done, 1)

            def gemm(name, block_of, ready=None, unrolled=False):
                st = gemms[name]

                def body(i, ready=None):
                    for c in range(st.per):
                        n = st.first + c
                        pe.wait_ge(lo_ready, i * st.per + (n + 1))
                        if ready is not None and c == 0:
                            block_of(st, i, c, n % 2, ready)
                        else:
                            block_of(st, i, c, n % 2)
                    if st.mod:
                        modulate(st, i)

                if unrolled or st.bodies == 1:
                    for i in range(st.bodies):
                        body(i, ready if i == 0 else None)
                elif ready is not None:
                    body(0, ready)
                    with pe.Fori(1, st.bodies) as i:
                        body(i)
                else:
                    with pe.Fori(0, st.bodies) as i:
                        body(i)

            def claim_tile(st, i, b):
                pe.wait_ge(taken[b], i + st.use0[b]) if st.use0[b] > 0 or not isinstance(i, int) else None

            def features(m_hi, m_lo, w, after=None):
                def block_of(st, i, c, slot, ready=None):
                    def part(t, k):
                        at = slice(k * BLK + t * P, k * BLK + (t + 1) * P)
                        return three(bank[2 * c + t][:, 0:w], w_hi[slot][:, at], w_lo[slot][:, at], m_hi(k), m_lo(k),
                                     k == 0, k == st.kt - 1)

                    if ready is not None:
                        for t in range(2):
                            claim_tile(st, i, 2 * c + t)
                        for k in range(st.kt):
                            ready(k)
                            for t in range(2):
                                ins = part(t, k)
                                if k == st.kt - 1:
                                    ins.then_inc(group_done, 1)
                        return
                    for t in range(2):
                        claim_tile(st, i, 2 * c + t)
                        for k in range(st.kt):
                            ins = part(t, k)
                        ins.then_inc(group_done, 1)
                        if after is not None:
                            after((2 * i + c) * 2 + t)
                return block_of

            def token_rows(t0, tiles, after=None):
                def block_of(st, i, c, slot):
                    for t in range(tiles):
                        b = 2 * c + t // 2
                        if t % 2 == 0:
                            claim_tile(st, i, b)
                        cols = slice(t0 + t * P, t0 + (t + 1) * P)
                        for k in range(KD):
                            at = slice(k * BLK, (k + 1) * BLK)
                            ins = three(bank[b][:, (t % 2) * BLK:(t % 2 + 1) * BLK], w_hi[slot][:, at], w_lo[slot][:, at],
                                        u_hi[:, k, cols], u_lo[:, k, cols], k == 0, k == KD - 1, swap=True)
                        if t % 2 == 1:
                            ins.then_inc(group_done, 1)
                        if after is not None:
                            after((2 * i + c) * tiles + t)
                return block_of

            def down_strips(h_hi, h_lo, w):
                def block_of(st, i, c, slot):
                    b, part = c // 2, c % 2
                    if part == 0:
                        claim_tile(st, i, b)
                    for k in range(DOWN_KT):
                        at = slice(k * P, (k + 1) * P)
                        kk = part * DOWN_KT + k
                        ins = three(bank[b][:, 0:w], w_hi[slot][:, at], w_lo[slot][:, at], h_hi[:, kk, 0:w], h_lo[:, kk, 0:w],
                                    kk == 0, kk == KF - 1)
                    ins.then_inc(group_done, 1)
                return block_of

            def u_of(cols):
                return (lambda k: u_hi[:, k, cols]), (lambda k: u_lo[:, k, cols])

            def column_sums(name, w, summed=True):
                claim(name, 4)
                if summed:
                    pe.wait_ge(acc_step, plan.at(name, "acc"))
                    parts = [root[:, s, 0:w] for s in range(2)]
                else:
                    parts = [sq[:, k % 2, 0:w] for k in range(KD)]
                for n, part in enumerate(parts):
                    if not summed:
                        pe.wait_ge(sq_ready, plan.at(name, "sq") + n + 1)
                    for t in range(w // P):
                        ins = pe.matmul(bank[4][:, t:t + 1], part[:, t * P:(t + 1) * P], ones[:, 0:1],
                                        start=n == 0 and t == 0, stop=n == len(parts) - 1, skip_group_check=True)
                    if not summed or n == len(parts) - 1:
                        ins.then_inc(sums_done, 1)

            def spread(name, w):
                pe.wait_ge(diag_ready, plan.at(name, "diag") + 1)
                claim(name, 5)
                pe.matmul(bank[5][:, 0:w], ones[:, :], diag[:, 0:w // P, :].rearrange("p t q -> p (t q)"),
                          start=True, stop=True).then_inc(bcast_done, 1)

            def u_tile(name):
                return lambda k: pe.wait_ge(u_ready, plan.at(name, "u") + k + 1)

            pe.wait_ge(const_ready, 16)
            pe.wait_ge(rows_ready, 16 * len(ROWS))
            at = 0
            for t, rows_of in enumerate(ROW_TILES):
                n = sum(r for _, r in rows_of)
                ins = pe.transpose(bank[6][:, at:at + n], rows[0:n, t, :], ident[0:n, 0:n])
                at += n
            ins.then_inc(boot_done, 1)
            for n in range(12):
                s, q = n // 4, n % 4
                if q == 0:
                    pe.wait_ge(tok_ready[s], 16)
                claim("boot", 4 + n % 2, n // 2)
                for f in range(2):
                    for tt in range(2):
                        ins = pe.transpose(bank[4 + n % 2][:, f * S + tt * P:f * S + (tt + 1) * P],
                                           tok[:, s, tt, (2 * q + f) * P:(2 * q + f + 1) * P], ident)
                ins.then_inc(boot_done, 1)
            pe.wait_ge(set_ready, 6)
            claim("boot", 5, 6)
            pe.matmul(bank[5][:, 16:20], ones[0:1, :], lam_s[:, :, :].rearrange("p l j -> p (l j)"), start=True, stop=True) \
              .then_inc(boot_done, 1)
            claim("boot", 6, 1)
            pe.wait_ge(rel_ready, 64)
            pe.matmul(bank[6][:, 0:8], ones[0:1, :], sink_row[:, :], start=True, stop=True).then_inc(boot_done, 1)
            claim("boot", 5, 7)
            pe.matmul(bank[5][0:8, :], rel[:, 0:8], hot[:, 0, :], start=True, stop=True).then_inc(boot_done, 1)
            claim("boot", 6, 2)
            pe.matmul(bank[6][0:8, :], rel[:, 8:16], hot[:, 1, :], start=True, stop=True).then_inc(boot_done, 1)
            pe.wait_ge(cond_ready, 1)

            mem_cols, x_cols = slice(0, S), slice(S, T)
            column_sums("n_mem", S, False)
            column_sums("n_mix", S, False)
            spread("n_mem", S)
            gemm("k_me", features(*u_of(mem_cols), S), u_tile("n_mem"))
            gemm("v_me", token_rows(0, 2))
            spread("n_mix", S)
            gemm("qk_mb", features(*u_of(x_cols), S), u_tile("n_mix"))
            gemm("v_mb", token_rows(S, 2))
            gemm("q_sw", features(*u_of(x_cols), S))

            def kv_sw(st, i, c, slot):
                claim_tile(st, 0, 0)
                for k in range(KD):
                    at = slice(k * BLK, k * BLK + P)
                    ins = three(bank[0][:, 0:S], w_hi[slot][:, at], w_lo[slot][:, at], u_hi[:, k, x_cols], u_lo[:, k, x_cols],
                                k == 0, k == KD - 1)
                ins.then_inc(group_done, 1)
                claim_tile(st, 0, 1)
                for t in range(2):
                    cols = slice(S + t * P, S + (t + 1) * P)
                    for k in range(KD):
                        at = slice(k * BLK + P, (k + 1) * BLK)
                        ins = three(bank[1][:, t * P:(t + 1) * P], w_hi[slot][:, at], w_lo[slot][:, at],
                                    u_hi[:, k, cols], u_lo[:, k, cols], k == 0, k == KD - 1, swap=True)
                ins.then_inc(group_done, 1)

            gemm("kv_sw", kv_sw)
            gemm("q_me", features(*u_of(x_cols), S))

            def scores1(n):
                kind, h = UNITS1[n]
                b = n % 2
                claim("att1", b, n // 2)
                if kind == "moba":
                    r = slice(64 * (h % 2), 64 * (h % 2) + 64)
                    q, k, table = qk_mb[r, h // 2, :], qk_mb[r, 4 + h // 2, :], h
                elif kind == "swa":
                    r = slice(64 * (h % 2), 64 * (h % 2) + 64)
                    q, k, table = q_sw[r, h // 2, :], k_sw[r, h // 4, :], 8 + h
                else:
                    q, k, table = q_me[:, h, :], k_me[:, h, :], None
                for qb in range(2):
                    dst = bank[b][:, qb * S:(qb + 1) * S]
                    ins = pe.matmul(dst, q[:, qb * P:(qb + 1) * P], k, start=True, stop=table is None)
                    if table is not None:
                        shift = P * (1 - qb)
                        ins = pe.matmul(dst, reverse, hank[:, table, shift:shift + S], start=False, stop=True)
                ins.then_inc(score_ready, 1)

            def transposes1(n):
                b = 2 + n % 2
                pe.wait_ge(prob_ready, n + 1)
                claim("att1", b, n // 2)
                for kt in range(2):
                    for qb in range(2):
                        ins = pe.transpose(bank[b][:, kt * S + qb * P:kt * S + (qb + 1) * P],
                                           probs[:, n % 2, qb * S + kt * P:qb * S + (kt + 1) * P], ident)
                ins.then_inc(pt_done, 1)

            def outputs1(n):
                kind, h = UNITS1[n]
                b = 4 + n % 2
                pe.wait_ge(taken[2 + n % 2], plan.at("att1", f"b{2 + n % 2}") + n // 2 + 1)
                claim("att1", b, n // 2)
                for kt in range(2):
                    if kind == "moba":
                        v = v_mb[:, kt, (h // 2) * P:(h // 2 + 1) * P]
                    elif kind == "swa":
                        v = v_sw[:, kt, :]
                    else:
                        v = v_me[:, kt, h * P:(h + 1) * P]
                    ins = pe.matmul(bank[b][:, 0:S], v, p_t[:, n % 2, kt, :], start=kt == 0, stop=kt == 1)
                ins.then_inc(o_done, 1)

            for name, b in (("q_me", 0), ("q_me", 1), ("q_me", 2), ("q_me", 3)):
                pe.wait_ge(taken[b], gemms[name].taken(0, b))
            pe.wait_ge(hank_ready, 16)
            n_units = len(UNITS1)
            for n in range(n_units + O_LAG):
                if n < n_units:
                    scores1(n)
                if T_LAG <= n < n_units + T_LAG:
                    transposes1(n - T_LAG)
                if n >= O_LAG:
                    outputs1(n - O_LAG)
            for n, units_done in enumerate((8, 16, 20)):
                pe.wait_ge(o_ready, units_done)
                gemm(f"branch{n}", features(lambda k, n=n: o1_hi[:, 4 * n + k, :], lambda k, n=n: o1_lo[:, 4 * n + k, :], S))
            for n in range(3):
                gemm(f"gates1_{n}", features(*u_of(x_cols), S))

            def merged_tile(n0):
                return lambda k: pe.wait_ge(merged_ready, n0 + k + 1)

            gemm("w_out", features(lambda k: o1_hi[:, k, :], lambda k: o1_lo[:, k, :], S), merged_tile(0))
            column_sums("n_mix_post", S)
            spread("n_mix_post", S)
            column_sums("n_ffn", S, False)
            spread("n_ffn", S)
            gemm("up1", features(*u_of(x_cols), S), u_tile("n_ffn"))
            pe.wait_ge(hid_ready, KF + 1)
            gemm("down1", down_strips(hid1_hi, hid1_lo, S))
            column_sums("n_ffn_post", S)
            spread("n_ffn_post", S)

            def layer(l):
                both, q_h, m_h = [CTX, LAT], halves_of(l, "q"), halves_of(l, "merge")
                wq, wm = S * len(q_h), S * len(m_h)
                all_cols = slice(0, T)
                column_sums(f"n0_{l}", T, l > 0)
                spread(f"n0_{l}", T)
                gemm(f"up_{l}0", features(*u_of(all_cols), T), u_tile(f"n0_{l}"))
                pe.wait_ge(hid_ready, KF * (2 + 2 * l) + 1)
                gemm(f"down_{l}0", down_strips(hid2_hi, hid2_lo, T))
                column_sums(f"n1_{l}", T)
                spread(f"n1_{l}", T)
                gemm(f"q_{l}", features(*u_of(span(q_h)), wq), u_tile(f"n1_{l}"))
                gemm(f"k_{l}", features(*u_of(all_cols), T))
                gemm(f"f_{l}", token_rows(span(q_h).start, 2 * len(q_h)))
                slots, tiles = v_slots(l), rope_tiles(l)

                def rotate(n):
                    t, j = tiles[n]
                    claim(f"rope_{l}", 4, n)
                    pe.matmul(bank[4][:, 0:S], rot, (q2 if t == 0 else k2)[:, j, S:T], start=True, stop=True) \
                      .then_inc(rot_done, 1)

                def tokens(n):
                    g, h = four_unit(l, n)
                    claim(f"four_{l}", 5, n)
                    for tt in range(2):
                        ins = pe.matmul(bank[5][:, :], f2[:, 2 * h + tt, g * P:(g + 1) * P],
                                        table(C_DFT + 512 * tt, 512), start=tt == 0, stop=tt == 1)
                    ins.then_inc(dft_done, 1)

                def channels(n):
                    pe.wait_ge(taken[5], plan.at(f"four_{l}", "b5") + n + 1)
                    claim(f"four_{l}", 6, n)
                    for s, c in enumerate((C_DC, C_DS)):
                        ins = pe.matmul(bank[6][:, 0:S], table(c, P), dft[:, n % 2, s * S:(s + 1) * S],
                                        start=s == 0, stop=s == 1)
                    ins.then_inc(dft_done, 1)

                def after_value_tile(m):
                    if m == 0:
                        for name in (f"k_{l}", f"f_{l}"):
                            st = gemms[name]
                            for b in st.banks:
                                pe.wait_ge(taken[b], st.taken(st.bodies - 1, b))
                        pe.wait_ge(tabs_ready, 16 * (l + 1))
                    ropes, n, step = slots[m]
                    for r in ropes:
                        rotate(r)
                    if n is not None:
                        (tokens, channels)[step](n)

                gemm(f"v_{l}", token_rows(0, 4, after_value_tile), unrolled=True)
                units = att_units(l)
                u0, p0 = plan.at(f"att_{l}", "unit"), plan.at(f"att_{l}", "pair")
                pe.wait_ge(rope_ready, rope_base(l) + 16)

                def scores(n):
                    h, half, qb = units[n]
                    nk = T if half == LAT else S
                    at = half * S + qb * P
                    for c in range(2):
                        b = 2 * (n % 2) + c
                        claim(f"att_{l}", b, n // 2)
                        r = slice(64 * c, 64 * c + 64)
                        ins = pe.matmul(bank[b][:, 0:nk], q2[r, h, at:at + P], k2[r, h, 0:nk], start=True, stop=True)
                    ins.then_inc(score_ready, 1)

                def transposes(n):
                    h, half, qb = units[n]
                    kt = 4 if half == LAT else 2
                    pe.wait_ge(prob_ready, n_units + u0 + n + 1)
                    claim(f"att_{l}", 4 + n % 2, n // 2)
                    for k in range(kt):
                        ins = pe.transpose(bank[4 + n % 2][:, k * P:(k + 1) * P],
                                           probs[:, n % 2, k * P:(k + 1) * P], ident)
                    ins.then_inc(pt_done, 1)

                def outputs(p):
                    h, half, _ = units[2 * p]
                    kt = 4 if half == LAT else 2
                    for b in (4, 5):
                        pe.wait_ge(taken[b], plan.at(f"att_{l}", f"b{b}") + p + 1)
                    claim(f"att_{l}", 6, p)
                    for k in range(kt):
                        ins = pe.matmul(bank[6][:, 0:S], v2[:, k, h * P:(h + 1) * P], a_t[:, p % 2, k, :],
                                        start=k == 0, stop=k == kt - 1)
                    ins.then_inc(o_done, 1)

                for n in range(len(units) + O_LAG):
                    if n < len(units):
                        scores(n)
                    if T_LAG <= n < len(units) + T_LAG:
                        transposes(n - T_LAG)
                    if n > O_LAG and (n - O_LAG) % 2 == 1:
                        outputs((n - O_LAG) // 2)
                m_cols = span(m_h)
                pe.wait_ge(yf_ready, yf_base(l) + 4 * len(q_h))
                gemm(f"four_out_{l}", features(lambda k: yf_hi[:, k, m_cols], lambda k: yf_lo[:, k, m_cols], wm))
                nt = wq // P
                claim(f"subln_{l}", 4)
                for h in range(KD):
                    pe.wait_ge(sq_ready, plan.at(f"subln_{l}", "sq") + h + 1)
                    for t in range(nt):
                        ins = pe.matmul(bank[4][:, h * nt + t:h * nt + t + 1], head_sq[:, h, t * P:(t + 1) * P], ones[:, 0:1],
                                        start=True, stop=True)
                ins.then_inc(sums_done, 1)

                def spread_head(h):
                    pe.wait_ge(diag_ready, plan.at(f"subln_{l}", "diag") + h + 1)
                    if h == 0:
                        claim(f"subln_{l}", 5)
                    else:
                        pe.wait_ge(xn_ready, plan.at(f"subln_{l}", "xn") + h)
                    pe.matmul(bank[5][:, 0:wq], ones[:, :], head_diag[:, h, 0:wq], start=True, stop=True) \
                      .then_inc(bcast_done, 1)

                gemm(f"gates_{l}1", features(*u_of(m_cols), wm, spread_head), unrolled=True)
                o0 = n_units + plan.at(f"subln_{l}", "o")
                gemm(f"attn_out_{l}", features(lambda k: o2_hi[:, k, m_cols], lambda k: o2_lo[:, k, m_cols], wm),
                     lambda k: pe.wait_ge(o_ready, o0 + k + 1))
                gemm(f"gates_{l}0", features(*u_of(m_cols), wm))
                gemm(f"w_o_{l}", features(lambda k: o2_hi[:, k, m_cols], lambda k: o2_lo[:, k, m_cols], wm),
                     merged_tile(KD * (1 + l)))
                column_sums(f"n2_{l}", wm)
                spread(f"n2_{l}", wm)
                gemm(f"up_{l}1", features(*u_of(m_cols), wm), u_tile(f"n2_{l}"))
                pe.wait_ge(hid_ready, KF * (3 + 2 * l) + 1)
                gemm(f"down_{l}1", down_strips(hid2_hi, hid2_lo, wm))

            for l in range(LAYERS):
                layer(l)
            column_sums("n_final", S)
            spread("n_final", S)
            pe.wait_ge(updated, 3 * KD)
            for n in range(4):
                tt, b = n // 2, 5 + n % 2
                claim("store", b, n // 2)
                for k in range(4):
                    ins = pe.transpose(bank[b][:, k * P:(k + 1) * P],
                                       fin[:, 4 * (n % 2) + k, tt * P:(tt + 1) * P], ident)
                ins.then_inc(boot_done, 1)


_INS = ["x", "mem", "norm_mix_pre", "norm_mix_post", "norm_ffn_pre", "norm_ffn_post", "norm_mem", "w_in", "rel_bias",
        "swa_sinks", "w_mem_kv", "w_branch_moba", "w_branch_swa", "w_branch_mem", "w_out", "w_ffn_up", "ffn_conv_w",
        "ffn_conv_b", "w_ffn_down", "c_2", "ctx_2", "c_ctx_2", "w_mod_2", "b_mod_2", "norm_g_2", "ffn_w_in_2",
        "ffn_w_out_2", "w_in_2", "b_gate_2", "lam_params_2", "subln_g_2", "w_attn_out_2", "w_four_out_2", "w_o_2",
        "final_g_2"]


def kernel(**inputs):
    import numpy as _np
    import concourse.bacc as _bacc
    from concourse import mybir as _mybir
    from concourse.bass_utils import run_bass_kernel_spmd as _run

    nc = _bacc.Bacc("TRN2", target_bir_lowering=False, num_devices=1, dynamic_dma_scratch_size=1024)
    arrays, aps = {}, {}
    consts = dict(zip(("shape_const", "shape_hot"), shape_constants()))
    for name, v in [(n, inputs[n]) for n in _INS] + list(consts.items()):
        v = _np.ascontiguousarray(v)
        arrays[f"in_{name}"] = v
        aps[name] = nc.dram_tensor(f"in_{name}", v.shape, _mybir.dt.from_np(v.dtype), kind="ExternalInput").ap()
    out = nc.dram_tensor("out_rows", (1, S, D), _mybir.dt.float32, kind="ExternalOutput").ap()
    two_blocks(nc, aps, out)
    r = _run(nc, [arrays], core_ids=[0])
    return r.results[0]["out_rows"]
```

```python
import math
from contextlib import ExitStack

import numpy as np
import concourse.bass as bass
from concourse import mybir

P = 128
D = 1024
KD = D // P
S = 256
T = 2 * S
F = 2816
KF = F // P
EPS = 1e-6
LAYERS = 2
N_MOD = 9
MOD_TILES = N_MOD * KD
MOD_PAIRS = MOD_TILES // 2
BLK = 256
DOWN_KT = KF // 2
DOWN_HALF = 6
MASKED = -1e30
T_LAG, O_LAG = 3, 4
HANK = 3 * P
CTX, LAT = 0, 1

ROWS = {}
ROW_TILES = [
    [("g_mem", 8), ("g_mix_pre", 8), ("c_ctx", 8), ("c_lat", 8)],
    [("g_mix_post", 8), ("g_ffn_pre", 8), ("g_ffn_post", 8), ("norm_g", 48), ("b_gate", 32), ("g_final", 8), ("subln", 2)],
    [("conv_w0", 44), ("conv_w1", 44)],
    [("conv_w2", 44), ("conv_b", 44)],
    [("b_mod0", 72)],
    [("b_mod1", 72)],
]
COL = {}
_at = 0
for _t, _rows in enumerate(ROW_TILES):
    _r = 0
    for _name, _n in _rows:
        ROWS[_name] = (_t, _r, _n)
        COL[_name] = _at + _r
        _r += _n
    _at += _r
N_COLS = _at
N_FIRST = sum(n for _, n in ROW_TILES[0])

C_ID, C_REV = 0, 128
N_CONST = 256
C_ROT, C_COS, C_SIN, C_DFT, C_DC, C_DS = 256, 384, 640, 896, 1920, 2048
N_TABS = 1920


def shape_constants():
    c = np.zeros((P, N_CONST + N_TABS), np.float32)
    c[:, C_ID:C_ID + P] = np.eye(P)
    c[:, C_REV:C_REV + P] = np.eye(P)[::-1]
    for g in range(0, P, 32):
        for j in range(16):
            c[g + 16 + j, C_ROT + g + j] = -1.0
            c[g + j, C_ROT + g + 16 + j] = 1.0
    inv = 1.0 / (10000.0 ** (np.arange(0, 32, 2, dtype=np.float32) / np.float32(32)))
    pos = np.arange(S)
    for r in range(P):
        w = r % 64
        p = (pos // 64 if w < 32 else pos % 64).astype(np.float32)
        ang = p * np.float32(inv[(w % 32) % 16])
        c[r, C_COS:C_COS + S] = np.cos(ang)
        c[r, C_SIN:C_SIN + S] = np.sin(ang)
    a = 2 * np.pi * (np.outer(np.arange(S), np.arange(S)) % S) / S
    for tt in range(2):
        at = C_DFT + 512 * tt
        c[:, at:at + S] = np.cos(a[tt * P:(tt + 1) * P])
        c[:, at + S:at + 2 * S] = np.sin(a[tt * P:(tt + 1) * P])
    b = 2 * np.pi * (np.outer(np.arange(P), np.arange(P)) % P) / P
    norm = 1.0 / math.sqrt(S * P)
    c[:, C_DC:C_DC + P] = np.cos(b) * norm
    c[:, C_DS:C_DS + P] = -np.sin(b) * norm
    hot = np.zeros((33, 2, 512), np.float32)
    for i in range(511):
        dist = 255 - i
        n = max(dist, 0)
        big = 16 + int(np.float32(np.log(np.float32(max(n, 1)) / np.float32(16)))
                       / np.float32(math.log(8.0)) * np.float32(16))
        bucket = n if n < 16 else min(big, 31)
        hot[bucket, :, i] = 1.0
        hot[32, 0, i] = float(dist < 0)
        hot[32, 1, i] = float(dist < 0 or dist >= 128)
    return c, hot.reshape(33, 1024)


class Plan:

    def __init__(self):
        self.total, self.before = {}, {}

    def add(self, step, **counts):
        self.before[step] = dict(self.total)
        for k, n in counts.items():
            self.total[k] = self.total.get(k, 0) + n

    def at(self, step, key):
        return self.before[step].get(key, 0)


class Gemm:

    def __init__(self, plan, name, src, blocks, per, kt, cols, gpb, banks, mod=False, acc=0, token_major=False):
        self.token_major = token_major
        self.name, self.src, self.kt, self.cols = name, src, kt, cols
        self.per, self.bodies, self.gpb, self.banks = per, blocks // per, gpb, banks
        self.blocks = blocks
        self.first = plan.total.get("blk", 0)
        self.g0 = plan.total.get("grp", 0)
        self.mod = mod
        self.pair0 = plan.total.get("pair_mod", 0)
        self.acc0, self.acc = plan.total.get("acc", 0), acc
        counts = {f"b{b}": self.bodies for b in banks}
        counts["pair_mod"] = self.bodies if mod else 0
        counts["acc"] = 2 * acc * self.bodies - 2 if acc else 0
        plan.add(name, blk=blocks, grp=blocks * gpb, **counts)
        self.use0 = {b: plan.at(name, f"b{b}") for b in banks}

    def done(self, i, n):
        return self.g0 + self.gpb * self.per * i + n

    def half(self, t, block):
        if self.cols == P:
            a, b = (0, DOWN_HALF) if t == 0 else (DOWN_HALF, self.kt)
            return block[:, a * P:b * P].rearrange("p (k n) -> p k n", n=P)
        return block[:, 0:self.kt * BLK].rearrange("p (k n) -> p k n", n=BLK)[:, :, t * P:(t + 1) * P]

    def freed(self, i, c, t):
        return self.done(i, self.gpb * c + (self.gpb if self.token_major else t + 1))

    def parts(self, i, c, t):
        return i * (2 * self.per) + (2 * (self.first + c) + t + 1)

    def taken(self, i, bank):
        return self.use0[bank] + i + 1


def make_plan(a):
    plan, gemms = Plan(), {}

    def gemm(name, src, blocks, per=2, kt=KD, cols=BLK, gpb=2, banks=(0, 1, 2, 3), mod=False, acc=0,
             token_major=False):
        gemms[name] = Gemm(plan, name, src, blocks, per, kt, cols, gpb, banks, mod, acc, token_major)

    def norm(name, kind, summed=False):
        plan.add(name, sq=0 if summed else KD, sums=1 if summed else KD, diag=1, bc=1, xn=KD, b4=1, **kind)

    TO_U, MOD_U, TO_X, TO_OUT = {"u": KD}, {"u": KD, "xm": KD}, {"upd": KD}, {"upd": KD}

    def cols(w, first):
        return lambda j: w[:, bass.ds(j * BLK + first, BLK)].rearrange("(k p) n -> p k n", p=P)

    def pairs(w):
        return lambda j, c: w[:, bass.ds(j * BLK + c * F, BLK)].rearrange("(k p) n -> p k n", p=P)

    def down(w):
        return lambda j, c: w[c * DOWN_KT * P:(c + 1) * DOWN_KT * P, bass.ds(j * P, P)] \
            .rearrange("(k p) n -> p k n", p=P)

    w_in, w_kv = a["w_in"][0], a["w_mem_kv"][0]
    plan.add("boot_mem", b4=2, b5=2, b6=1)
    norm("n_mem", TO_U)
    gemm("k_me", cols(w_kv, 0), 2)
    plan.add("boot_x", b4=2, b5=2, b6=1)
    gemm("v_me", cols(w_kv, 512), 2, gpb=1, banks=(0, 2), token_major=True)
    norm("n_mix", TO_U)
    gemm("qk_mb", cols(w_in, 0), 4, mod=True)
    plan.add("boot_rest", b4=2, b5=4, b6=2)
    gemm("v_mb", cols(w_in, 1024), 2, gpb=1, banks=(0, 2), mod=True, token_major=True)
    plan.add("ctx_sums", sq=KD, sums=KD, b4=1)
    gemm("q_sw", cols(w_in, 1536), 2, mod=True)
    gemm("kv_sw", cols(w_in, 2048), 1, per=1, banks=(0, 1))
    gemm("q_me", cols(w_in, 2304), 2, mod=True)
    plan.add("att1", b0=7, b1=7, b6=6, b2=10, b3=10, b4=10, b5=10)
    for n, w in enumerate(("w_branch_moba", "w_branch_swa", "w_branch_mem")):
        gemm(f"branch{n}", cols(a[w][0], 0), 4, kt=4)
    for n in range(3):
        gemm(f"gates1_{n}", cols(w_in, 2816 + n * D), 4, mod=n < 2)
    gemm("w_out", cols(a["w_out"][0], 0), 4, acc=4)
    norm("n_mix_post", TO_X, summed=True)
    norm("n_ffn", TO_U)
    gemm("up1", pairs(a["w_ffn_up"][0]), 22)
    gemm("down1", down(a["w_ffn_down"][0]), 16, per=4, kt=DOWN_KT, cols=P, banks=(0, 1), mod=True, acc=2)
    norm("n_ffn_post", TO_X, summed=True)
    for l in range(LAYERS):
        last = l == LAYERS - 1
        w = a["w_in_2"][l]
        halves = 1 if last else 2
        norm(f"n0_{l}", MOD_U, summed=l > 0)
        gemm(f"up_{l}0", pairs(a["ffn_w_in_2"][l, 0]), 22, mod=True)
        gemm(f"down_{l}0", down(a["ffn_w_out_2"][l, 0]), 16, per=4, kt=DOWN_KT, cols=P, banks=(0, 1),
             mod=True, acc=2)
        norm(f"n1_{l}", MOD_U, summed=True)
        gemm(f"q_{l}", cols(w, 0), 4, mod=True)
        gemm(f"k_{l}", cols(w, 1024), 4, mod=not last)
        gemm(f"f_{l}", cols(w, 3072), 2, gpb=halves, banks=(0, 2) if last else (0, 1, 2, 3),
             token_major=True)
        plan.add(f"rope_{l}", b4=16)
        plan.add(f"four_{l}", b5=4 * halves, b6=4 * halves)
        gemm(f"v_{l}", cols(w, 2048), 4, token_major=True)
        units = 16 * halves
        per_slot = {f"b{2 * s + c}": len(range(s, units, 3)) for s in range(3) for c in range(2)}
        plan.add(f"att_{l}", **per_slot, b6=units, unit=units, pair=units // 2)
        gemm(f"four_out_{l}", cols(a["w_four_out_2"][l], 0), 4, kt=4)
        plan.add(f"subln_{l}", sq=KD, sums=1, diag=KD, bc=KD, xn=KD, o=KD, b4=1, b6=0)
        gemm(f"gates_{l}1", cols(w, 4608), 4, mod=not last)
        gemm(f"attn_out_{l}", cols(a["w_attn_out_2"][l], 0), 4, mod=not last)
        gemm(f"gates_{l}0", cols(w, 3584), 4, mod=not last)
        gemm(f"w_o_{l}", cols(a["w_o_2"][l], 0), 4, mod=not last, acc=4)
        norm(f"n2_{l}", MOD_U, summed=True)
        gemm(f"up_{l}1", pairs(a["ffn_w_in_2"][l, 1]), 22, mod=not last)
        gemm(f"down_{l}1", down(a["ffn_w_out_2"][l, 1]), 16, per=4, kt=DOWN_KT, cols=P, banks=(0, 1),
             mod=not last, acc=2)
    norm("n_final", TO_OUT, summed=True)
    plan.add("store", b5=2, b6=2)
    assert plan.total["pair_mod"] == LAYERS * MOD_PAIRS
    for l in range(LAYERS):
        for i in range(3):
            assert plan.at(f"n{i}_{l}", "pair_mod") >= MOD_PAIRS * l + MOD_PAIRS // 3 * (i + 1)
    for st in gemms.values():
        assert not st.mod or st.pair0 // MOD_PAIRS == (st.pair0 + st.bodies - 1) // MOD_PAIRS
    return plan, gemms


def two_blocks(nc, a, out):
    f32, f32r = mybir.dt.float32, mybir.dt.float32r
    ACT, ALU, AX = mybir.ActivationFunctionType, mybir.AluOpType, mybir.AxisListType
    plan, gemms = make_plan(a)
    stream = list(gemms.values())
    scratch = nc.dram_tensor("bias_tables", (2, 8, 512), f32, kind="Internal").ap()

    ctx = ExitStack()
    with ctx:
        def sb(name, shape, dt=f32, on=ctx):
            return on.enter_context(nc.sbuf_tensor(name, shape, dt))

        def sem(name):
            return ctx.enter_context(nc.semaphore(name))

        raw = [sb(f"raw{n}", [P, 2048]) for n in range(2)]
        w_hi = [sb(f"w_hi{n}", [P, 2048], f32r) for n in range(2)]
        w_lo = [sb(f"w_lo{n}", [P, 2048], f32r) for n in range(2)]
        mod_raw = [sb(f"mod_raw{n}", [P, KD, P]) for n in range(2)]
        x = sb("x", [P, KD, T])
        u_hi = sb("u_hi", [P, KD, T], f32r)
        u_lo = sb("u_lo", [P, KD, T], f32r)
        const = sb("const", [P, N_CONST])
        ones = sb("ones", [P, P])
        eps = sb("eps", [P, 1])
        col = sb("col", [P, N_COLS])
        cond = sb("cond", [P, KD, 2])
        mod_acc = sb("mod_acc", [P, 2, 2, P])
        mod_sum = sb("mod_sum", [P, 2 * MOD_TILES])
        mod = sb("mod", [P, MOD_TILES, 2])
        mod_a = sb("mod_a", [P, 3, KD, 2])
        mod_g = sb("mod_g", [P, 3, KD, 2])
        sub_g = sb("sub_g", [P, LAYERS])
        sinks = sb("sinks", [P, 8])
        lam = sb("lam", [P, LAYERS])
        stat = sb("stat", [P, 4, 16])
        xn = sb("xn", [P, 2, T])
        root = sb("root", [P, 2, T])
        diag = root[:, 0, :].rearrange("p (t q) -> p t q", t=4)
        probs = root
        rms = sb("rms", [P, 2, 4 * KD])
        work = sb("work", [P, 4, T])
        sq = work[:, :, :].rearrange("p s t -> p (s t)").rearrange("p (k t) -> p k t", k=KD)
        ctx_rms = sb("ctx_rms", [P, S // P])
        table_pick = sb("table_pick", [1, 1])

        a1 = ExitStack()
        tok = sb("tok", [P, 3, 2, D], on=a1)
        hank = tok[:, :, :, :].rearrange("p a b n -> p (a b n)").rearrange("p (h n) -> p h n", h=16)
        branch = tok[:, :, :, :].rearrange("p a b n -> p (a b n)").rearrange("p (j t) -> p j t", t=S)
        qk_mb = sb("qk_mb", [P, 8, S], on=a1)
        v_mb = sb("v_mb", [P, 2, 512], on=a1)
        q_sw = sb("q_sw", [P, 4, S], on=a1)
        k_sw = sb("k_sw", [P, 2, S], on=a1)
        v_sw = sb("v_sw", [P, 2, P], on=a1)
        q_me = sb("q_me", [P, 4, S], on=a1)
        y = sb("y", [P, KD, S], on=a1)
        k_me = y[:, 0:4, :]
        v_me = y[:, 4:8, :].rearrange("p (t a) s -> p t (a s)", t=2)
        boot = ExitStack()
        rows = sb("rows", [P, len(ROW_TILES), P], on=boot)
        hot = sb("hot", [33, 2, 512], on=boot)
        tables = sb("tables", [8, 2, 512], on=boot)
        rel = sb("rel", [33, 16], on=boot)
        sink_row = sb("sink_row", [1, 8], on=boot)
        lam_in = sb("lam_in", [1, LAYERS, 4, 64], on=boot)
        lam_p = sb("lam_p", [1, LAYERS, 2, 64], on=boot)
        lam_s = sb("lam_s", [1, LAYERS, 2], on=boot)
        lam_e = sb("lam_e", [P, LAYERS, 2], on=boot)
        boot.close()
        o1_hi = sb("o1_hi", [P, 12, S], f32r, on=a1)
        o1_lo = sb("o1_lo", [P, 12, S], f32r, on=a1)
        p_t = xn[:, :, :].rearrange("p s (k q) -> p s k q", k=2)
        a1.close()
        h1 = ExitStack()
        hid1_hi = sb("hid1_hi", [P, KF, S], f32r, on=h1)
        hid1_lo = sb("hid1_lo", [P, KF, S], f32r, on=h1)
        h1.close()
        a2 = ExitStack()
        q2 = sb("q2", [P, KD, T], on=a2)
        a2k = ExitStack()
        k2 = sb("k2", [P, KD, T], on=a2k)
        v2 = sb("v2", [P, 4, D], on=a2k)
        a2k.close()
        o2_hi = sb("o2_hi", [P, KD, T], f32r, on=a2)
        o2_lo = sb("o2_lo", [P, KD, T], f32r, on=a2)
        fa = sb("fa", [P, 4096], on=a2)
        f2 = fa[:, 0:2048].rearrange("p (t n) -> p t n", t=4)
        a_t = fa[:, 2048:4096].rearrange("p (s k q) -> p s k q", s=2, k=4)
        fr = fa[:, :].rearrange("p (j t) -> p j t", t=T)
        yf_hi = sb("yf_hi", [P, 4, T], f32r, on=a2)
        yf_lo = sb("yf_lo", [P, 4, T], f32r, on=a2)
        head_sq = k2
        head_diag = v2[:, :, :].rearrange("p t n -> p (t n)").rearrange("p (h t) -> p h t", t=T)
        dft = work[:, 2:4, :]
        tabs = sb("tabs", [P, N_TABS], on=a2)
        a2.close()
        h2 = ExitStack()
        hid2_hi = sb("hid2_hi", [P, KF, T], f32r, on=h2)
        hid2_lo = sb("hid2_lo", [P, KF, T], f32r, on=h2)
        h2.close()
        h3 = ExitStack()
        fin = sb("fin", [P, KD, S], on=h3)
        rows_out = sb("rows_out", [P, 2, D], on=h3)
        h3.close()

        bank = [ctx.enter_context(nc.psum_tensor(f"bank{b}", [P, 512], f32)) for b in range(8)]

        ident = const[:, C_ID:C_ID + P]
        reverse = const[:, C_REV:C_REV + P]

        def table(first, n):
            return tabs[:, first - N_CONST:first - N_CONST + n]

        rot, cos, sin = table(C_ROT, P), table(C_COS, S), table(C_SIN, S)

        raw_ready = [sem(f"raw_ready{n}") for n in range(2)]
        hi_ready = sem("hi_ready")
        lo_ready = sem("lo_ready")
        mod_ready = [sem(f"mod_ready{n}") for n in range(2)]
        mod_step = sem("mod_step")
        mod_done = sem("mod_done")
        group_done = sem("group_done")
        taken = [sem(f"taken{b}") for b in range(8)]
        tok_ready = [sem(f"tok_ready{n}") for n in range(3)]
        const_ready = sem("const_ready")
        tabs_ready = sem("tabs_ready")
        rows_ready = [sem("first_rows_ready"), sem("rows_ready")]
        rel_ready = sem("rel_ready")
        set_ready = sem("set_ready")
        boot_done = sem("boot_done")
        scratch_ready = sem("scratch_ready")
        hank_ready = sem("hank_ready")
        cond_ready = sem("cond_ready")
        ctx_ready = sem("ctx_ready")
        sq_ready = sem("sq_ready")
        acc_step = sem("acc_step")
        sums_done = sem("sums_done")
        diag_ready = sem("diag_ready")
        bcast_done = sem("bcast_done")
        xn_ready = sem("xn_ready")
        xm_ready = sem("xm_ready")
        u_part = sem("u_part")
        u_ready = sem("u_ready")
        updated = sem("updated")
        cv_first = sem("cv_first")
        cv_mid = sem("cv_mid")
        gelu_ready = sem("gelu_ready")
        table_set = sem("table_set")
        hid_prod = sem("hid_prod")
        hid_part = sem("hid_part")
        hid_ready = sem("hid_ready")
        gated = sem("gated")
        dve_step = sem("dve_step")
        merge_step = sem("merge_step")
        merged_ready = sem("merged_ready")
        score_ready = sem("score_ready")
        nmax_ready = sem("nmax_ready")
        weight_ready = sem("weight_ready")
        scaled_ready = sem("scaled_ready")
        prob_ready = sem("prob_ready")
        pt_done = sem("pt_done")
        o_done = sem("o_done")
        head_taken = sem("head_taken")
        o_ready = sem("o_ready")
        rot_done = sem("rot_done")
        rope_ready = sem("rope_ready")
        dft_done = sem("dft_done")
        yf_ready = sem("yf_ready")
        out_done = sem("out_done")

        block = ctx.enter_context(nc.Block())

        SCORE1 = (0, 1, 6)
        UNITS1 = [("moba", h) for h in range(8)] + [("swa", h) for h in range(8)] + [("mem", h) for h in range(4)]

        def halves_of(l, step):
            if l == LAYERS - 1 and step in ("q", "f", "merge", "ffn1"):
                return [LAT]
            return [CTX, LAT]

        def span(halves):
            return slice(halves[0] * S, (halves[-1] + 1) * S)

        def gate_base(l, nth):
            return 24 + 16 * l + 8 * nth

        def mod_pair(st, i):
            return i + st.pair0

        def dft_base(l):
            return 16 * l

        def rope_base(l):
            return 16 * l

        def rope_tiles(l):
            return [(t, j) for t in range(2) for j in range(KD)]

        def att_units(l):
            return [(h, half, qb) for h in range(8) for half in reversed(halves_of(l, "q")) for qb in range(2)]

        def v_slots(l):
            n_four = 4 * len(halves_of(l, "q"))
            slots = []
            for m in range(16):
                ropes = [m] if m < 14 else [14, 15] if m == 14 else []
                slots.append((ropes, m // 2 if m // 2 < n_four else None, m % 2))
            return slots

        def four_unit(l, n):
            hs = halves_of(l, "q")
            return n // len(hs), hs[n % len(hs)]

        def score_bank(n, c):
            return 2 * (n % 3) + c

        def exp_tile(n, c):
            s = 2 * (n % 3) + c
            return work[:, s, :] if s < 4 else xn[:, s - 4, :]

        def yf_base(l):
            return 8 * l

        row_src = {
            "g_mix_pre": a["norm_mix_pre"], "g_mix_post": a["norm_mix_post"], "g_ffn_pre": a["norm_ffn_pre"],
            "g_ffn_post": a["norm_ffn_post"], "g_mem": a["norm_mem"], "norm_g": a["norm_g_2"],
            "b_gate": a["b_gate_2"], "g_final": a["final_g_2"], "conv_w0": a["ffn_conv_w"][0, 0],
            "conv_w1": a["ffn_conv_w"][0, 1], "conv_w2": a["ffn_conv_w"][0, 2], "conv_b": a["ffn_conv_b"],
            "c_ctx": a["c_ctx_2"], "c_lat": a["c_2"], "subln": a["subln_g_2"],
            "b_mod0": a["b_mod_2"][0], "b_mod1": a["b_mod_2"][1],
        }
        flat = {1: "(r p) -> r p", 2: "a (r p) -> (a r) p", 3: "a b (r p) -> (a b r) p"}

        def load_rows(queue, first):
            for name, (t, r, n) in ROWS.items():
                if (t == 0) == first:
                    v = row_src[name]
                    queue.dma_start(rows[r:r + n, t, :], v.rearrange(flat[len(v.shape)], p=P)) \
                         .then_inc(rows_ready[min(t, 1)], 16)

        @block.sync
        def _(sp):
            def load(st, i, c):
                n = st.first + c
                j = i * (st.per // 2) + c // 2 if st.per != 2 else i
                if st.per == 2 and st.name[:2] != "up":
                    src = st.src(i * 2 + c)
                elif st.per == 1:
                    src = st.src(0)
                else:
                    src = st.src(j, c % 2)
                slot = raw[n % 2][:, 0:st.kt * st.cols].rearrange("p (k n) -> p k n", k=st.kt)
                sp.dma_start(slot, src).then_inc(raw_ready[n % 2], 16)

            def mod_loads(st, i):
                pair = mod_pair(st, i)
                l, in_layer = st.pair0 // MOD_PAIRS, st.pair0 % MOD_PAIRS
                for c in range(2):
                    if not (isinstance(pair, int) and pair == 0):
                        sp.wait_ge(mod_step, (pair - 1) * (4 * KD) + 2 * KD * (c + 1))
                    sp.dma_start(mod_raw[c][:, :, :],
                                 a["w_mod_2"][l][:, bass.ds((i + in_layer) * 2 * P + c * P, P)]
                                 .rearrange("(k p) n -> p k n", p=P)).then_inc(mod_ready[c], 16)

            def body(st, i):
                for c in range(st.per):
                    s = st.parts(i, c, 1) - 4
                    if not (isinstance(s, int) and s < 1):
                        sp.wait_ge(lo_ready, s)
                    load(st, i, c)
                    if st.mod and c == st.per - 1:
                        mod_loads(st, i)

            sp.dma_start(const[:, :], a["shape_const"][:, 0:N_CONST]).then_inc(const_ready, 16)
            sp.dma_start(tok[:, 0, :, :], a["mem"][0].rearrange("(t p) n -> p t n", p=P)).then_inc(tok_ready[0], 16)
            body(stream[0], 0)
            for n, name in ((1, "x"), (2, "ctx_2")):
                if n == 2:
                    load_rows(sp, False)
                sp.dma_start(tok[:, n, :, :], a[name][0].rearrange("(t p) n -> p t n", p=P)).then_inc(tok_ready[n], 16)
            sp.dma_start(hot[:, :, :], a["shape_hot"].rearrange("b (v n) -> b v n", v=2)).then_inc(rel_ready, 16)
            sp.wait_ge(set_ready, 1)
            sp.dma_start(rel[0:32, :], a["rel_bias"]).then_inc(rel_ready, 16)
            sp.dma_start(sink_row[:, :], a["swa_sinks"]).then_inc(rel_ready, 16)
            sp.dma_start(lam_in[:, :, :, :].rearrange("o l j d -> o (l j d)"),
                          a["lam_params_2"].rearrange("(o l) j d -> o (l j d)", o=1)).then_inc(rel_ready, 16)
            for st in stream:
                if st is not stream[0]:
                    body(st, 0)
                if st.bodies > 1:
                    with sp.Fori(1, st.bodies) as i:
                        body(st, i)
            for tt in range(2):
                sp.wait_ge(taken[5 + tt], plan.at("store", f"b{5 + tt}") + 2)
            sp.dma_start(out.rearrange("b (t p) n -> p (b t) n", p=P), rows_out[:, :, :]).then_inc(out_done, 16)
            sp.wait_ge(out_done, 16)

        @block.gpsimd
        def _(pool):
            def body(st, i):
                for c in range(st.per):
                    slot = (st.first + c) % 2
                    for t in range(2):
                        pool.wait_ge(hi_ready, st.parts(i, c, t))
                        pool.tensor_tensor(st.half(t, w_lo[slot]), st.half(t, raw[slot]), st.half(t, w_hi[slot]).bitcast(f32),
                                           ALU.subtract).then_inc(lo_ready, 1)

            def weigh_second_maps(l):
                for n, (_, half, _) in enumerate(att_units(l)):
                    nk = T if half == LAT else S
                    p2 = exp_tile(n, 1)[:, 0:nk]
                    pool.wait_ge(weight_ready, plan.at(f"att_{l}", "unit") + n + 1)
                    pool.tensor_scalar(p2, p2, stat[:, n % 4, 9:10], None, ALU.mult).then_inc(scaled_ready, 1)

            for st in stream:
                if st.name[:8] == "four_out":
                    body(st, 0)
                    weigh_second_maps(int(st.name[9:]))
                    with pool.Fori(1, st.bodies) as i:
                        body(st, i)
                elif st.bodies == 1:
                    body(st, 0)
                else:
                    with pool.Fori(0, st.bodies) as i:
                        body(st, i)

        @block.scalar
        def _(act):
            table_calls = [0]

            load_rows(act, True)

            def split(s):
                for st in stream:
                    if st.first <= s < st.first + st.blocks:
                        break
                else:
                    return
                act.wait_ge(raw_ready[s % 2], 16 * (s // 2 + 1))
                for t in range(2):
                    if s >= 2:
                        old = [q for q in stream if q.first <= s - 2 < q.first + q.blocks][0]
                        q = s - 2 - old.first
                        whole = old.kt != st.kt or old.cols != st.cols
                        act.wait_ge(group_done, old.freed(q // old.per, q % old.per, 1 if whole else t))
                    act.activation(st.half(t, w_hi[s % 2]), st.half(t, raw[s % 2]), ACT.Copy).then_inc(hi_ready, 1)

            def split_two_ahead(st, i, c, final):
                if final and c + 2 >= st.per:
                    return split(st.first + st.per * (st.bodies - 1) + c + 2)
                n = st.first + c + 2
                act.wait_ge(raw_ready[n % 2], i * (8 * st.per) + 16 * (n // 2 + 1))
                for t in range(2):
                    act.wait_ge(group_done, st.freed(i, c, t))
                    act.activation(st.half(t, w_hi[n % 2]), st.half(t, raw[n % 2]), ACT.Copy).then_inc(hi_ready, 1)

            def gemm(name, evac=None, unrolled=False, table=None):
                st = gemms[name]

                def body(i, final):
                    if table is not None:
                        act.wait_ge(table_set, i + (table_calls[0] + 1))
                        act.activation(table_pick[:, :], eps[0:1, 0:1], table).then_inc(table_set, 1)
                    for c in range(st.per):
                        evac_first = final and c == st.per - 1 or st.token_major
                        if evac is not None and evac_first:
                            evac(st, i, c)
                        split_two_ahead(st, i, c, final)
                        if evac is not None and not evac_first:
                            evac(st, i, c)

                if unrolled:
                    for i in range(st.bodies - 1):
                        body(i, False)
                elif st.bodies > 1:
                    with act.Fori(0, st.bodies - 1) as i:
                        body(i, False)
                body(st.bodies - 1, True)
                if table is not None:
                    table_calls[0] += st.bodies

            def copy_tiles(dst, cols):
                def evac(st, i, c):
                    for t in range(2):
                        act.wait_ge(group_done, st.done(i, 2 * c + t + 1))
                        b = 2 * c + t
                        act.activation(dst[:, bass.ds(i * 4 + b, 1), cols], bank[b][:, 0:cols.stop - cols.start]
                                       .rearrange("p (o t) -> p o t", o=1), ACT.Copy).then_inc(taken[b], 1)
                return evac

            def copy_rows(dst, first, tiles):
                per_block = tiles // 2

                def evac(st, i, c):
                    for t in range(per_block):
                        act.wait_ge(group_done, st.done(i, per_block * c + t + 1))
                        b = 2 * c + t
                        act.activation(dst[:, first + 2 * t:first + 2 * t + 2, bass.ds(i * 2 * BLK + c * BLK, BLK)],
                                       bank[b][:, :].rearrange("p (t n) -> p t n", t=2), ACT.Copy) \
                           .then_inc(taken[b], 1)
                return evac

            def squares(name, src, ready):
                for k in range(KD):
                    for s, v in ready(k):
                        act.wait_ge(s, v)
                    act.activation(sq[:, k, :], src(k), ACT.Square).then_inc(sq_ready, 1)

            def mean_root(name, w, n_sums, first=0):
                act.wait_ge(sums_done, plan.at(name, "sums") + n_sums)
                if plan.at(name, "diag"):
                    act.wait_ge(diag_ready, plan.at(name, "diag"))
                act.activation(rms[:, 0, first:first + w // P], bank[4][:, 0:w // P], ACT.Sqrt, bias=eps[:, 0:1], scale=1.0 / D) \
                   .then_inc(taken[4], 1)

            def hi_tiles(name, w, t0):
                for k in range(KD):
                    act.wait_ge(xn_ready, plan.at(name, "xn") + k + 1)
                    act.activation(u_hi[:, k, t0:t0 + w], xn[:, k % 2, 0:w], ACT.Copy).then_inc(u_part, 1)

            def modulated(name, l, i, halves):
                x0, u0, m0 = plan.at(name, "xn"), plan.at(name, "u"), plan.at(name, "xm")
                w, t = S * len(halves), span(halves)
                for k in range(KD):
                    act.wait_ge(xn_ready, x0 + k + 1)
                    act.wait_ge(u_ready, u0 + k - 1)
                    for h in halves:
                        lo = (h - halves[0]) * S
                        ins = act.activation(work[:, k % 2, lo:lo + S], xn[:, k % 2, lo:lo + S], ACT.Identity,
                                             bias=mod[:, 3 * i * KD + k, h:h + 1], scale=mod_a[:, i, k, h:h + 1])
                    ins.then_inc(xm_ready, 1)
                    act.wait_ge(xm_ready, m0 + k + 1)
                    act.activation(u_hi[:, k, t], work[:, k % 2, 0:w], ACT.Copy).then_inc(u_part, 1)

            def silu_tiles(w):
                def evac(st, i, c):
                    if c == 0:
                        for t in range(2):
                            act.wait_ge(group_done, st.done(i, t + 1))
                            act.wait_ge(taken[2 + t], st.taken(i, 2 + t) - 1)
                            act.activation(work[:, t, 0:w], bank[t][:, 0:w], ACT.Silu).then_inc(taken[t], 1)
                return evac

            squares("n_mem", lambda k: y[:, k, :], lambda k: [(taken[4 + k // 2 % 2], k // 4 + 1)])
            mean_root("n_mem", S, KD)
            split(0)
            split(1)
            hi_tiles("n_mem", S, 0)
            act.wait_ge(taken[6], 1)
            act.activation(cond[:, :, :], col[:, COL["c_ctx"]:COL["c_ctx"] + 2 * KD]
                           .rearrange("p (c k) -> p k c", c=2), ACT.Silu).then_inc(cond_ready, 1)

            gemm("k_me", copy_tiles(k_me, slice(0, S)))
            squares("n_mix", lambda k: x[:, k, S:T],
                    lambda k: [(taken[4 + k // 2 % 2], plan.at("boot_x", f"b{4 + k // 2 % 2}") + k // 4 + 1)])
            gemm("v_me", copy_rows(v_me, 0, 2))
            mean_root("n_mix", S, KD)
            hi_tiles("n_mix", S, S)
            gemm("qk_mb", copy_tiles(qk_mb, slice(0, S)))
            act.wait_ge(boot_done, 15)
            act.activation(lam_e[:, :, :], bank[5][:, 16:20].rearrange("p (l j) -> p l j", l=2), ACT.Exp) \
               .then_inc(taken[5], 1)
            for b in (4, 5, 6):
                act.wait_ge(taken[b], plan.at("ctx_sums", f"b{b}"))
            act.dma_start(scratch.rearrange("v h n -> h v n"), tables[:, :, :]).then_inc(scratch_ready, 16)
            act.wait_ge(scratch_ready, 16)
            shifted = bass.AP(tensor=scratch.tensor, offset=0, ap=[[1, P], [512, 16], [1, HANK]])
            act.dma_start(hank, shifted).then_inc(hank_ready, 16)
            squares("ctx_sums", lambda k: x[:, k, 0:S], lambda k: [(taken[4], plan.at("ctx_sums", "b4"))])
            gemm("v_mb", copy_rows(v_mb, 0, 2))
            act.wait_ge(sums_done, plan.at("ctx_sums", "sums") + KD)
            act.activation(ctx_rms[:, :], bank[4][:, 0:S // P], ACT.Sqrt, bias=eps[:, 0:1], scale=1.0 / D) \
               .then_inc(taken[4], 1)
            gemm("q_sw", copy_tiles(q_sw, slice(0, S)))

            def kv_sw(st, i, c):
                act.wait_ge(group_done, st.done(0, 1))
                for kv in range(2):
                    for to in range(2):
                        ins = act.activation(k_sw[64 * to:64 * to + 64, kv, :], bank[0][64 * kv:64 * kv + 64, 0:S], ACT.Copy)
                ins.then_inc(taken[0], 1)
                act.wait_ge(group_done, st.done(0, 2))
                act.activation(v_sw[:, :, :], bank[1][:, 0:2 * P].rearrange("p (t n) -> p t n", t=2), ACT.Copy) \
                   .then_inc(taken[1], 1)

            gemm("kv_sw", kv_sw)
            gemm("q_me", copy_tiles(q_me, slice(0, S)))

            def exp1(n):
                kind, h = UNITS1[n]
                scale = 0.125 if kind != "mem" else 1.0 / math.sqrt(128)
                act.wait_ge(nmax_ready, n + 1)
                if n >= 2:
                    act.wait_ge(prob_ready, n - 1)
                st_ = stat[:, n % 2, :]
                if kind == "swa":
                    act.activation(st_[:, 6:8], st_[:, 2:4], ACT.Exp, bias=sinks[:, h:h + 1])
                for q in range(2):
                    ins = act.activation(work[:, n % 2, q * S:(q + 1) * S], bank[SCORE1[n % 3]][:, q * S:(q + 1) * S], ACT.Exp,
                                         bias=st_[:, 2 + q:3 + q], scale=scale, accum_out=st_[:, 4 + q:5 + q])
                ins.then_inc(taken[SCORE1[n % 3]], 1)

            def copy_pt1(n):
                act.wait_ge(pt_done, n + 1)
                if n >= 2:
                    act.wait_ge(o_done, n - 1)
                act.activation(p_t[:, n % 2, :, :], bank[2 + n % 2][:, :].rearrange("p (k q) -> p k q", k=2), ACT.Copy) \
                   .then_inc(taken[2 + n % 2], 1)

            for n in range(len(UNITS1) + T_LAG):
                if n >= T_LAG:
                    copy_pt1(n - T_LAG)
                if n < len(UNITS1):
                    exp1(n)
            for n in range(3):
                gemm(f"branch{n}", copy_tiles(branch[:, 8 * n:8 * n + 8, :], slice(0, S)))

            def gates(w, base, bias=None):
                def evac(st, i, c):
                    for t in range(2):
                        b = 2 * c + t
                        act.wait_ge(group_done, st.done(i, b + 1))
                        act.wait_ge(gated, i * 4 + (base + 1))
                        kw = {} if bias is None else {"bias": col[:, bass.ds(i * 4 + (b + bias), 1)]}
                        act.activation(work[:, b, 0:w], bank[b][:, 0:w], ACT.Sigmoid, **kw).then_inc(taken[b], 1)
                return evac

            for n in range(3):
                gemm(f"gates1_{n}", gates(S, 8 * n))
            gemm("w_out")
            mean_root("n_mix_post", S, 1)
            squares("n_ffn", lambda k: x[:, k, S:T], lambda k: [(updated, k + 1)])
            mean_root("n_ffn", S, KD)
            hi_tiles("n_ffn", S, S)

            def conv_tiles(st, i, c):
                for t in range(2):
                    act.wait_ge(group_done, st.done(i, 2 * c + t + 1))
                    if c == 0:
                        act.wait_ge(hid_ready, i * 2 + 1)
                    at = i * 2 + (c * KF + t)
                    b = 2 * c + t
                    act.activation(work[:, b, 0:S], bank[b][:, 0:S], ACT.Identity,
                                   bias=col[:, bass.ds(at + COL["conv_b"], 1)],
                                   scale=col[:, bass.ds(at + COL["conv_w2"], 1)]).then_inc(cv_first, 1)
                if c == 0:
                    for t in range(2):
                        act.wait_ge(taken[t], st.taken(i, t))
                        act.activation(work[:, t, 0:S], work[:, t, 0:S], ACT.Gelu_apprx_tanh).then_inc(gelu_ready, 1)

            gemm("up1", conv_tiles, table=ACT.Gelu_apprx_tanh)
            gemm("down1")
            mean_root("n_ffn_post", S, 1)

            def layer(l):
                both, q_h, m_h = [CTX, LAT], halves_of(l, "q"), halves_of(l, "merge")
                wq, wm = S * len(q_h), S * len(m_h)
                if l == 0:
                    act.wait_ge(diag_ready, plan.at("n0_0", "diag"))
                    act.activation(rms[:, 0, 0:S // P], ctx_rms[:, :], ACT.Copy).then_inc(ctx_ready, 1)
                    squares("n0_0", lambda k: x[:, k, S:T], lambda k: [(updated, KD + k + 1)])
                    mean_root("n0_0", S, KD, S // P)
                else:
                    mean_root(f"n0_{l}", T, 1)
                modulated(f"n0_{l}", l, 0, both)
                gemm(f"up_{l}0", silu_tiles(T), table=ACT.Silu)
                gemm(f"down_{l}0")
                mean_root(f"n1_{l}", T, 1)
                act.dma_start(tabs[:, :], a["shape_const"][:, N_CONST:]).then_inc(tabs_ready, 16)
                modulated(f"n1_{l}", l, 1, both)
                gemm(f"q_{l}", copy_tiles(q2, span(q_h)))
                gemm(f"k_{l}", copy_tiles(k2, slice(0, T)))
                gemm(f"f_{l}", copy_rows(f2, 2 * q_h[0], 2 * len(q_h)))
                slots = v_slots(l)

                def values(st, i, c):
                    for t in range(4):
                        _, n, step = slots[(2 * i + c) * 4 + t]
                        if n is not None and step == 0:
                            act.wait_ge(dft_done, dft_base(l) + 2 * n + 1)
                            act.activation(dft[:, n % 2, :], bank[5][:, :], ACT.Copy).then_inc(taken[5], 1)
                        if t % 2 == 1:
                            b = 2 * c + t // 2
                            act.wait_ge(group_done, st.done(i, b + 1))
                            at = (2 * i + c) * BLK
                            act.activation(v2[:, t - 1:t + 1, at:at + BLK],
                                           bank[b][:, :].rearrange("p (t n) -> p t n", t=2), ACT.Copy) \
                               .then_inc(taken[b], 1)

                gemm(f"v_{l}", values, unrolled=True)
                units = att_units(l)
                u0, p0 = plan.at(f"att_{l}", "unit"), plan.at(f"att_{l}", "pair")

                def exps(n):
                    h, half, qb = units[n]
                    nk = T if half == LAT else S
                    act.wait_ge(nmax_ready, len(UNITS1) + u0 + n + 1)
                    act.wait_ge(prob_ready, len(UNITS1) + u0 + n - 2)
                    st_ = stat[:, n % 4, :]
                    for c in range(2):
                        b = score_bank(n, c)
                        act.activation(exp_tile(n, c)[:, 0:nk], bank[b][:, 0:nk], ACT.Exp, bias=st_[:, 2 + c:3 + c],
                                       scale=0.125, accum_out=st_[:, 4 + c:5 + c]).then_inc(taken[b], 1)

                def copy_pt(n):
                    h, half, qb = units[n]
                    kt = 4 if half == LAT else 2
                    act.wait_ge(pt_done, len(UNITS1) + u0 + n + 1)
                    if n >= 4:
                        act.wait_ge(o_done, len(UNITS1) + p0 + n // 2 - 1)
                    act.activation(a_t[:, (n // 2) % 2, 0:kt, qb * P:(qb + 1) * P],
                                   bank[6][:, 0:kt * P].rearrange("p (k q) -> p k q", k=kt), ACT.Copy) \
                       .then_inc(taken[6], 1)

                def heads(p):
                    h, half, _ = units[2 * p]
                    act.wait_ge(o_done, len(UNITS1) + p0 + p + 1)
                    act.activation(q2[:, h, half * S:(half + 1) * S], bank[7][:, 0:S], ACT.Copy).then_inc(head_taken, 1)

                for n in range(len(units) + O_LAG + 1):
                    if n >= O_LAG + 2 and n % 2 == O_LAG % 2:
                        heads((n - O_LAG - 2) // 2)
                    if T_LAG <= n < len(units) + T_LAG:
                        copy_pt(n - T_LAG)
                    if n < len(units):
                        exps(n)
                act.wait_ge(head_taken, plan.at(f"subln_{l}", "pair"))
                for h in range(KD):
                    act.activation(head_sq[:, h, 0:wq], q2[:, h, span(q_h)], ACT.Square).then_inc(sq_ready, 1)
                gemm(f"four_out_{l}", copy_tiles(fr, span(m_h)))
                act.wait_ge(sums_done, plan.at(f"subln_{l}", "sums") + 1)
                act.wait_ge(diag_ready, plan.at(f"subln_{l}", "diag"))
                nt = KD * wq // P
                act.activation(rms[:, 0, 0:nt], bank[4][:, 0:nt], ACT.Sqrt, bias=eps[:, 0:1], scale=1.0 / P) \
                   .then_inc(taken[4], 1)
                b_gate = COL["b_gate"] + 2 * l * KD
                gemm(f"gates_{l}1", gates(wm, gate_base(l, 0), b_gate + KD))
                gemm(f"attn_out_{l}", copy_tiles(q2, span(m_h)))
                gemm(f"gates_{l}0", gates(wm, gate_base(l, 1), b_gate))
                gemm(f"w_o_{l}")
                mean_root(f"n2_{l}", wm, 1)
                modulated(f"n2_{l}", l, 2, m_h)
                gemm(f"up_{l}1", silu_tiles(wm), table=ACT.Silu)
                gemm(f"down_{l}1")

            for l in range(LAYERS):
                layer(l)
            mean_root("n_final", S, 1)

        @block.vector
        def _(dve):
            steps = [0]

            def link(ins):
                steps[0] += 1
                ins.then_inc(dve_step, 1)
                dve.wait_ge(dve_step, steps[0])

            dve.memset(rel[32:33, :], MASKED).then_inc(set_ready, 1)
            dve.memset(ones[:, :], 1.0).then_inc(set_ready, 1)
            dve.memset(eps[:, :], EPS).then_inc(set_ready, 1)
            dve.sem_inc(hid_ready, 1)
            dve.sem_inc(gated, 1)
            dve.sem_inc(taken[7], 1)
            dve.sem_inc(mod_done, 1)
            dve.sem_inc(table_set, 1)
            def rstd_of(name, w):
                nt = w // P
                dve.wait_ge(taken[4], plan.at(name, "b4") + 1)
                if name == "n0_0":
                    dve.wait_ge(ctx_ready, 1)
                link(dve.reciprocal(rms[:, 1, 0:nt], rms[:, 0, 0:nt]))
                dve.tensor_tensor(diag[:, 0:nt, :], ident.unsqueeze(1).broadcast_to([P, nt, P]),
                                  rms[:, 1, 0:nt].unsqueeze(2).broadcast_to([P, nt, P]), ALU.mult).then_inc(diag_ready, 1)
                dve.wait_ge(bcast_done, plan.at(name, "bc") + 1)

            def lo_part(k, src, u0, w, t0):
                dve.wait_ge(u_part, u0 + k + 1)
                dve.tensor_tensor(u_lo[:, k, t0:t0 + w], src, u_hi[:, k, t0:t0 + w].bitcast(f32), ALU.subtract) \
                   .then_inc(u_ready, 1)

            def norm_u(name, src, gain, t0):
                x0, u0 = plan.at(name, "xn"), plan.at(name, "u")
                rstd_of(name, S)
                for k in range(KD + 1):
                    if k < KD:
                        if u0 + k >= 2:
                            dve.wait_ge(u_ready, u0 + k - 1)
                        dve.scalar_tensor_tensor(xn[:, k % 2, 0:S], src(k), col[:, COL[gain] + k:COL[gain] + k + 1],
                                                 bank[5][:, 0:S], ALU.mult, ALU.mult).then_inc(xn_ready, 1)
                    if k >= 1:
                        lo_part(k - 1, xn[:, (k - 1) % 2, 0:S], u0, S, t0)

            def norm_x(name, gain, dst=None):
                x0, n0 = plan.at(name, "xn"), plan.at(name, "upd")
                rstd_of(name, S)
                for k in range(KD):
                    g = col[:, COL[gain] + k:COL[gain] + k + 1]
                    if dst is not None:
                        dve.scalar_tensor_tensor(dst[:, k, :], x[:, k, S:T], g, bank[5][:, 0:S], ALU.mult, ALU.mult) \
                           .then_inc(updated, 1)
                        continue
                    if k >= 2:
                        dve.wait_ge(updated, n0 + k - 1)
                    dve.scalar_tensor_tensor(xn[:, k % 2, 0:S], y[:, k, :], g, bank[5][:, 0:S], ALU.mult, ALU.mult) \
                       .then_inc(xn_ready, 1)
                    dve.wait_ge(xn_ready, x0 + k + 1)
                    dve.tensor_tensor(x[:, k, S:T], x[:, k, S:T], xn[:, k % 2, 0:S], ALU.add).then_inc(updated, 1)

            def norm_mod(name, halves):
                u0, m0 = plan.at(name, "u"), plan.at(name, "xm")
                w, t = S * len(halves), span(halves)
                rstd_of(name, w)
                for k in range(KD + 1):
                    if k < KD:
                        if k >= 2:
                            dve.wait_ge(xm_ready, m0 + k - 1)
                        dve.tensor_tensor(xn[:, k % 2, 0:w], x[:, k, t], bank[5][:, 0:w], ALU.mult).then_inc(xn_ready, 1)
                    if k >= 1:
                        lo_part(k - 1, work[:, (k - 1) % 2, 0:w], u0, w, t.start)

            def sum_squares(st, i, t, src, w, final):
                alone = max(0, t - (st.acc - 2)) if final else 0
                n = i * (2 * st.acc) + (st.acc0 + 2 * t - alone)
                dve.tensor_tensor(xn[:, t % 2:t % 2 + 1, 0:w], src, src, ALU.mult).then_inc(acc_step, 1)
                if final and t >= st.acc - 2:
                    return
                dve.wait_ge(acc_step, n + 1)
                acc = root[:, t % 2, 0:w]
                dve.tensor_tensor(acc, acc, xn[:, t % 2, 0:w], ALU.add).then_inc(acc_step, 1)
                dve.wait_ge(acc_step, n + 2)

            def clear_sums():
                link(dve.memset(root[:, :, :], 0.0))

            def mod_products(st, i):
                pair = mod_pair(st, i)
                dve.wait_ge(mod_done, pair + 1)
                for c in range(2):
                    dve.wait_ge(mod_ready[c], pair * 16 + 16)
                    for k in range(KD):
                        for h in range(2):
                            acc, by = mod_acc[:, c, h, :], cond[:, k, h:h + 1]
                            if k == 0:
                                ins = dve.tensor_scalar(acc, mod_raw[c][:, k, :], by, None, ALU.mult)
                            else:
                                dve.wait_ge(mod_step, pair * (4 * KD) + (2 * KD * c + 2 * k + h - 1))
                                ins = dve.scalar_tensor_tensor(acc, mod_raw[c][:, k, :], by, acc, ALU.mult, ALU.add)
                            ins.then_inc(mod_step, 1)

            def take_mod(st, i):
                dve.wait_ge(mod_done, mod_pair(st, i) + 2)
                at = bass.ds(i * 4 + 4 * (st.pair0 % MOD_PAIRS), 4)
                dve.tensor_reduce(mod_sum[:, at], bank[7][:, :].rearrange("p (c n) -> p c n", c=4), AX.X, ALU.add) \
                   .then_inc(taken[7], 1)

            def gemm(name, evac=None, unrolled=False):
                st = gemms[name]
                if evac is None and not st.mod:
                    return

                def body(i, **final):
                    if st.mod:
                        mod_products(st, i)
                    if evac is not None:
                        evac(st, i, **final)
                    if st.mod:
                        take_mod(st, i)

                if unrolled or st.bodies == 1:
                    for i in range(st.bodies):
                        body(i)
                elif st.acc:
                    with dve.Fori(0, st.bodies - 1) as i:
                        body(i, final=False)
                    body(st.bodies - 1, final=True)
                else:
                    with dve.Fori(0, st.bodies) as i:
                        body(i)

            def multiply_gate(st, i, b, at, w):
                dve.wait_ge(taken[b], st.taken(i, b))
                dve.tensor_tensor(at, at, work[:, b:b + 1, 0:w], ALU.mult).then_inc(gated, 1)

            def multiply_gates(dst, w, cols):
                def evac(st, i):
                    for b in range(4):
                        multiply_gate(st, i, b, dst[:, bass.ds(i * 4 + b, 1), cols], w)
                return evac

            def merge_gates(dst, others, w, cols, hi, lo, base, g0):
                per = len(others) + 1

                def evac(st, i):
                    for b in range(4):
                        at = bass.ds(i * 4 + b, 1)
                        m = dst[:, at, cols]
                        multiply_gate(st, i, b, m, w)
                        dve.wait_ge(gated, i * 4 + (g0 + b + 2))
                        for n, o in enumerate(others):
                            dve.tensor_tensor(m, m, o[:, at, cols], ALU.add).then_inc(merge_step, 1)
                            dve.wait_ge(merge_step, i * (4 * per) + (base + per * b + n + 1))
                        dve.tensor_copy(hi[:, at, cols], m).then_inc(merge_step, 1)
                        dve.wait_ge(merge_step, i * (4 * per) + (base + per * b + per))
                        dve.tensor_tensor(lo[:, at, cols], m, hi[:, at, cols].bitcast(f32), ALU.subtract) \
                           .then_inc(merged_ready, 1)
                return evac

            def take_tokens(first, dst):
                for q in range(4):
                    b = 4 + q % 2
                    dve.wait_ge(boot_done, first + q)
                    dve.tensor_copy(dst[:, 2 * q:2 * q + 2, :], bank[b][:, :].rearrange("p (f t) -> p f t", f=2)) \
                       .then_inc(taken[b], 1)

            def take_columns(done, first, n):
                dve.wait_ge(boot_done, done)
                link(dve.tensor_copy(col[:, first:first + n], bank[6][:, 0:n]))
                dve.sem_inc(taken[6], 1)

            take_tokens(1, y)
            take_columns(5, 0, N_FIRST)
            norm_u("n_mem", lambda k: y[:, k, :], "g_mem", 0)
            take_tokens(6, x[:, :, S:T])
            take_columns(10, N_FIRST, N_COLS - N_FIRST)
            norm_u("n_mix", lambda k: x[:, k, S:T], "g_mix_pre", S)
            dve.wait_ge(cond_ready, 1)
            dve.wait_ge(rel_ready, 64)
            for l in range(LAYERS):
                dve.tensor_tensor(lam_p[:, l, :, :], lam_in[:, l, 0:4:2, :], lam_in[:, l, 1:4:2, :], ALU.mult).then_inc(set_ready, 1)
            dve.wait_ge(set_ready, 5)
            dve.tensor_reduce(lam_s[:, :, :], lam_p[:, :, :, :], AX.X, ALU.add).then_inc(set_ready, 1)
            gemm("qk_mb")
            take_tokens(11, x[:, :, 0:S])
            dve.wait_ge(taken[5], plan.at("boot_rest", "b5") + 3)
            for l in range(LAYERS):
                init = 0.8 - 0.6 * math.exp(-0.3 * l)
                link(dve.tensor_scalar(lam[:, l:l + 1], lam_e[:, l, 0:1], lam_e[:, l, 1:2], init, ALU.subtract, ALU.add))
                link(dve.tensor_scalar(sub_g[:, l:l + 1], col[:, COL["subln"] + l:COL["subln"] + l + 1],
                                       1.0 - init, None, ALU.mult))
            dve.wait_ge(boot_done, 16)
            dve.tensor_copy(sinks[:, :], bank[6][:, 0:8]).then_inc(taken[6], 1)
            for v in range(2):
                dve.wait_ge(boot_done, 17 + v)
                dve.tensor_scalar(tables[:, v, :], bank[5 + v][0:8, :], 8.0, None, ALU.mult).then_inc(taken[5 + v], 1)
            for name in ("v_mb", "q_sw", "q_me"):
                gemm(name)

            def max1(n):
                kind, h = UNITS1[n]
                scale = 0.125 if kind != "mem" else 1.0 / math.sqrt(128)
                dve.wait_ge(score_ready, n + 1)
                st_ = stat[:, n % 2, :]
                link(dve.tensor_reduce(st_[:, 0:2], bank[SCORE1[n % 3]][:, :].rearrange("p (q k) -> p q k", q=2), AX.X, ALU.max))
                if kind == "swa":
                    link(dve.tensor_scalar(st_[:, 0:2], st_[:, 0:2], scale, sinks[:, h:h + 1], ALU.mult, ALU.max))
                    dve.tensor_scalar(st_[:, 2:4], st_[:, 0:2], -1.0, None, ALU.mult).then_inc(nmax_ready, 1)
                else:
                    dve.tensor_scalar(st_[:, 2:4], st_[:, 0:2], -scale, None, ALU.mult).then_inc(nmax_ready, 1)

            def probs1(n):
                kind, h = UNITS1[n]
                b = SCORE1[n % 3]
                dve.wait_ge(taken[b], plan.at("att1", f"b{b}") + n // 3 + 1)
                st_ = stat[:, n % 2, :]
                if kind == "swa":
                    link(dve.tensor_tensor(st_[:, 4:6], st_[:, 4:6], st_[:, 6:8], ALU.add))
                link(dve.reciprocal(st_[:, 8:10], st_[:, 4:6]))
                if n >= 2:
                    dve.wait_ge(pt_done, n - 1)
                for q in range(2):
                    cols = slice(q * S, (q + 1) * S)
                    ins = dve.tensor_scalar(probs[:, n % 2, cols], work[:, n % 2, cols], st_[:, 8 + q:9 + q], None, ALU.mult)
                ins.then_inc(prob_ready, 1)

            def out1(n):
                kind, h = UNITS1[n]
                b = 4 + n % 2
                dve.wait_ge(o_done, n + 1)
                if kind == "moba":
                    tile, to, of, w = h // 2, 64 * (h % 2), 64 * (h % 2), 64
                elif kind == "swa":
                    tile, to, of, w = 4 + h // 2, 64 * (h % 2), 64 * (h // 4), 64
                else:
                    tile, to, of, w = 8 + h, 0, 0, P
                if n >= 2:
                    dve.wait_ge(o_ready, n - 1)
                src = work[to:to + w, 2 + n % 2, 0:S]
                dve.tensor_copy(src, bank[b][of:of + w, 0:S]).then_inc(taken[b], 1)
                dve.wait_ge(taken[b], plan.at("att1", f"b{b}") + n // 2 + 1)
                link(dve.tensor_copy(o1_hi[to:to + w, tile, :], src))
                dve.tensor_tensor(o1_lo[to:to + w, tile, :], src, o1_hi[to:to + w, tile, :].bitcast(f32), ALU.subtract) \
                   .then_inc(o_ready, 1)

            n_units = len(UNITS1)
            dve.wait_ge(u_ready, 2 * KD)
            for n in range(n_units + O_LAG + 1):
                if n < n_units:
                    max1(n)
                if 1 <= n <= n_units:
                    probs1(n - 1)
                if n >= O_LAG + 1:
                    out1(n - O_LAG - 1)
            def first_branch(n):
                return branch[:, KD * n:KD * (n + 1), :]

            for n in range(2):
                gemm(f"gates1_{n}", multiply_gates(first_branch(n), S, slice(0, S)))
            gemm("gates1_2", merge_gates(first_branch(2), (first_branch(0), first_branch(1)), S, slice(0, S),
                                         o1_hi, o1_lo, 0, 16))

            def copy_y(tiles, per):
                def evac(st, i, final):
                    for t in range(tiles):
                        dve.wait_ge(group_done, st.done(i, per * (t + 1)))
                        at = y[:, bass.ds(i * tiles + t, 1), :]
                        dve.tensor_copy(at, bank[t][:, 0:S].rearrange("p (o t) -> p o t", o=1)).then_inc(taken[t], 1)
                        dve.wait_ge(taken[t], st.taken(i, t))
                        sum_squares(st, i, t, at, S, final)
                return evac

            clear_sums()
            gemm("w_out", copy_y(4, 1))
            norm_x("n_mix_post", "g_mix_post")
            dve.wait_ge(updated, KD)
            norm_u("n_ffn", lambda k: x[:, k, S:T], "g_ffn_pre", S)

            def split_hidden(i, t, base, src, hi, lo):
                dve.tensor_copy(hi, src).then_inc(hid_part, 1)
                dve.wait_ge(hid_part, i * 2 + (base + t + 1))
                dve.tensor_tensor(lo, src, hi.bitcast(f32), ALU.subtract).then_inc(hid_ready, 1)

            def conv_ffn(st, i):
                for b in range(4):
                    c, t = b // 2, b % 2
                    at = i * 2 + (c * KF + t)
                    dve.wait_ge(cv_first, i * 4 + (b + 1))
                    dve.scalar_tensor_tensor(work[:, b, 1:S], bank[b][:, 0:S - 1], col[:, bass.ds(at + COL["conv_w1"], 1)],
                                             work[:, b, 1:S], ALU.mult, ALU.add).then_inc(cv_mid, 1)
                    dve.wait_ge(cv_mid, i * 4 + (b + 1))
                    dve.scalar_tensor_tensor(work[:, b, 2:S], bank[b][:, 0:S - 2], col[:, bass.ds(at + COL["conv_w0"], 1)],
                                             work[:, b, 2:S], ALU.mult, ALU.add).then_inc(taken[b], 1)
                dve.wait_ge(hid_ready, i * 2 + 1)
                for t in range(2):
                    dve.wait_ge(gelu_ready, i * 2 + (t + 1))
                    dve.wait_ge(taken[2 + t], st.taken(i, 2 + t))
                    prod = work[:, t, S:2 * S]
                    dve.tensor_tensor(prod, work[:, t, 0:S], work[:, 2 + t, 0:S], ALU.mult).then_inc(hid_prod, 1)
                    dve.wait_ge(hid_prod, i * 2 + (t + 1))
                    at = bass.ds(i * 2 + t, 1)
                    split_hidden(i, t, 0, work[:, t:t + 1, S:2 * S], hid1_hi[:, at, :], hid1_lo[:, at, :])

            gemm("up1", conv_ffn)

            clear_sums()
            gemm("down1", copy_y(2, 4))
            norm_x("n_ffn_post", "g_ffn_post")

            def modulation(l, i):
                pairs, n = MOD_PAIRS // 3, 3 * KD
                dve.wait_ge(taken[7], l * MOD_PAIRS + (i + 1) * pairs + 1)
                b0, g0 = COL[f"b_mod{l}"] + i * n, COL["norm_g"] + (3 * l + i) * KD
                m = mod[:, i * n:(i + 1) * n, :]
                for h in range(2):
                    ins = dve.tensor_tensor(m[:, :, h], mod_sum[:, 2 * i * n + h:2 * (i + 1) * n:2], col[:, b0:b0 + n], ALU.add)
                link(ins)
                for h in range(2):
                    dve.scalar_tensor_tensor(mod_a[:, i, :, h], m[:, KD:2 * KD, h], 1.0, col[:, g0:g0 + KD], ALU.add, ALU.mult)
                link(dve.tensor_scalar(mod_g[:, i, :, :], m[:, 2 * KD:3 * KD, :], 1.0 if i == 1 else 0.5, None, ALU.mult))

            def ffn(name, base, w):
                def body(st, i):
                    dve.wait_ge(hid_ready, i * 2 + (base + 1))
                    for t in range(2):
                        dve.wait_ge(group_done, st.done(i, 3 + t))
                        dve.wait_ge(taken[t], st.taken(i, t))
                        dve.tensor_tensor(work[:, 2 + t, 0:w], bank[2 + t][:, 0:w], work[:, t, 0:w], ALU.mult) \
                           .then_inc(taken[2 + t], 1)
                        dve.wait_ge(taken[2 + t], st.taken(i, 2 + t))
                        at = bass.ds(i * 2 + t, 1)
                        split_hidden(i, t, base, work[:, 2 + t:3 + t, 0:w], hid2_hi[:, at, 0:w], hid2_lo[:, at, 0:w])
                gemm(name, body)

            def residual(i_mod, halves, per, tiles):
                def body(st, i, final):
                    for t in range(tiles):
                        dve.wait_ge(group_done, st.done(i, per(t)))
                        for h in halves:
                            at = x[:, bass.ds(i * tiles + t, 1), h * S:(h + 1) * S]
                            lo = (h - halves[0]) * S
                            ins = dve.scalar_tensor_tensor(at, bank[t][:, lo:lo + S].rearrange("p (o t) -> p o t", o=1),
                                                           mod_g[:, i_mod, bass.ds(i * tiles + t, 1), h], at,
                                                           ALU.mult, ALU.add)
                        ins.then_inc(taken[t], 1)
                        dve.wait_ge(taken[t], st.taken(i, t))
                        sum_squares(st, i, t, x[:, bass.ds(i * tiles + t, 1), span(halves)], S * len(halves),
                                    final)
                return body

            def layer(l):
                both, q_h, m_h = [CTX, LAT], halves_of(l, "q"), halves_of(l, "merge")
                wq, wm = S * len(q_h), S * len(m_h)
                modulation(l, 0)
                norm_mod(f"n0_{l}", both)
                ffn(f"up_{l}0", KF * (1 + 2 * l), T)
                clear_sums()
                gemm(f"down_{l}0", residual(0, both, lambda t: 4 * t + 4, 2))
                modulation(l, 1)
                norm_mod(f"n1_{l}", both)
                gemm(f"q_{l}")
                gemm(f"k_{l}")
                r0, y0 = rope_base(l), yf_base(l)
                tiles = rope_tiles(l)

                def rotate(n):
                    t, j = tiles[n]
                    cur = (q2 if t == 0 else k2)[:, j, S:T]
                    tmp = xn[:, n % 2, 0:S]
                    dve.wait_ge(rot_done, r0 + n + 1)
                    dve.tensor_tensor(tmp, bank[4][:, 0:S], sin, ALU.mult).then_inc(taken[4], 1)
                    link(dve.tensor_tensor(cur, cur, cos, ALU.mult))
                    dve.wait_ge(taken[4], plan.at(f"rope_{l}", "b4") + n + 1)
                    dve.tensor_tensor(cur, cur, tmp, ALU.add).then_inc(rope_ready, 1)
                    dve.wait_ge(rope_ready, r0 + n + 1)

                def channels(n):
                    g, h = four_unit(l, n)
                    tmp = xn[:, n % 2, S:2 * S]
                    hi, lo = yf_hi[:, g, h * S:(h + 1) * S], yf_lo[:, g, h * S:(h + 1) * S]
                    dve.wait_ge(dft_done, dft_base(l) + 2 * n + 2)
                    dve.tensor_copy(tmp, bank[6][:, 0:S]).then_inc(taken[6], 1)
                    dve.wait_ge(taken[6], plan.at(f"four_{l}", "b6") + n + 1)
                    link(dve.tensor_copy(hi, tmp))
                    dve.tensor_tensor(lo, tmp, hi.bitcast(f32), ALU.subtract).then_inc(yf_ready, 1)
                    dve.wait_ge(yf_ready, y0 + n + 1)

                for ropes, n, step in v_slots(l):
                    for r in ropes:
                        rotate(r)
                    if n is not None and step == 1:
                        channels(n)
                units = att_units(l)
                u0, p0 = plan.at(f"att_{l}", "unit"), plan.at(f"att_{l}", "pair")

                def maxima(n):
                    h, half, qb = units[n]
                    nk = T if half == LAT else S
                    st_ = stat[:, n % 4, :]
                    dve.wait_ge(score_ready, n_units + u0 + n + 1)
                    for c in range(2):
                        link(dve.tensor_reduce(st_[:, c:c + 1], bank[score_bank(n, c)][:, 0:nk], AX.X, ALU.max))
                    dve.tensor_scalar(st_[:, 2:4], st_[:, 0:2], -0.125, None, ALU.mult).then_inc(nmax_ready, 1)

                def weights(n):
                    st_ = stat[:, n % 4, :]
                    for c in range(2):
                        b = score_bank(n, c)
                        dve.wait_ge(taken[b], plan.at(f"att_{l}", f"b{b}") + n // 3 + 1)
                    link(dve.reciprocal(st_[:, 8:10], st_[:, 4:6]))
                    dve.tensor_tensor(st_[:, 9:10], st_[:, 9:10], lam[:, l:l + 1], ALU.mult).then_inc(weight_ready, 1)

                def differences(n):
                    h, half, qb = units[n]
                    nk = T if half == LAT else S
                    dve.wait_ge(scaled_ready, u0 + n + 1)
                    dve.wait_ge(pt_done, n_units + u0 + n - 1)
                    dve.scalar_tensor_tensor(probs[:, n % 2, 0:nk], exp_tile(n, 0)[:, 0:nk], stat[:, n % 4, 8:9],
                                             exp_tile(n, 1)[:, 0:nk], ALU.mult, ALU.subtract).then_inc(prob_ready, 1)

                for n in range(len(units) + 2):
                    if n < len(units):
                        maxima(n)
                    if 1 <= n <= len(units):
                        weights(n - 1)
                    if n >= 2:
                        differences(n - 2)
                d0, c0, x0, o0 = (plan.at(f"subln_{l}", k) for k in ("diag", "bc", "xn", "o"))
                nt = wq // P
                dve.wait_ge(taken[4], plan.at(f"subln_{l}", "b4") + 1)
                link(dve.reciprocal(rms[:, 1, 0:KD * nt], rms[:, 0, 0:KD * nt]))
                for h in range(KD):
                    dve.tensor_tensor(head_diag[:, h, 0:wq].rearrange("p (t q) -> p t q", t=nt),
                                      ident.unsqueeze(1).broadcast_to([P, nt, P]),
                                      rms[:, 1, h * nt:(h + 1) * nt].unsqueeze(2).broadcast_to([P, nt, P]), ALU.mult) \
                       .then_inc(diag_ready, 1)

                def norm_head(h):
                    dve.wait_ge(bcast_done, c0 + h + 1)
                    if h >= 2:
                        dve.wait_ge(o_ready, n_units + o0 + h - 1)
                    tmp = xn[:, h % 2, 0:wq]
                    dve.scalar_tensor_tensor(tmp, q2[:, h, span(q_h)], sub_g[:, l:l + 1], bank[5 + h % 2][:, 0:wq],
                                             ALU.mult, ALU.mult).then_inc(xn_ready, 1)
                    dve.wait_ge(xn_ready, x0 + h + 1)
                    hi, lo = o2_hi[:, h, span(q_h)], o2_lo[:, h, span(q_h)]
                    link(dve.tensor_copy(hi, tmp))
                    dve.tensor_tensor(lo, tmp, hi.bitcast(f32), ALU.subtract).then_inc(o_ready, 1)

                def fourier_gates(st, i):
                    for b in range(4):
                        multiply_gate(st, i, b, fr[:, 4 * i + b:4 * i + b + 1, span(m_h)], wm)
                        norm_head(4 * i + b)

                gemm(f"gates_{l}1", fourier_gates, unrolled=True)
                gemm(f"attn_out_{l}")
                gemm(f"gates_{l}0", merge_gates(q2, (fr,), wm, span(m_h), o2_hi, o2_lo,
                                                3 * KD + 2 * KD * l, gate_base(l, 1)))
                clear_sums()
                gemm(f"w_o_{l}", residual(1, m_h, lambda t: t + 1, 4))
                modulation(l, 2)
                norm_mod(f"n2_{l}", m_h)
                ffn(f"up_{l}1", KF * (2 + 2 * l), wm)
                clear_sums()
                gemm(f"down_{l}1", residual(2, m_h, lambda t: 4 * t + 4, 2))

            for l in range(LAYERS):
                layer(l)
            norm_x("n_final", "g_final", fin)
            for n in range(4):
                tt, b = n // 2, 5 + n % 2
                dve.wait_ge(boot_done, 18 + n + 1)
                dve.tensor_copy(rows_out[:, tt, (n % 2) * 512:(n % 2) * 512 + 512], bank[b][:, :]).then_inc(taken[b], 1)

        @block.tensor
        def _(pe):
            def claim(step, b, nth=0):
                n = plan.at(step, f"b{b}") + nth
                if n > 0:
                    pe.wait_ge(taken[b], n)

            def three(dst, hi, lo, m_hi, m_lo, first, final, swap=False):
                for n, (w, m) in enumerate(((hi, m_hi), (hi, m_lo), (lo, m_hi))):
                    s, v = (m, w) if swap else (w, m)
                    ins = pe.matmul(dst, s, v, start=first and n == 0, stop=final and n == 2)
                return ins

            def modulate(st, i):
                pair = mod_pair(st, i)
                pe.wait_ge(taken[7], pair + 1)
                pe.wait_ge(mod_step, pair * (4 * KD) + 4 * KD)
                for c in range(2):
                    for h in range(2):
                        ins = pe.transpose(bank[7][:, (2 * c + h) * P:(2 * c + h + 1) * P], mod_acc[:, c, h, :], ident)
                ins.then_inc(mod_done, 1)

            def gemm(name, block_of, ready=None, unrolled=False):
                st = gemms[name]

                def body(i, ready=None):
                    for c in range(st.per):
                        slot = (st.first + c) % 2
                        if ready is not None and c == 0:
                            block_of(st, i, c, slot, ready)
                        else:
                            block_of(st, i, c, slot)
                    if st.mod:
                        modulate(st, i)

                if unrolled or st.bodies == 1:
                    for i in range(st.bodies):
                        body(i, ready if i == 0 else None)
                elif ready is not None:
                    body(0, ready)
                    with pe.Fori(1, st.bodies) as i:
                        body(i)
                else:
                    with pe.Fori(0, st.bodies) as i:
                        body(i)

            def claim_tile(st, i, b):
                pe.wait_ge(taken[b], i + st.use0[b]) if st.use0[b] > 0 or not isinstance(i, int) else None

            def features(m_hi, m_lo, width, after=None):
                def block_of(st, i, c, slot, ready=None):
                    def part(t, k):
                        at = slice(k * BLK + t * P, k * BLK + (t + 1) * P)
                        return three(bank[2 * c + t][:, 0:width], w_hi[slot][:, at], w_lo[slot][:, at], m_hi(k), m_lo(k),
                                     k == 0, k == st.kt - 1)

                    if ready is not None:
                        pe.wait_ge(lo_ready, st.parts(i, c, 1))
                        for t in range(2):
                            claim_tile(st, i, 2 * c + t)
                        for k in range(st.kt):
                            ready(k, 0)
                            for t in range(2):
                                w = slice(k * BLK + t * P, k * BLK + (t + 1) * P)
                                pe.matmul(bank[2 * c + t][:, 0:width], w_hi[slot][:, w], m_hi(k), start=k == 0, stop=False)
                                pe.matmul(bank[2 * c + t][:, 0:width], w_lo[slot][:, w], m_hi(k), start=False, stop=False)
                            ready(k, 1)
                            for t in range(2):
                                w = slice(k * BLK + t * P, k * BLK + (t + 1) * P)
                                ins = pe.matmul(bank[2 * c + t][:, 0:width], w_hi[slot][:, w], m_lo(k), start=False,
                                                stop=k == st.kt - 1)
                                if k == st.kt - 1:
                                    ins.then_inc(group_done, 1)
                        return
                    for t in range(2):
                        pe.wait_ge(lo_ready, st.parts(i, c, t))
                        claim_tile(st, i, 2 * c + t)
                        for k in range(st.kt):
                            ins = part(t, k)
                        ins.then_inc(group_done, 1)
                        if after is not None:
                            after((2 * i + c) * 2 + t)
                return block_of

            def token_rows(t0, tiles, after=None):
                def block_of(st, i, c, slot):
                    pe.wait_ge(lo_ready, st.parts(i, c, 1))
                    for t in range(tiles):
                        b = 2 * c + t // 2
                        if t % 2 == 0:
                            claim_tile(st, i, b)
                        cols = slice(t0 + t * P, t0 + (t + 1) * P)
                        for k in range(KD):
                            at = slice(k * BLK, (k + 1) * BLK)
                            ins = three(bank[b][:, (t % 2) * BLK:(t % 2 + 1) * BLK], w_hi[slot][:, at], w_lo[slot][:, at],
                                        u_hi[:, k, cols], u_lo[:, k, cols], k == 0, k == KD - 1, swap=True)
                        if t % 2 == 1:
                            ins.then_inc(group_done, 1)
                        if after is not None:
                            after((2 * i + c) * tiles + t)
                return block_of

            def down_strips(h_hi, h_lo, w, base):
                def block_of(st, i, c, slot):
                    b, part = c // 2, c % 2
                    pe.wait_ge(hid_ready, base + (part + 1) * DOWN_KT + 1)
                    if part == 0:
                        claim_tile(st, i, b)
                    for k in range(DOWN_KT):
                        if k in (0, DOWN_HALF):
                            pe.wait_ge(lo_ready, st.parts(i, c, k // DOWN_HALF))
                        at = slice(k * P, (k + 1) * P)
                        kk = part * DOWN_KT + k
                        ins = three(bank[b][:, 0:w], w_hi[slot][:, at], w_lo[slot][:, at], h_hi[:, kk, 0:w], h_lo[:, kk, 0:w],
                                    kk == 0, kk == KF - 1)
                        if k in (DOWN_HALF - 1, DOWN_KT - 1):
                            ins.then_inc(group_done, 1)
                return block_of

            def u_of(cols):
                return (lambda k: u_hi[:, k, cols]), (lambda k: u_lo[:, k, cols])

            def column_sums(name, w, summed=True):
                claim(name, 4)
                if summed:
                    parts = [root[:, s, 0:w] for s in range(2)] + [xn[:, s, 0:w] for s in range(2)]
                else:
                    parts = [sq[:, k, :] for k in range(KD)]
                for n, part in enumerate(parts):
                    if not summed:
                        pe.wait_ge(sq_ready, plan.at(name, "sq") + n + 1)
                    elif n != 1:
                        pe.wait_ge(acc_step, plan.at(name, "acc") - 2 + max(0, n - 1))
                    for t in range(w // P):
                        ins = pe.matmul(bank[4][:, t:t + 1], part[:, t * P:(t + 1) * P], ones[:, 0:1],
                                        start=n == 0 and t == 0, stop=n == len(parts) - 1, skip_group_check=True)
                    if not summed or n == len(parts) - 1:
                        ins.then_inc(sums_done, 1)

            def spread(name, w):
                pe.wait_ge(diag_ready, plan.at(name, "diag") + 1)
                claim(name, 5)
                pe.matmul(bank[5][:, 0:w], ones[:, :], diag[:, 0:w // P, :].rearrange("p t q -> p (t q)"),
                          start=True, stop=True).then_inc(bcast_done, 1)

            def u_tile(name):
                return lambda k, part: pe.wait_ge((u_part, u_ready)[part], plan.at(name, "u") + k + 1)

            def tokens_in(n, step):
                pe.wait_ge(tok_ready[n], 16)
                for q in range(4):
                    b = 4 + q % 2
                    claim(step, b, q // 2)
                    for f in range(2):
                        for tt in range(2):
                            ins = pe.transpose(bank[b][:, f * S + tt * P:f * S + (tt + 1) * P],
                                               tok[:, n, tt, (2 * q + f) * P:(2 * q + f + 1) * P], ident)
                    ins.then_inc(boot_done, 1)

            mem_cols, x_cols = slice(0, S), slice(S, T)
            pe.wait_ge(const_ready, 16)
            tokens_in(0, "boot_mem")
            pe.wait_ge(set_ready, 2)
            column_sums("n_mem", S, False)
            n_rows = [sum(r for _, r in rows_of) for rows_of in ROW_TILES]
            pe.wait_ge(rows_ready[0], 16 * len(ROW_TILES[0]))
            pe.transpose(bank[6][:, 0:N_FIRST], rows[0:N_FIRST, 0, :], ident[0:N_FIRST, 0:N_FIRST]).then_inc(boot_done, 1)
            spread("n_mem", S)

            gemm("k_me", features(*u_of(mem_cols), S), u_tile("n_mem"))
            tokens_in(1, "boot_x")
            pe.wait_ge(rows_ready[1], 16 * (len(ROWS) - len(ROW_TILES[0])))
            claim("boot_x", 6)
            at = 0
            for t, n in enumerate(n_rows[1:]):
                ins = pe.transpose(bank[6][:, at:at + n], rows[0:n, t + 1, :], ident[0:n, 0:n])
                at += n
            ins.then_inc(boot_done, 1)
            gemm("v_me", token_rows(0, 2))
            column_sums("n_mix", S, False)
            spread("n_mix", S)
            gemm("qk_mb", features(*u_of(x_cols), S), u_tile("n_mix"))
            tokens_in(2, "boot_rest")
            pe.wait_ge(set_ready, 6)
            claim("boot_rest", 5, 2)
            pe.matmul(bank[5][:, 16:20], ones[0:1, :], lam_s[:, :, :].rearrange("p l j -> p (l j)"), start=True, stop=True) \
              .then_inc(boot_done, 1)
            claim("boot_rest", 6)
            pe.wait_ge(rel_ready, 64)
            pe.matmul(bank[6][:, 0:8], ones[0:1, :], sink_row[:, :], start=True, stop=True).then_inc(boot_done, 1)
            claim("boot_rest", 5, 3)
            pe.matmul(bank[5][0:8, :], rel[:, 0:8], hot[:, 0, :], start=True, stop=True).then_inc(boot_done, 1)
            claim("boot_rest", 6, 1)
            pe.matmul(bank[6][0:8, :], rel[:, 8:16], hot[:, 1, :], start=True, stop=True).then_inc(boot_done, 1)
            gemm("v_mb", token_rows(S, 2))
            column_sums("ctx_sums", S, False)
            gemm("q_sw", features(*u_of(x_cols), S))

            def kv_sw(st, i, c, slot):
                pe.wait_ge(lo_ready, st.parts(0, 0, 1))
                claim_tile(st, 0, 0)
                for k in range(KD):
                    at = slice(k * BLK, k * BLK + P)
                    ins = three(bank[0][:, 0:S], w_hi[slot][:, at], w_lo[slot][:, at], u_hi[:, k, x_cols], u_lo[:, k, x_cols],
                                k == 0, k == KD - 1)
                ins.then_inc(group_done, 1)
                claim_tile(st, 0, 1)
                for t in range(2):
                    cols = slice(S + t * P, S + (t + 1) * P)
                    for k in range(KD):
                        at = slice(k * BLK + P, (k + 1) * BLK)
                        ins = three(bank[1][:, t * P:(t + 1) * P], w_hi[slot][:, at], w_lo[slot][:, at],
                                    u_hi[:, k, cols], u_lo[:, k, cols], k == 0, k == KD - 1, swap=True)
                ins.then_inc(group_done, 1)

            gemm("kv_sw", kv_sw)
            gemm("q_me", features(*u_of(x_cols), S))

            def scores1(n):
                kind, h = UNITS1[n]
                b = SCORE1[n % 3]
                claim("att1", b, n // 3)
                if kind == "moba":
                    r = slice(64 * (h % 2), 64 * (h % 2) + 64)
                    q, k, table = qk_mb[r, h // 2, :], qk_mb[r, 4 + h // 2, :], h
                elif kind == "swa":
                    r = slice(64 * (h % 2), 64 * (h % 2) + 64)
                    q, k, table = q_sw[r, h // 2, :], k_sw[r, h // 4, :], 8 + h
                else:
                    q, k, table = q_me[:, h, :], k_me[:, h, :], None
                for qb in range(2):
                    dst = bank[b][:, qb * S:(qb + 1) * S]
                    ins = pe.matmul(dst, q[:, qb * P:(qb + 1) * P], k, start=True, stop=table is None)
                    if table is not None:
                        shift = P * (1 - qb)
                        ins = pe.matmul(dst, reverse, hank[:, table, shift:shift + S], start=False, stop=True)
                ins.then_inc(score_ready, 1)

            def transposes1(n):
                b = 2 + n % 2
                pe.wait_ge(prob_ready, n + 1)
                claim("att1", b, n // 2)
                for kt in range(2):
                    for qb in range(2):
                        ins = pe.transpose(bank[b][:, kt * S + qb * P:kt * S + (qb + 1) * P],
                                           probs[:, n % 2, qb * S + kt * P:qb * S + (kt + 1) * P], ident)
                ins.then_inc(pt_done, 1)

            def outputs1(n):
                kind, h = UNITS1[n]
                b = 4 + n % 2
                pe.wait_ge(taken[2 + n % 2], plan.at("att1", f"b{2 + n % 2}") + n // 2 + 1)
                claim("att1", b, n // 2)
                for kt in range(2):
                    if kind == "moba":
                        v = v_mb[:, kt, (h // 2) * P:(h // 2 + 1) * P]
                    elif kind == "swa":
                        v = v_sw[:, kt, :]
                    else:
                        v = v_me[:, kt, h * P:(h + 1) * P]
                    ins = pe.matmul(bank[b][:, 0:S], v, p_t[:, n % 2, kt, :], start=kt == 0, stop=kt == 1)
                ins.then_inc(o_done, 1)

            for name, b in (("q_me", 0), ("q_me", 1), ("q_me", 2), ("q_me", 3)):
                pe.wait_ge(taken[b], gemms[name].taken(0, b))
            pe.wait_ge(hank_ready, 16)
            n_units = len(UNITS1)
            for n in range(n_units + O_LAG):
                if n < n_units:
                    scores1(n)
                if T_LAG <= n < n_units + T_LAG:
                    transposes1(n - T_LAG)
                if n >= O_LAG:
                    outputs1(n - O_LAG)
            for n, units_done in enumerate((8, 16, 20)):
                pe.wait_ge(o_ready, units_done)
                gemm(f"branch{n}", features(lambda k, n=n: o1_hi[:, 4 * n + k, :], lambda k, n=n: o1_lo[:, 4 * n + k, :], S))
            for n in range(3):
                gemm(f"gates1_{n}", features(*u_of(x_cols), S))

            def merged_tile(n0):
                return lambda k, part: pe.wait_ge(merged_ready, n0 + k + 1)

            gemm("w_out", features(lambda k: o1_hi[:, k, :], lambda k: o1_lo[:, k, :], S), merged_tile(0))
            column_sums("n_mix_post", S)
            spread("n_mix_post", S)
            column_sums("n_ffn", S, False)
            spread("n_ffn", S)
            gemm("up1", features(*u_of(x_cols), S), u_tile("n_ffn"))
            gemm("down1", down_strips(hid1_hi, hid1_lo, S, 0))
            column_sums("n_ffn_post", S)
            spread("n_ffn_post", S)

            def layer(l):
                both, q_h, m_h = [CTX, LAT], halves_of(l, "q"), halves_of(l, "merge")
                wq, wm = S * len(q_h), S * len(m_h)
                all_cols = slice(0, T)
                column_sums(f"n0_{l}", T if l else S, l > 0)
                spread(f"n0_{l}", T)
                gemm(f"up_{l}0", features(*u_of(all_cols), T), u_tile(f"n0_{l}"))
                gemm(f"down_{l}0", down_strips(hid2_hi, hid2_lo, T, KF * (1 + 2 * l)))
                column_sums(f"n1_{l}", T)
                spread(f"n1_{l}", T)
                gemm(f"q_{l}", features(*u_of(span(q_h)), wq), u_tile(f"n1_{l}"))
                gemm(f"k_{l}", features(*u_of(all_cols), T))
                gemm(f"f_{l}", token_rows(span(q_h).start, 2 * len(q_h)))
                slots, tiles = v_slots(l), rope_tiles(l)

                def rotate(n):
                    t, j = tiles[n]
                    claim(f"rope_{l}", 4, n)
                    pe.matmul(bank[4][:, 0:S], rot, (q2 if t == 0 else k2)[:, j, S:T], start=True, stop=True) \
                      .then_inc(rot_done, 1)

                def tokens(n):
                    g, h = four_unit(l, n)
                    claim(f"four_{l}", 5, n)
                    for tt in range(2):
                        ins = pe.matmul(bank[5][:, :], f2[:, 2 * h + tt, g * P:(g + 1) * P],
                                        table(C_DFT + 512 * tt, 512), start=tt == 0, stop=tt == 1)
                    ins.then_inc(dft_done, 1)

                def channels(n):
                    pe.wait_ge(taken[5], plan.at(f"four_{l}", "b5") + n + 1)
                    claim(f"four_{l}", 6, n)
                    for s, c in enumerate((C_DC, C_DS)):
                        ins = pe.matmul(bank[6][:, 0:S], table(c, P), dft[:, n % 2, s * S:(s + 1) * S],
                                        start=s == 0, stop=s == 1)
                    ins.then_inc(dft_done, 1)

                def after_value_tile(m):
                    if m == 0:
                        for name in (f"k_{l}", f"f_{l}"):
                            st = gemms[name]
                            for b in st.banks:
                                pe.wait_ge(taken[b], st.taken(st.bodies - 1, b))
                        pe.wait_ge(tabs_ready, 16 * (l + 1))
                    ropes, n, step = slots[m]
                    for r in ropes:
                        rotate(r)
                    if n is not None:
                        (tokens, channels)[step](n)

                gemm(f"v_{l}", token_rows(0, 4, after_value_tile), unrolled=True)
                units = att_units(l)
                u0, p0 = plan.at(f"att_{l}", "unit"), plan.at(f"att_{l}", "pair")
                pe.wait_ge(rope_ready, rope_base(l) + 16)

                def scores(n):
                    h, half, qb = units[n]
                    nk = T if half == LAT else S
                    at = half * S + qb * P
                    for c in range(2):
                        b = score_bank(n, c)
                        claim(f"att_{l}", b, n // 3)
                        r = slice(64 * c, 64 * c + 64)
                        ins = pe.matmul(bank[b][:, 0:nk], q2[r, h, at:at + P], k2[r, h, 0:nk], start=True, stop=True)
                    ins.then_inc(score_ready, 1)

                def transposes(n):
                    h, half, qb = units[n]
                    kt = 4 if half == LAT else 2
                    pe.wait_ge(prob_ready, n_units + u0 + n + 1)
                    claim(f"att_{l}", 6, n)
                    for k in range(kt):
                        ins = pe.transpose(bank[6][:, k * P:(k + 1) * P],
                                           probs[:, n % 2, k * P:(k + 1) * P], ident)
                    ins.then_inc(pt_done, 1)

                def outputs(p):
                    h, half, _ = units[2 * p]
                    kt = 4 if half == LAT else 2
                    pe.wait_ge(taken[6], plan.at(f"att_{l}", "b6") + 2 * p + 2)
                    if p == 0:
                        pe.wait_ge(taken[7], plan.at(f"att_{l}", "pair_mod") + 1)
                    else:
                        pe.wait_ge(head_taken, p0 + p)
                    for k in range(kt):
                        ins = pe.matmul(bank[7][:, 0:S], v2[:, k, h * P:(h + 1) * P], a_t[:, p % 2, k, :],
                                        start=k == 0, stop=k == kt - 1)
                    ins.then_inc(o_done, 1)

                for n in range(len(units) + O_LAG):
                    if n < len(units):
                        scores(n)
                    if T_LAG <= n < len(units) + T_LAG:
                        transposes(n - T_LAG)
                    if n > O_LAG and (n - O_LAG) % 2 == 1:
                        outputs((n - O_LAG) // 2)
                m_cols = span(m_h)
                pe.wait_ge(yf_ready, yf_base(l) + 4 * len(q_h))
                gemm(f"four_out_{l}", features(lambda k: yf_hi[:, k, m_cols], lambda k: yf_lo[:, k, m_cols], wm))
                nt = wq // P
                claim(f"subln_{l}", 4)
                for h in range(KD):
                    pe.wait_ge(sq_ready, plan.at(f"subln_{l}", "sq") + h + 1)
                    for t in range(nt):
                        ins = pe.matmul(bank[4][:, h * nt + t:h * nt + t + 1], head_sq[:, h, t * P:(t + 1) * P], ones[:, 0:1],
                                        start=True, stop=True)
                ins.then_inc(sums_done, 1)

                def spread_heads(m):
                    for h in [[], [0, 1]][m] if m < 2 else [m]:
                        pe.wait_ge(diag_ready, plan.at(f"subln_{l}", "diag") + h + 1)
                        if h < 2:
                            claim(f"subln_{l}", 5 + h)
                        else:
                            pe.wait_ge(xn_ready, plan.at(f"subln_{l}", "xn") + h - 1)
                        pe.matmul(bank[5 + h % 2][:, 0:wq], ones[:, :], head_diag[:, h, 0:wq], start=True, stop=True) \
                          .then_inc(bcast_done, 1)

                gemm(f"gates_{l}1", features(*u_of(m_cols), wm, spread_heads), unrolled=True)
                o0 = n_units + plan.at(f"subln_{l}", "o")
                gemm(f"attn_out_{l}", features(lambda k: o2_hi[:, k, m_cols], lambda k: o2_lo[:, k, m_cols], wm),
                     lambda k, part: pe.wait_ge(o_ready, o0 + k + 1))
                gemm(f"gates_{l}0", features(*u_of(m_cols), wm))
                gemm(f"w_o_{l}", features(lambda k: o2_hi[:, k, m_cols], lambda k: o2_lo[:, k, m_cols], wm),
                     merged_tile(KD * (1 + l)))
                column_sums(f"n2_{l}", wm)
                spread(f"n2_{l}", wm)
                gemm(f"up_{l}1", features(*u_of(m_cols), wm), u_tile(f"n2_{l}"))
                gemm(f"down_{l}1", down_strips(hid2_hi, hid2_lo, wm, KF * (2 + 2 * l)))

            for l in range(LAYERS):
                layer(l)
            column_sums("n_final", S)
            spread("n_final", S)
            pe.wait_ge(updated, 3 * KD)
            for n in range(4):
                tt, b = n // 2, 5 + n % 2
                claim("store", b, n // 2)
                for k in range(4):
                    ins = pe.transpose(bank[b][:, k * P:(k + 1) * P],
                                       fin[:, 4 * (n % 2) + k, tt * P:(tt + 1) * P], ident)
                ins.then_inc(boot_done, 1)


_INS = ["x", "mem", "norm_mix_pre", "norm_mix_post", "norm_ffn_pre", "norm_ffn_post", "norm_mem", "w_in", "rel_bias",
        "swa_sinks", "w_mem_kv", "w_branch_moba", "w_branch_swa", "w_branch_mem", "w_out", "w_ffn_up", "ffn_conv_w",
        "ffn_conv_b", "w_ffn_down", "c_2", "ctx_2", "c_ctx_2", "w_mod_2", "b_mod_2", "norm_g_2", "ffn_w_in_2",
        "ffn_w_out_2", "w_in_2", "b_gate_2", "lam_params_2", "subln_g_2", "w_attn_out_2", "w_four_out_2", "w_o_2",
        "final_g_2"]


def kernel(**inputs):
    import numpy as _np
    import concourse.bacc as _bacc
    from concourse import mybir as _mybir
    from concourse.bass_utils import run_bass_kernel_spmd as _run

    nc = _bacc.Bacc("TRN2", target_bir_lowering=False, num_devices=1, dynamic_dma_scratch_size=1024)
    arrays, aps = {}, {}
    consts = dict(zip(("shape_const", "shape_hot"), shape_constants()))
    for name, v in [(n, inputs[n]) for n in _INS] + list(consts.items()):
        v = _np.ascontiguousarray(v)
        arrays[f"in_{name}"] = v
        aps[name] = nc.dram_tensor(f"in_{name}", v.shape, _mybir.dt.from_np(v.dtype), kind="ExternalInput").ap()
    out = nc.dram_tensor("out_rows", (1, S, D), _mybir.dt.float32, kind="ExternalOutput").ap()
    two_blocks(nc, aps, out)
    r = _run(nc, [arrays], core_ids=[0])
    return r.results[0]["out_rows"]
```
